# Optimizing a Trainium2 kernel written in Bass

```python
import math
import jax
import jax.numpy as jnp
from jax import lax
import numpy as np
import jax, jax.numpy as jnp

D_MODEL = 1024
BATCH = 1
SEQ = 256
DEPTH = 2

GRID_W = 64
CTX_LEN = 256
N_MIXERS = 3
EXPAND = 2
D_INNER = EXPAND * D_MODEL
NORM_EPS = 1e-6

RWKV_HEAD = 64
RWKV_HEADS = D_INNER // RWKV_HEAD
RWKV_DECAY_LORA = 64
RWKV_ICLR_LORA = 64
RWKV_VRES_LORA = 32
RWKV_N_MU = 6
RWKV_GN_EPS = 64e-5

HYENA_EMB = 33
HYENA_FILTER_WIDTH = 64
HYENA_SIN_W = 1.0
HYENA_FAST_DECAY = 0.3
HYENA_SLOW_DECAY = 1.5
HYENA_TARGET = 1e-2

HGRN_KEY = 128
HGRN_HEADS = D_INNER // HGRN_KEY
HGRN_VAL = D_INNER // HGRN_HEADS
HGRN_CHUNK = 32


def rms_norm(x, g, eps=NORM_EPS):
    xf = x.astype(jnp.float32)
    y = xf * lax.rsqrt(jnp.mean(xf * xf, axis=-1, keepdims=True) + eps)
    return (y * g.astype(jnp.float32)).astype(x.dtype)

def adaln(cond, w, b):
    return jnp.split(jax.nn.silu(cond) @ w + b, 3, axis=-1)

def split_heads(a, n_heads):
    return a.reshape(a.shape[:-1] + (n_heads, a.shape[-1] // n_heads))

def merge_heads(a):
    return a.reshape(a.shape[:-2] + (a.shape[-2] * a.shape[-1],))

def grid_shift(h):
    b, t, d = h.shape
    rows = t // GRID_W
    g = h.reshape(b, rows, GRID_W, d)
    q = d // 4
    left = jnp.pad(g[:, :, :-1, :q], ((0, 0), (0, 0), (1, 0), (0, 0)))
    right = jnp.pad(g[:, :, 1:, q:2 * q], ((0, 0), (0, 0), (0, 1), (0, 0)))
    up = jnp.pad(g[:, :-1, :, 2 * q:3 * q], ((0, 0), (1, 0), (0, 0), (0, 0)))
    down = jnp.pad(g[:, 1:, :, 3 * q:], ((0, 0), (0, 1), (0, 0), (0, 0)))
    return jnp.concatenate([left, right, up, down], axis=-1).reshape(b, t, d)

def seq_shift(h):
    half = h.shape[-1] // 2
    prev = jnp.pad(h[:, :-1, :half], ((0, 0), (1, 0), (0, 0)))
    nxt = jnp.pad(h[:, 1:, half:], ((0, 0), (0, 1), (0, 0)))
    return jnp.concatenate([prev, nxt], axis=-1)

def rwkv7_col_groups(vres):
    widths = [D_INNER] * 4 + [RWKV_DECAY_LORA] * 2 + [RWKV_ICLR_LORA] * 2
    groups = [0, 1, 2, 3, 4, 4, 5, 5]
    if vres:
        widths.append(RWKV_VRES_LORA)
        groups.append(2)
    return np.repeat(np.asarray(groups), np.asarray(widths))

def rwkv7_prepare(h, h_shift, p, v_first):
    e = D_INNER
    vres = 'v0' in p
    mu_cols = p['mu'][rwkv7_col_groups(vres)].T
    proj = h @ p['w_in'] + (h_shift - h) @ (p['w_in'] * mu_cols)
    r, k, v, gate = (proj[..., j * e:(j + 1) * e] for j in range(4))
    lo = proj[..., 4 * e:]
    nd, na = 2 * RWKV_DECAY_LORA, 2 * RWKV_ICLR_LORA
    w_lo = split_heads(lo[..., :nd], 2)
    a_lo = split_heads(lo[..., nd:nd + na], 2)
    if vres:
        v = v + (v_first - v) * jax.nn.sigmoid(p['v0'] + lo[..., nd + na:] @ p['v2'])
    else:
        v_first = v
    kk = split_heads(k * p['k_k'], RWKV_HEADS).astype(jnp.float32)
    kk = kk / jnp.maximum(jnp.sqrt(jnp.sum(kk * kk, axis=-1, keepdims=True)), 1e-12)
    return (split_heads(r, RWKV_HEADS), k, split_heads(v, RWKV_HEADS), gate, kk, w_lo, a_lo, v_first)

def rwkv7_direction(k, w_lo, a_lo, p, z):
    w_raw = -jax.nn.softplus(-(p['w0'][z] + jnp.tanh(w_lo[..., z, :]) @ p['w2'][z])) - 0.5
    decay = jnp.exp(-jnp.exp(w_raw.astype(jnp.float32)))
    a = jax.nn.sigmoid(p['a0'][z] + a_lo[..., z, :] @ p['a2'][z])
    k_dir = k * (1.0 + (a - 1.0) * p['k_a'])
    return (split_heads(decay, RWKV_HEADS), split_heads(k_dir, RWKV_HEADS), split_heads(a, RWKV_HEADS))

def rwkv7_scan(r, decay, k, v, kk, a, s0, reverse):
    xs = tuple(jnp.moveaxis(t.astype(jnp.float32), 1, 0) for t in (r, decay, k, v, -kk, kk * a))

    def step(s, inp):
        r_t, w_t, k_t, v_t, a_t, b_t = inp
        sa = jnp.einsum('bhvk,bhk->bhv', s, a_t)
        s = s * w_t[:, :, None, :] + sa[..., None] * b_t[:, :, None, :] + v_t[..., None] * k_t[:, :, None, :]
        return s, jnp.einsum('bhvk,bhk->bhv', s, r_t)

    s_last, ys = lax.scan(step, s0, xs, reverse=reverse)
    return jnp.moveaxis(ys, 0, 1), s_last

def rwkv7_readout(y, bonus, gate, p, dtype):
    mean = jnp.mean(y, axis=-1, keepdims=True)
    var = jnp.mean(jnp.square(y - mean), axis=-1, keepdims=True)
    yn = merge_heads((y - mean) * lax.rsqrt(var + RWKV_GN_EPS))
    yn = yn * p['ln_w'].astype(jnp.float32) + p['ln_b'].astype(jnp.float32)
    return ((yn + merge_heads(bonus)) * jax.nn.silu(gate.astype(jnp.float32))).astype(dtype)

def rwkv7_mixer(hx, hc, p, v_first_x, v_first_c, ctx_out):
    rx, kx, vx, gx, kkx, wlx, alx, v_first_x = rwkv7_prepare(hx, grid_shift(hx), p, v_first_x)
    rc, kc, vc, gc, kkc, wlc, alc, v_first_c = rwkv7_prepare(hc, seq_shift(hc), p, v_first_c)
    s0 = jnp.zeros((hx.shape[0], RWKV_HEADS, RWKV_HEAD, RWKV_HEAD), jnp.float32)
    r_k = p['r_k'].astype(jnp.float32)
    yx = bx = yc = bc = 0.0
    for z in range(2):
        dc, kdc, ac = rwkv7_direction(kc, wlc, alc, p, z)
        dx, kdx, ax = rwkv7_direction(kx, wlx, alx, p, z)
        yc_z, s_ctx = rwkv7_scan(rc, dc, kdc, vc, kkc, ac, s0, z == 1)
        yx_z, _ = rwkv7_scan(rx, dx, kdx, vx, kkx, ax, s_ctx, z == 1)
        yx = yx + yx_z
        bx = bx + jnp.sum(rx * kdx * r_k, axis=-1, keepdims=True) * vx
        if ctx_out:
            yc = yc + yc_z
            bc = bc + jnp.sum(rc * kdc * r_k, axis=-1, keepdims=True) * vc
    ux = rwkv7_readout(yx, bx, gx, p, hx.dtype)
    uc = rwkv7_readout(yc, bc, gc, p, hc.dtype) if ctx_out else None
    return ux, uc, v_first_x, v_first_c

def hyena_filters(length, p):
    f32 = jnp.float32
    t = jnp.linspace(0.0, 1.0, length, dtype=f32)[:, None]
    bands = (HYENA_EMB - 1) // 2
    freqs = jnp.linspace(1e-4, bands - 1, bands, dtype=f32)[None, :]
    ang = (2.0 * math.pi / length) * jnp.arange(length, dtype=f32)[:, None] * freqs
    z = jnp.concatenate([t, jnp.cos(ang), -jnp.sin(ang)], axis=-1)
    sf = p['sin_freq'].astype(f32)
    hdn = jnp.sin(sf * (z @ p['f_w1'].astype(f32) + p['f_b1'].astype(f32)))
    hdn = jnp.sin(sf * (hdn @ p['f_w2'].astype(f32) + p['f_b2'].astype(f32)))
    hdn = jnp.sin(sf * (hdn @ p['f_w3'].astype(f32) + p['f_b3'].astype(f32)))
    filt = hdn @ p['f_w4'].astype(f32)
    deltas = jnp.abs(jnp.linspace(math.log(HYENA_TARGET) / HYENA_SLOW_DECAY,
                                  math.log(HYENA_TARGET) / HYENA_FAST_DECAY, D_INNER, dtype=f32))
    window = jnp.exp(-t * deltas)
    return filt.reshape(length, 2, D_INNER) * window[:, None, :]

def bidir_long_conv(u, filt, skip):
    length = u.shape[1]
    hf, hb = filt[:, 0], filt[:, 1]
    k = jnp.concatenate([hf[:1] + hb[:1], hf[1:], jnp.zeros_like(hf[:1]), hb[:0:-1]], axis=0)
    n = 2 * length
    uf32 = u.astype(jnp.float32)
    uf = jnp.fft.rfft(uf32, n=n, axis=1)
    kf = jnp.fft.rfft(k, n=n, axis=0)
    y = jnp.fft.irfft(uf * kf[None], n=n, axis=1)[:, :length]
    return (y + uf32 * skip.astype(jnp.float32)).astype(u.dtype)

def centred_dwconv3(u, w, b):
    c = u.shape[-1]
    y = lax.conv_general_dilated(u, w[:, None, :].astype(u.dtype), window_strides=(1,), padding=((1, 1),),
                                 dimension_numbers=('NWC', 'WIO', 'NWC'), feature_group_count=c)
    return y + b

def hyena_sequence(h, p):
    e = D_INNER
    proj = h @ p['w_in']
    s = centred_dwconv3(proj[..., :3 * e], p['conv_w'], p['conv_b'])
    x0, x1, v = s[..., :e], s[..., e:2 * e], s[..., 2 * e:]
    v = bidir_long_conv(v * x1, hyena_filters(h.shape[1], p), p['filter_bias'])
    return v * x0 * jax.nn.silu(proj[..., 3 * e:])

def hyena_mixer(hx, hc, p, ctx_out):
    ux = hyena_sequence(hx, p)
    uc = hyena_sequence(hc, p) if ctx_out else None
    return ux, uc

def hgrn2_prepare(h, p, lb):
    e = D_INNER
    proj = h @ p['w_in']
    q = split_heads(jax.nn.silu(proj[..., :e]), HGRN_HEADS)
    i = split_heads(proj[..., 3 * e:4 * e], HGRN_HEADS)
    gate = proj[..., 4 * e:]
    dirs = []
    for z in range(2):
        f = lb + (1.0 - lb) * jax.nn.sigmoid(proj[..., (1 + z) * e:(2 + z) * e].astype(jnp.float32))
        dirs.append((split_heads(1.0 - f, HGRN_HEADS), split_heads(jnp.log(f), HGRN_HEADS)))
    return q, i, gate, dirs

def gla_chunkwise(q, k, v, log_f, s0):
    b, t, h, _ = q.shape
    dv = v.shape[-1]
    n = t // HGRN_CHUNK

    def chunks(a):
        return a.astype(jnp.float32).reshape(b, n, HGRN_CHUNK, h, a.shape[-1]).transpose(1, 0, 3, 2, 4)

    causal = jnp.asarray(np.tril(np.ones((HGRN_CHUNK, HGRN_CHUNK), dtype=bool)))[:, :, None]

    def step(s, inp):
        qc, kc, vc, gc = inp
        cum = jnp.cumsum(gc, axis=2)
        last = cum[:, :, -1:, :]
        o = jnp.einsum('bhck,bhkv->bhcv', qc * jnp.exp(cum), s)
        rel = jnp.exp(jnp.where(causal, cum[:, :, :, None, :] - cum[:, :, None, :, :], -jnp.inf))
        att = jnp.einsum('bhtk,bhsk,bhtsk->bhts', qc, kc, rel)
        o = o + jnp.einsum('bhts,bhsv->bhtv', att, vc)
        s = jnp.exp(last[:, :, 0, :, None]) * s + jnp.einsum('bhsk,bhsv->bhkv', kc * jnp.exp(last - cum), vc)
        return s, o

    s_last, o = lax.scan(step, s0, (chunks(q), chunks(k), chunks(v), chunks(log_f)))
    return o.transpose(1, 0, 3, 2, 4).reshape(b, t, h, dv), s_last

def gla_direction(q, k, v, log_f, s0, reverse):
    if reverse:
        o, s = gla_chunkwise(jnp.flip(q, 1), jnp.flip(k, 1), jnp.flip(v, 1), jnp.flip(log_f, 1), s0)
        return jnp.flip(o, 1), s
    return gla_chunkwise(q, k, v, log_f, s0)

def hgrn2_readout(o, gate, g_norm, dtype):
    o = o * lax.rsqrt(jnp.mean(o * o, axis=-1, keepdims=True) + NORM_EPS) * g_norm.astype(jnp.float32)
    return (merge_heads(o) * jax.nn.silu(gate.astype(jnp.float32))).astype(dtype)

def hgrn2_mixer(hx, hc, p, lb, ctx_out):
    qx, ix, gx, dirs_x = hgrn2_prepare(hx, p, lb)
    qc, ic, gc, dirs_c = hgrn2_prepare(hc, p, lb)
    s0 = jnp.zeros((hx.shape[0], HGRN_HEADS, HGRN_KEY, HGRN_VAL), jnp.float32)
    ox = oc = 0.0
    for z in range(2):
        oc_z, s_ctx = gla_direction(qc, dirs_c[z][0], ic, dirs_c[z][1], s0, z == 1)
        ox_z, _ = gla_direction(qx, dirs_x[z][0], ix, dirs_x[z][1], s_ctx, z == 1)
        ox = ox + ox_z
        if ctx_out:
            oc = oc + oc_z
    ux = hgrn2_readout(ox, gx, p['g_norm'], hx.dtype)
    uc = hgrn2_readout(oc, gc, p['g_norm'], hc.dtype) if ctx_out else None
    return ux, uc

def first_inputs(seed: int = 0) -> dict:
    key = jax.random.key(seed)
    keys = iter(jax.random.split(key, 96))
    f32 = jnp.float32
    e, d = D_INNER, D_MODEL

    def normal(shape, scale):
        return jax.random.normal(next(keys), shape, f32) * scale

    def near_one(shape):
        return 1.0 + normal(shape, 0.05)

    def rwkv(prefix, vres):
        width = 4 * e + 2 * RWKV_DECAY_LORA + 2 * RWKV_ICLR_LORA + (RWKV_VRES_LORA if vres else 0)
        out = {
            prefix + 'w_in': normal((d, width), d ** -0.5),
            prefix + 'mu': jax.random.uniform(next(keys), (RWKV_N_MU, d), f32),
            prefix + 'w0': jnp.linspace(-6.5, -1.5, e, dtype=f32)[None, :] + normal((2, e), 0.1),
            prefix + 'w2': normal((2, RWKV_DECAY_LORA, e), 0.1),
            prefix + 'a0': normal((2, e), 0.1),
            prefix + 'a2': normal((2, RWKV_ICLR_LORA, e), 0.1),
            prefix + 'k_k': 0.85 + normal((e,), 0.05),
            prefix + 'k_a': near_one((e,)),
            prefix + 'r_k': normal((RWKV_HEADS, RWKV_HEAD), 0.1),
            prefix + 'ln_w': near_one((e,)),
            prefix + 'ln_b': normal((e,), 0.02),
        }
        if vres:
            out[prefix + 'v0'] = near_one((e,))
            out[prefix + 'v2'] = normal((RWKV_VRES_LORA, e), 0.1)
        return out

    inputs = {
        'x': normal((BATCH, SEQ, d), 1.0),
        'c': normal((BATCH, d), 1.0),
        'ctx': normal((BATCH, CTX_LEN, d), 1.0),
        'c_ctx': normal((d,), 1.0),
        'ada_w': normal((DEPTH, d, 3 * d), 0.5 * d ** -0.5),
        'ada_b': normal((DEPTH, 3 * d), 0.02),
        'norm_pre': near_one((DEPTH, d)),
        'norm_post': near_one((DEPTH, d)),
        'w_out': normal((DEPTH, e, d), e ** -0.5),
    }
    inputs.update(rwkv('l0_', False))
    inputs.update({
        'l1_w_in': normal((d, 4 * e), d ** -0.5),
        'l1_conv_w': normal((3, 3 * e), 3 ** -0.5),
        'l1_conv_b': normal((3 * e,), 0.02),
        'l1_f_w1': normal((HYENA_EMB, HYENA_FILTER_WIDTH), HYENA_EMB ** -0.5),
        'l1_f_b1': normal((HYENA_FILTER_WIDTH,), 0.1),
        'l1_f_w2': normal((HYENA_FILTER_WIDTH, HYENA_FILTER_WIDTH), HYENA_FILTER_WIDTH ** -0.5),
        'l1_f_b2': normal((HYENA_FILTER_WIDTH,), 0.1),
        'l1_f_w3': normal((HYENA_FILTER_WIDTH, HYENA_FILTER_WIDTH), HYENA_FILTER_WIDTH ** -0.5),
        'l1_f_b3': normal((HYENA_FILTER_WIDTH,), 0.1),
        'l1_f_w4': normal((HYENA_FILTER_WIDTH, 2 * e), HYENA_FILTER_WIDTH ** -0.5),
        'l1_sin_freq': HYENA_SIN_W * near_one((HYENA_FILTER_WIDTH,)),
        'l1_filter_bias': normal((e,), 1.0),
    })
    inputs.update({
        'l2_w_in': normal((d, 5 * e), d ** -0.5),
        'l2_g_norm': near_one((HGRN_VAL,)),
        'hgrn_lb_logits': normal((DEPTH, e), 1.0),
    })
    inputs.update(rwkv('l3_', True))
    return inputs

def first_block(x, c, ctx, c_ctx, ada_w, ada_b, norm_pre, norm_post, w_out,
              l0_w_in, l0_mu, l0_w0, l0_w2, l0_a0, l0_a2, l0_k_k, l0_k_a, l0_r_k, l0_ln_w, l0_ln_b,
              l1_w_in, l1_conv_w, l1_conv_b, l1_f_w1, l1_f_b1, l1_f_w2, l1_f_b2, l1_f_w3, l1_f_b3,
              l1_f_w4, l1_sin_freq, l1_filter_bias,
              l2_w_in, l2_g_norm, hgrn_lb_logits,
              l3_w_in, l3_mu, l3_w0, l3_w2, l3_a0, l3_a2, l3_k_k, l3_k_a, l3_r_k, l3_ln_w, l3_ln_b,
              l3_v0, l3_v2):
    rwkv0 = dict(w_in=l0_w_in, mu=l0_mu, w0=l0_w0, w2=l0_w2, a0=l0_a0, a2=l0_a2, k_k=l0_k_k,
                 k_a=l0_k_a, r_k=l0_r_k, ln_w=l0_ln_w, ln_b=l0_ln_b)
    hyena1 = dict(w_in=l1_w_in, conv_w=l1_conv_w, conv_b=l1_conv_b, f_w1=l1_f_w1, f_b1=l1_f_b1,
                  f_w2=l1_f_w2, f_b2=l1_f_b2, f_w3=l1_f_w3, f_b3=l1_f_b3, f_w4=l1_f_w4,
                  sin_freq=l1_sin_freq, filter_bias=l1_filter_bias)
    hgrn2 = dict(w_in=l2_w_in, g_norm=l2_g_norm)
    rwkv3 = dict(w_in=l3_w_in, mu=l3_mu, w0=l3_w0, w2=l3_w2, a0=l3_a0, a2=l3_a2, k_k=l3_k_k,
                 k_a=l3_k_a, r_k=l3_r_k, ln_w=l3_ln_w, ln_b=l3_ln_b, v0=l3_v0, v2=l3_v2)
    layer_params = [rwkv0, hyena1, hgrn2, rwkv3]

    lb_soft = jax.nn.softmax(hgrn_lb_logits.astype(jnp.float32), axis=0)
    lower_bounds = jnp.cumsum(lb_soft, axis=0) - lb_soft[0]

    v_first_x = None
    v_first_c = None
    for l in range(DEPTH):
        kind = l % N_MIXERS
        p = layer_params[l]
        ctx_out = l < DEPTH - 1
        sh_x, sc_x, gt_x = adaln(c[:, None, :], ada_w[l], ada_b[l])
        sh_c, sc_c, gt_c = adaln(c_ctx[None, None, :], ada_w[l], ada_b[l])
        hx = rms_norm(x, norm_pre[l]) * (1.0 + sc_x) + sh_x
        hc = rms_norm(ctx, norm_pre[l]) * (1.0 + sc_c) + sh_c
        if kind == 0:
            ux, uc, v_first_x, v_first_c = rwkv7_mixer(hx, hc, p, v_first_x, v_first_c, ctx_out)
        elif kind == 1:
            ux, uc = hyena_mixer(hx, hc, p, ctx_out)
        else:
            ux, uc = hgrn2_mixer(hx, hc, p, lower_bounds[l], ctx_out)
        x = x + rms_norm(ux @ w_out[l], norm_post[l]) * gt_x
        if ctx_out:
            ctx = ctx + rms_norm(uc @ w_out[l], norm_post[l]) * gt_c
    return x


N_BRANCH = 3
BRANCH_W = D_MODEL // 2
RET_HEADS = 4
RET_DK = BRANCH_W // RET_HEADS
DIFF_HEADS = 4
DIFF_DV = BRANCH_W // DIFF_HEADS
DIFF_DQK = DIFF_DV // 2
MLP_GROUPS = 4
MLP_GW = BRANCH_W // MLP_GROUPS
CHUNK = 128
RET_CHUNK = 128
Q_BLOCK = 128
ROPE_BASE = 10000.0
EPS = 1e-6
KV_SIZES = (BRANCH_W, BRANCH_W, BRANCH_W, BRANCH_W)
REST_SIZES = (BRANCH_W,) * 7 + (N_BRANCH * D_MODEL,)
IN_SIZES = KV_SIZES + REST_SIZES
KV_COLS = 4 * BRANCH_W
IN_COLS = KV_COLS + 7 * BRANCH_W + N_BRANCH * D_MODEL


def rms_norm_2(x, g=None):
    xf = x.astype(jnp.float32)
    y = xf * lax.rsqrt(jnp.mean(xf * xf, axis=-1, keepdims=True) + EPS)
    if g is not None:
        y = y * g.astype(jnp.float32)
    return y.astype(x.dtype)

def layer_norm(x):
    xf = x.astype(jnp.float32)
    mu = jnp.mean(xf, axis=-1, keepdims=True)
    var = jnp.mean(jnp.square(xf - mu), axis=-1, keepdims=True)
    return ((xf - mu) * lax.rsqrt(var + EPS)).astype(x.dtype)

def modulate(x, g, shift, scale):
    return rms_norm_2(x, g) * (1.0 + scale) + shift

def split_cols(z, sizes):
    idx = np.cumsum(sizes)[:-1].tolist()
    return jnp.split(z, idx, axis=-1)

def to_heads(t, n_heads):
    b, n, w = t.shape
    return t.reshape(b, n, n_heads, w // n_heads).transpose(0, 2, 1, 3)

def to_diff_heads(t):
    b, n, _ = t.shape
    return t.reshape(b, n, DIFF_HEADS, 2, DIFF_DQK).transpose(0, 2, 3, 1, 4)

def from_heads(t):
    b, h, n, d = t.shape
    return t.transpose(0, 2, 1, 3).reshape(b, n, h * d)

def rope_angles(row_pos, col_pos, head_dim):
    n_freq = head_dim // 4
    inv = ROPE_BASE ** (-jnp.arange(n_freq, dtype=jnp.float32) / n_freq)
    ang = jnp.concatenate([row_pos[:, None] * inv, col_pos[:, None] * inv], axis=-1)
    return jnp.cos(ang), jnp.sin(ang)

def apply_rope(x, cos, sin):
    x1, x2 = jnp.split(x, 2, axis=-1)
    cos = cos.astype(x.dtype)
    sin = sin.astype(x.dtype)
    return jnp.concatenate([x1 * cos - x2 * sin, x1 * sin + x2 * cos], axis=-1)

def retention_chunkwise(q, k, v, log_gamma, state0):
    in_dtype = q.dtype
    q, k, v = q.astype(jnp.float32), k.astype(jnp.float32), v.astype(jnp.float32)
    b, h, n, dk = q.shape
    dv = v.shape[-1]
    nc = n // RET_CHUNK
    qc = q.reshape(b, h, nc, RET_CHUNK, dk)
    kc = k.reshape(b, h, nc, RET_CHUNK, dk)
    vc = v.reshape(b, h, nc, RET_CHUNK, dv)
    pos = jnp.arange(RET_CHUNK, dtype=jnp.float32)
    lg = log_gamma.astype(jnp.float32)[:, None]
    dist = pos[:, None] - pos[None, :]
    d_in = jnp.where(dist >= 0, jnp.exp(lg[:, :, None] * jnp.maximum(dist, 0.0)), 0.0)
    q_dec = jnp.exp(lg * (pos + 1.0))
    k_dec = jnp.exp(lg * (RET_CHUNK - 1.0 - pos))
    chunk_dec = jnp.exp(lg[:, 0] * RET_CHUNK)
    s = jnp.einsum('bhnid,bhnjd->bhnij', qc, kc) * d_in[None, :, None]
    inner = jnp.einsum('bhnij,bhnje->bhnie', s, vc)
    kv = jnp.einsum('bhnjd,hj,bhnje->bhnde', kc, k_dec, vc)

    def step(state, kv_n):
        return chunk_dec[None, :, None, None] * state + kv_n, state

    final, prev = lax.scan(step, state0.astype(jnp.float32), jnp.moveaxis(kv, 2, 0))
    prev = jnp.moveaxis(prev, 0, 2)
    cross = jnp.einsum('bhnid,hi,bhnde->bhnie', qc, q_dec, prev)
    out = (inner + cross).reshape(b, h, n, dv)
    return out.astype(in_dtype), final

def retention_final_state(k, v, log_gamma):
    n = k.shape[2]
    w = jnp.exp(log_gamma[:, None] * (n - 1.0 - jnp.arange(n, dtype=jnp.float32)))
    return jnp.einsum('bhjd,hj,bhje->bhde', k.astype(jnp.float32), w, v.astype(jnp.float32))

def bidir_retention(q, k, v, log_gamma, state_f, state_b):
    out_f, fin_f = retention_chunkwise(q, k, v, log_gamma[0], state_f)
    out_b, fin_b = retention_chunkwise(jnp.flip(q, 2), jnp.flip(k, 2), jnp.flip(v, 2), log_gamma[1], state_b)
    return out_f + jnp.flip(out_b, 2), fin_f, fin_b

def diff_attend(q, k, v, lam):
    s = jnp.einsum('bhmqd,bhmkd->bhmqk', q.astype(jnp.float32), k.astype(jnp.float32)) * (DIFF_DQK ** -0.5)
    p = jax.nn.softmax(s, axis=-1)
    a = p[:, :, 0] - lam * p[:, :, 1]
    return jnp.einsum('bhqk,bhkv->bhqv', a, v.astype(jnp.float32)).astype(v.dtype)

def diff_attend_blocked(q, k, v, lam):
    b, h, _, n, d = q.shape
    nb = n // Q_BLOCK
    qb = jnp.moveaxis(q.reshape(b, h, 2, nb, Q_BLOCK, d), 3, 0)
    o = lax.map(lambda blk: diff_attend(blk, k, v, lam), qb)
    return jnp.moveaxis(o, 0, 2).reshape(b, h, n, -1)

def chunk_mlp(u, v, gate, w_s, b_s):
    b, n, _ = u.shape
    nch = n // CHUNK
    vn = layer_norm(v).reshape(b, nch, CHUNK, MLP_GROUPS, MLP_GW)
    sp = jnp.einsum('gij,bnjgc->bnigc', w_s, vn) + b_s.T[:, :, None]
    return u * sp.reshape(b, n, BRANCH_W) * jax.nn.silu(gate)

def merge_branches(o_ret, o_mlp, o_diff, merge_logits, w_bo, w_o):
    g_ret, g_mlp, g_diff = jnp.split(jax.nn.sigmoid(merge_logits), N_BRANCH, axis=-1)
    y = g_ret * (o_ret @ w_bo[0]) + g_mlp * (o_mlp @ w_bo[1]) + g_diff * (o_diff @ w_bo[2])
    return y @ w_o

def second_inputs(seed: int = 0) -> dict:
    key = jax.random.key(seed)
    ks = jax.random.split(key, 16)
    f32 = jnp.float32
    nrm = jax.random.normal
    x = nrm(ks[0], (BATCH, SEQ, D_MODEL), f32)
    c = nrm(ks[1], (BATCH, D_MODEL), f32)
    ctx = nrm(ks[2], (BATCH, CTX_LEN, D_MODEL), f32)
    c_ctx = nrm(ks[3], (D_MODEL,), f32)
    w_mod = nrm(ks[4], (DEPTH, D_MODEL, 3 * D_MODEL), f32) * (0.5 * D_MODEL ** -0.5)
    b_mod = 0.02 * nrm(ks[5], (DEPTH, 3 * D_MODEL), f32)
    g_pre = 1.0 + 0.05 * nrm(ks[6], (DEPTH, D_MODEL), f32)
    g_post = 1.0 + 0.05 * nrm(ks[7], (DEPTH, D_MODEL), f32)
    w_in = nrm(ks[8], (DEPTH, D_MODEL, IN_COLS), f32) * (D_MODEL ** -0.5)
    base = jnp.log(2.0 ** (5.0 + jnp.arange(RET_HEADS, dtype=f32)) - 1.0)
    ret_decay_logit = base[None, None, :] + 0.1 * nrm(ks[9], (DEPTH, 2, RET_HEADS), f32)
    mlp_w_s = nrm(ks[10], (DEPTH, MLP_GROUPS, CHUNK, CHUNK), f32) * (CHUNK ** -0.5)
    mlp_b_s = 1.0 + 0.1 * nrm(ks[11], (DEPTH, MLP_GROUPS, CHUNK), f32)
    diff_lambda_q = 0.1 * nrm(ks[12], (DEPTH, 2, DIFF_DQK), f32)
    diff_lambda_k = 0.1 * nrm(ks[13], (DEPTH, 2, DIFF_DQK), f32)
    w_branch_out = nrm(ks[14], (DEPTH, N_BRANCH, BRANCH_W, D_MODEL), f32) * (BRANCH_W ** -0.5)
    w_out = nrm(ks[15], (DEPTH, D_MODEL, D_MODEL), f32) * (D_MODEL ** -0.5)
    return {"x": x, "c": c, "ctx": ctx, "c_ctx": c_ctx, "w_mod": w_mod, "b_mod": b_mod,
            "g_pre": g_pre, "g_post": g_post, "w_in": w_in, "ret_decay_logit": ret_decay_logit,
            "mlp_w_s": mlp_w_s, "mlp_b_s": mlp_b_s, "diff_lambda_q": diff_lambda_q,
            "diff_lambda_k": diff_lambda_k, "w_branch_out": w_branch_out, "w_out": w_out}

def second_block(x, c, ctx, c_ctx, w_mod, b_mod, g_pre, g_post, w_in, ret_decay_logit,
              mlp_w_s, mlp_b_s, diff_lambda_q, diff_lambda_k, w_branch_out, w_out):
    b = x.shape[0]
    n_lat = x.shape[1]
    rows = n_lat // GRID_W
    row_pos = jnp.repeat(jnp.arange(rows, dtype=jnp.float32), GRID_W)
    col_pos = jnp.tile(jnp.arange(GRID_W, dtype=jnp.float32), rows)
    cos_r, sin_r = rope_angles(row_pos, col_pos, RET_DK)
    cos_d, sin_d = rope_angles(row_pos, col_pos, DIFF_DQK)
    silu_c = jax.nn.silu(c)
    silu_cc = jax.nn.silu(c_ctx)
    ret_scale = RET_DK ** -0.5

    for l in range(DEPTH):
        last = l == DEPTH - 1
        shift, scale, gate = jnp.split((silu_c @ w_mod[l] + b_mod[l])[:, None, :], 3, axis=-1)
        shift_c, scale_c, gate_c = jnp.split(silu_cc @ w_mod[l] + b_mod[l], 3, axis=-1)
        h = modulate(x, g_pre[l], shift, scale)
        hc = modulate(ctx, g_pre[l], shift_c, scale_c)
        log_gamma = -jax.nn.softplus(-ret_decay_logit[l].astype(jnp.float32))
        lam_init = 0.8 - 0.6 * math.exp(-0.3 * l)
        lam = (jnp.exp(jnp.sum(diff_lambda_q[l, 0] * diff_lambda_k[l, 0]))
               - jnp.exp(jnp.sum(diff_lambda_q[l, 1] * diff_lambda_k[l, 1])) + lam_init).astype(jnp.float32)

        if last:
            c_rk, c_rv, c_dk, c_dv = split_cols(hc @ w_in[l][:, :KV_COLS], KV_SIZES)
        else:
            zc = split_cols(hc @ w_in[l], IN_SIZES)
            c_rk, c_rv, c_dk, c_dv = zc[:4]
        crk = to_heads(c_rk, RET_HEADS) * ret_scale
        crv = to_heads(c_rv, RET_HEADS)
        cdk = to_diff_heads(c_dk)
        cdv = to_heads(c_dv, DIFF_HEADS)
        if last:
            s_f = retention_final_state(crk, crv, log_gamma[0])
            s_b = retention_final_state(jnp.flip(crk, 2), jnp.flip(crv, 2), log_gamma[1])
        else:
            c_rq, c_rg, c_dq, c_dg, c_mu, c_mv, c_mg, c_mlog = zc[4:]
            zero = jnp.zeros((b, RET_HEADS, RET_DK, RET_DK), jnp.float32)
            c_ret, s_f, s_b = bidir_retention(to_heads(c_rq, RET_HEADS), crk, crv, log_gamma, zero, zero)
            co_ret = from_heads(rms_norm_2(c_ret)) * jax.nn.silu(c_rg)
            c_diff = diff_attend(to_diff_heads(c_dq), cdk, cdv, lam)
            co_diff = from_heads(rms_norm_2(c_diff) * (1.0 - lam_init)) * jax.nn.silu(c_dg)
            co_mlp = chunk_mlp(c_mu, c_mv, c_mg, mlp_w_s[l], mlp_b_s[l])
            c_out = merge_branches(co_ret, co_mlp, co_diff, c_mlog, w_branch_out[l], w_out[l])
            ctx_next = ctx + gate_c * rms_norm_2(c_out, g_post[l])

        rk_, rv_, dk_, dv_, rq_, rg_, dq_, dg_, mu_, mv_, mg_, mlog_ = split_cols(h @ w_in[l], IN_SIZES)
        rq = apply_rope(to_heads(rq_, RET_HEADS), cos_r, sin_r)
        rk = apply_rope(to_heads(rk_, RET_HEADS), cos_r, sin_r) * ret_scale
        rv = to_heads(rv_, RET_HEADS)
        ret_o, _, _ = bidir_retention(rq, rk, rv, log_gamma, s_f, s_b)
        o_ret = from_heads(rms_norm_2(ret_o)) * jax.nn.silu(rg_)

        dq = apply_rope(to_diff_heads(dq_), cos_d, sin_d)
        dk = apply_rope(to_diff_heads(dk_), cos_d, sin_d)
        dv = to_heads(dv_, DIFF_HEADS)
        k_all = jnp.concatenate([cdk, dk], axis=3)
        v_all = jnp.concatenate([cdv, dv], axis=2)
        diff_o = diff_attend_blocked(dq, k_all, v_all, lam)
        o_diff = from_heads(rms_norm_2(diff_o) * (1.0 - lam_init)) * jax.nn.silu(dg_)

        o_mlp = chunk_mlp(mu_, mv_, mg_, mlp_w_s[l], mlp_b_s[l])
        out = merge_branches(o_ret, o_mlp, o_diff, mlog_, w_branch_out[l], w_out[l])
        x = x + gate * rms_norm_2(out, g_post[l])
        if not last:
            ctx = ctx_next
    return x


def setup_inputs(seed=0):
    out = dict(first_inputs(seed))
    for name, value in second_inputs(seed + 1).items():
        if name != "x":
            out[name + "_2"] = value
    return out


def reference(
    x, c, ctx, c_ctx, ada_w, ada_b, norm_pre, norm_post, w_out, l0_w_in, l0_mu, l0_w0, l0_w2,
    l0_a0, l0_a2, l0_k_k, l0_k_a, l0_r_k, l0_ln_w, l0_ln_b, l1_w_in, l1_conv_w, l1_conv_b,
    l1_f_w1, l1_f_b1, l1_f_w2, l1_f_b2, l1_f_w3, l1_f_b3, l1_f_w4, l1_sin_freq, l1_filter_bias,
    l2_w_in, l2_g_norm, hgrn_lb_logits, l3_w_in, l3_mu, l3_w0, l3_w2, l3_a0, l3_a2, l3_k_k,
    l3_k_a, l3_r_k, l3_ln_w, l3_ln_b, l3_v0, l3_v2, c_2, ctx_2, c_ctx_2, w_mod_2, b_mod_2,
    g_pre_2, g_post_2, w_in_2, ret_decay_logit_2, mlp_w_s_2, mlp_b_s_2, diff_lambda_q_2,
    diff_lambda_k_2, w_branch_out_2, w_out_2,
):
    x = first_block(
        x, c, ctx, c_ctx, ada_w, ada_b, norm_pre, norm_post, w_out, l0_w_in, l0_mu, l0_w0,
        l0_w2, l0_a0, l0_a2, l0_k_k, l0_k_a, l0_r_k, l0_ln_w, l0_ln_b, l1_w_in, l1_conv_w,
        l1_conv_b, l1_f_w1, l1_f_b1, l1_f_w2, l1_f_b2, l1_f_w3, l1_f_b3, l1_f_w4, l1_sin_freq,
        l1_filter_bias, l2_w_in, l2_g_norm, hgrn_lb_logits, l3_w_in, l3_mu, l3_w0, l3_w2, l3_a0,
        l3_a2, l3_k_k, l3_k_a, l3_r_k, l3_ln_w, l3_ln_b, l3_v0, l3_v2,
    )
    return second_block(
        x, c_2, ctx_2, c_ctx_2, w_mod_2, b_mod_2, g_pre_2, g_post_2, w_in_2, ret_decay_logit_2,
        mlp_w_s_2, mlp_b_s_2, diff_lambda_q_2, diff_lambda_k_2, w_branch_out_2, w_out_2,
    )


_drawn_inputs = setup_inputs


def setup_inputs(seed=0):
    import zlib

    import numpy as np

    out = dict(_drawn_inputs(seed))
    spreads = {}
    factors = {'l0_a0': 4.612,
     'l0_ln_w': 3.661,
     'l0_ln_b': 8.0,
     'l1_conv_b': 4.023,
     'g_post_2': 2.89,
     'diff_lambda_q_2': 4.462,
     'diff_lambda_k_2': 8.0}
    for name, (base, spread) in spreads.items():
        noise = np.random.default_rng([zlib.crc32(name.encode()), seed]).standard_normal(out[name].shape)
        drawn = base * np.exp(spread * noise) if base else spread * noise
        out[name] = jnp.asarray(drawn.astype(out[name].dtype))
    for name, factor in factors.items():
        out[name] = (out[name] * factor).astype(out[name].dtype)
    return out
```

```python
import math
from contextlib import ExitStack, contextmanager

import numpy as np

import concourse.bass as bass
from concourse import mybir

F32 = mybir.dt.float32
ALU = mybir.AluOpType
ACT = mybir.ActivationFunctionType
AX_X = mybir.AxisListType.X
ds = bass.ds

P = 128
D = 1024
KD = D // P
E = 2048
KE = E // P
NX = 256
NT = 2 * NX
GRID = 64
HEAD = 64
C = 64
NCH = NT // C
LORA = 64
LEVELS = 6
EPS = 1e-6
GN_EPS = 64e-5
DECAY = math.exp(-0.5)
BW = 512
KB = BW // P
HEADS = 4
V_W0, V_A0, V_KK, V_KA, V_RK, V_LNW, V_LNB = 0, 2, 4, 5, 6, 7, 8
RING = 8
BIG = float(2 ** 23) * 1.5


class Named:
    pass


class Steps:

    def __init__(self, eng, sem):
        self.eng, self.sem, self.n = eng, sem, 0

    def __call__(self, ins):
        self.n += 1
        ins.then_inc(self.sem, 1)
        return self.n

    def wait(self, n=None):
        self.eng.wait_ge(self.sem, self.n if n is None else n)


STAGES = [0]


@contextmanager
def stage(nc, *names):
    with ExitStack() as c:
        STAGES[0] += 1
        sems = [c.enter_context(nc.semaphore(f"{n}_{STAGES[0]}")) for n in names]
        with nc.Block() as block:
            yield block, dict(zip(names, sems))
        for s in sems:
            nc.gpsimd.sem_clear(s)
        nc.all_engine_barrier()


@contextmanager
def repeat(eng, n):
    if n == 1:
        yield 0
    else:
        with eng.Fori(0, n) as i:
            yield i


def dense(nc, R, w, M, K, N, rhs, out, evac=None):
    S = max(1, K // 8)
    width = K * P // S
    G = min(M, RING // S)
    assert M % G == 0 and (G % 4 == 0)
    with stage(nc, *[f"w_loaded{s}" for s in range(RING)], "tile_done", "bank_free", "part") as (block, s):
        loaded = [s[f"w_loaded{j}"] for j in range(RING)]

        @block.sync
        def _(sp):
            with repeat(sp, M // G) as i:
                for j in range(G):
                    sp.wait_ge(s["tile_done"], i * G + (j + 1))
                    for h in range(S):
                        src = w[ds(i * G + j, 1), :, h * width:(h + 1) * width].rearrange("a p n -> p (a n)")
                        sp.dma_start(R.ring[:, j * S + h, 0:width], src).then_inc(loaded[j * S + h], 16)

        @block.tensor
        def _(pe):
            pe.sem_inc(s["tile_done"], G)
            with repeat(pe, M // G) as i:
                for j in range(G):
                    pe.wait_ge(s["bank_free"], i * G + (j + 1))
                    for k in range(K):
                        if k % 8 == 0:
                            pe.wait_ge(loaded[j * S + k // 8], i * 16 + 16)
                        a = (k % 8) * P
                        mm = pe.matmul(R.ps[:, j % 4, 0:N], R.ring[:, j * S + k // 8, a:a + P], rhs(k),
                                       start=(k == 0), stop=(k == K - 1))
                    mm.then_inc(s["tile_done"], 1)

        @block.vector
        def _(dve):
            dve.sem_inc(s["bank_free"], 4)
            with repeat(dve, M // G) as i:
                for j in range(G):
                    dve.wait_ge(s["tile_done"], i * G + (G + j + 1))
                    if evac is None:
                        last = dve.tensor_copy(out(i * G + j), R.ps[:, j % 4, 0:N])
                    else:
                        last = evac(dve, s, i * G + j, i * G + j, j % 4)
                    last.then_inc(s["bank_free"], 1)


def token_major(nc, R, w, rhs, ntiles, out):
    with stage(nc, "w_loaded", "done", "copied") as (block, s):
        wt = R.ring[:, 0:4, :].rearrange("p a (b n) -> p (a b) n", n=512)

        @block.sync
        def _(sp):
            sp.dma_start(wt, w).then_inc(s["w_loaded"], 16)

        @block.tensor
        def _(pe):
            pe.wait_ge(s["w_loaded"], 16)
            for t in range(ntiles):
                for k in range(KD):
                    mm = pe.matmul(R.ps[:, t, :], rhs(k, t), wt[:, k, :], start=(k == 0), stop=(k == KD - 1))
                mm.then_inc(s["done"], 1)

        @block.vector
        def _(dve):
            for t in range(ntiles):
                dve.wait_ge(s["done"], t + 1)
                dve.tensor_copy(out(t), R.ps[:, t, :]).then_inc(s["copied"], 1)


def inverse_rms(nc, R, src, rstd, N, width, tiles):
    with stage(nc, "squared", "summed", "mean", "root", "used") as (block, s):
        @block.scalar
        def _(act):
            for t in range(tiles):
                act.activation(R.sq[:, t, 0:N], src(t), ACT.Square).then_inc(s["squared"], 1)
            act.wait_ge(s["mean"], 1)
            act.activation(rstd, rstd, ACT.Sqrt).then_inc(s["root"], 1)

        @block.tensor
        def _(pe):
            for t in range(tiles):
                pe.wait_ge(s["squared"], t + 1)
                mm = pe.matmul(R.ps[:, 0, 0:N], R.ones[:, :], R.sq[:, t, 0:N], start=(t == 0), stop=(t == tiles - 1))
            mm.then_inc(s["summed"], 1)

        @block.vector
        def _(dve):
            dve.wait_ge(s["summed"], 1)
            dve.tensor_scalar(rstd, R.ps[:, 0, 0:N], 1.0 / width, EPS, ALU.mult, ALU.add).then_inc(s["mean"], 1)
            dve.wait_ge(s["root"], 1)
            dve.reciprocal(rstd, rstd).then_inc(s["used"], 1)


def modulate(nc, R, mods, g, N):
    inverse_rms(nc, R, lambda t: R.x[:, t, 0:N], R.rstd[:, 0:N], N, D, KD)
    with stage(nc, "gain", "scaled", "shifted") as (block, s):
        @block.vector
        def _(dve):
            for c in range(N // NX):
                dve.scalar_tensor_tensor(R.gain[:, c, :], mods[:, c, KD:2 * KD], 1.0, g, ALU.add, ALU.mult).then_inc(s["gain"], 1)
            for k in range(KD):
                dve.tensor_tensor(R.h[:, k, 0:N], R.x[:, k, 0:N], R.rstd[:, 0:N], ALU.mult).then_inc(s["scaled"], 1)

        @block.scalar
        def _(act):
            act.wait_ge(s["gain"], N // NX)
            for k in range(KD):
                act.wait_ge(s["scaled"], k + 1)
                for c in range(N // NX):
                    cols = slice(c * NX, (c + 1) * NX)
                    act.activation(R.h[:, k, cols], R.h[:, k, cols], ACT.Identity, bias=mods[:, c, k:k + 1],
                                   scale=R.gain[:, c, k:k + 1]).then_inc(s["shifted"], 1)


def add_back(nc, R, o, mods, g, N):
    inverse_rms(nc, R, lambda t: o[:, t, 0:N], R.rstd[:, 0:N], N, D, KD)
    with stage(nc, "gain", "scaled", "added") as (block, s):
        @block.vector
        def _(dve):
            for c in range(N // NX):
                dve.tensor_tensor(R.gain[:, c, :], mods[:, c, 2 * KD:3 * KD], g, ALU.mult).then_inc(s["gain"], 1)
            for k in range(KD):
                dve.tensor_tensor(o[:, k, 0:N], o[:, k, 0:N], R.rstd[:, 0:N], ALU.mult).then_inc(s["scaled"], 1)
            dve.wait_ge(s["gain"], N // NX)
            for k in range(KD):
                dve.wait_ge(s["scaled"], k + 1)
                for c in range(N // NX):
                    cols = slice(c * NX, (c + 1) * NX)
                    dve.scalar_tensor_tensor(R.x[:, k, cols], o[:, k, cols], R.gain[:, c, k:k + 1],
                                             R.x[:, k, cols], ALU.mult, ALU.add).then_inc(s["added"], 1)


def alloc(nc, R, sb, c):
    R.x = sb("x", KD, NT)
    R.h = sb("h", KD, NT)
    R.sq = sb("sq", KD, NT)
    R.ring = sb("ring", RING, D)
    R.eye, R.ones, R.head_ones = sb("eye", P), sb("ones", P), sb("head_ones", P)
    R.cond, R.vec = sb("cond", KD, 4), sb("vec", 9, 24)
    R.mods_raw, R.mods = sb("mods_raw", 4, 24, 2), sb("mods", 4, 2, 24)
    R.rstd, R.gain, R.eps = sb("rstd", NT), sb("gain", 2, KD), sb("eps", 1)
    R.ps = c.enter_context(nc.psum_tensor("ps", [P, 8, 512], F32))


def setup(nc, R, I):
    with stage(nc, "loaded", "silu", "ones") as (block, s):
        loads = [(R.x[:, :, :], I["x_t"]), (R.eye[:, :], I["eye"]), (R.head_ones[:, :], I["head_ones"]),
                 (R.cond[:, :, :], I["cond"]), (R.vec[:, :, :], I["vectors"])]

        @block.sync
        def _(sp):
            for dst, src in loads:
                sp.dma_start(dst, src).then_inc(s["loaded"], 16)

        @block.gpsimd
        def _(pool):
            pool.memset(R.ones[:, :], 1.0).then_inc(s["ones"], 1)
            pool.memset(R.eps[:, :], EPS).then_inc(s["ones"], 1)

        @block.scalar
        def _(act):
            act.wait_ge(s["loaded"], 16 * len(loads))
            act.activation(R.cond[:, :, :], R.cond[:, :, :], ACT.Silu).then_inc(s["silu"], 1)
    for n, w in enumerate((I["ada0"], I["ada1"], I["mod0"], I["mod1"])):
        a = 2 * (n // 2)
        dense(nc, R, w, 3 * KD, KD, 2, lambda k: R.cond[:, k, a:a + 2], lambda m: R.mods_raw[:, n, ds(m, 1), :].rearrange("p a c -> p (a c)"))
    with stage(nc, "bias") as (block, s):
        @block.vector
        def _(dve):
            for n in range(4):
                for c in range(2):
                    dve.tensor_tensor(R.mods[:, n, c, :], R.mods_raw[:, n, :, c], R.vec[:, n, 0:24], ALU.add).then_inc(s["bias"], 1)



def shift_mix(nc, R, W, I):
    with stage(nc, "diff", "loaded") as (block, s):
        @block.sync
        def _(sp):
            sp.dma_start(W.mu[:, :, :], I["mu"]).then_inc(s["loaded"], 16)
            sp.wait_ge(s["loaded"], 16)

        @block.vector
        def _(dve):
            step = Steps(dve, s["diff"])
            h, d = R.h, R.sq
            for q in range(4):
                ks = slice(2 * q, 2 * q + 2)
                for k in (2 * q, 2 * q + 1):
                    hg = h[:, k, 0:NX].rearrange("p (r c) -> p r c", c=GRID)
                    dg = d[:, k, 0:NX].rearrange("p (r c) -> p r c", c=GRID)
                    if q == 0:
                        step(dve.tensor_tensor(dg[:, :, 1:], hg[:, :, :-1], hg[:, :, 1:], ALU.subtract))
                        step(dve.tensor_scalar(dg[:, :, 0:1], hg[:, :, 0:1], -1.0, None, ALU.mult))
                    elif q == 1:
                        step(dve.tensor_tensor(dg[:, :, :-1], hg[:, :, 1:], hg[:, :, :-1], ALU.subtract))
                        step(dve.tensor_scalar(dg[:, :, GRID - 1:], hg[:, :, GRID - 1:], -1.0, None, ALU.mult))
                    elif q == 2:
                        step(dve.tensor_tensor(dg[:, 1:, :], hg[:, :-1, :], hg[:, 1:, :], ALU.subtract))
                        step(dve.tensor_scalar(dg[:, 0:1, :], hg[:, 0:1, :], -1.0, None, ALU.mult))
                    else:
                        step(dve.tensor_tensor(dg[:, :-1, :], hg[:, 1:, :], hg[:, :-1, :], ALU.subtract))
                        step(dve.tensor_scalar(dg[:, 3:4, :], hg[:, 3:4, :], -1.0, None, ALU.mult))
            a, b = h[:, 0:4, NX:], d[:, 0:4, NX:]
            step(dve.tensor_tensor(b[:, :, 1:], a[:, :, :-1], a[:, :, 1:], ALU.subtract))
            step(dve.tensor_scalar(b[:, :, 0:1], a[:, :, 0:1], -1.0, None, ALU.mult))
            a, b = h[:, 4:8, NX:], d[:, 4:8, NX:]
            step(dve.tensor_tensor(b[:, :, :-1], a[:, :, 1:], a[:, :, :-1], ALU.subtract))
            step(dve.tensor_scalar(b[:, :, NX - 1:], a[:, :, NX - 1:], -1.0, None, ALU.mult))

    def mixes(groups):
        with stage(nc, "mixed") as (block, s):
            @block.vector
            def _(dve):
                for g, dst, N in groups:
                    for k in range(KD):
                        dve.scalar_tensor_tensor(dst[:, k, 0:N], R.sq[:, k, 0:N], W.mu[:, g, k:k + 1],
                                                 R.h[:, k, 0:N], ALU.mult, ALU.add).then_inc(s["mixed"], 1)

    mixes([(4, W.mix_k, NT), (5, W.mix_v, NT)])
    with stage(nc, "loaded", "done", "tanh") as (block, s):
        wt = R.ring[:, 0:2, :].rearrange("p a (k n) -> p a k n", n=P)

        @block.sync
        def _(sp):
            sp.dma_start(R.ring[:, 0:2, :], I["w_low"]).then_inc(s["loaded"], 16)

        @block.tensor
        def _(pe):
            pe.wait_ge(s["loaded"], 16)
            for n, mix in enumerate((W.mix_k, W.mix_v)):
                for k in range(KD):
                    mm = pe.matmul(R.ps[:, n, :], wt[:, n, k, :], mix[:, k, :], start=(k == 0), stop=(k == KD - 1))
                mm.then_inc(s["done"], 1)

        @block.scalar
        def _(act):
            act.wait_ge(s["done"], 1)
            act.activation(W.low[:, 0, :], R.ps[:, 0, :], ACT.Tanh).then_inc(s["tanh"], 1)
            act.wait_ge(s["done"], 2)
            act.activation(W.low[:, 1, :], R.ps[:, 1, :], ACT.Copy).then_inc(s["tanh"], 1)

    mixes([(0, W.mix_r, NX), (1, W.mix_k, NT), (2, W.mix_v, NT), (3, W.mix_g, NX)])


def nat(p):
    return 64 * p


def oth(p):
    return 64 - 64 * p


def rwkv_layer(nc, R, I):
    with ExitStack() as c:
        def sb(name, *shape):
            return c.enter_context(nc.sbuf_tensor(name, [P, *shape], F32))

        W = Named()
        W.mix_r, W.mix_g = sb("mix_r", KD, NX), sb("mix_g", KD, NX)
        W.mix_k, W.mix_v = sb("mix_k", KD, NT), sb("mix_v", KD, NT)
        W.low = sb("low", 2, NT)
        with ExitStack() as c2:
            W.mu = c2.enter_context(nc.sbuf_tensor("mu", [P, 6, KD], F32))
            shift_mix(nc, R, W, I)
        W.u_pairs = R.ring[:, 4:8, :].rearrange("p a (k n) -> p (a k) n", n=NX)
        hv = R.h[:, :, :]
        W.r, W.gate = hv[:, 0, 0:NX], hv[:, 0, NX:]
        W.k, W.kk, W.ksum, W.k1, W.k2, W.cum = (hv[:, n, :] for n in range(1, 7))
        W.sg = hv[:, 7, :]
        sv = R.sq[:, :, :]
        W.t0, W.t1, W.t2 = sv[:, 0, :], sv[:, 1, :], sv[:, 2, :]
        W.vtok = sv[:, 3, :].rearrange("p (j n) -> p j n", n=P)
        W.ytok = sv[:, 4, 0:NX].rearrange("p (j n) -> p j n", n=P)
        W.bonus = sv[:, 4, NX:].rearrange("p (j n) -> p j n", n=P)
        W.rate = sv[:, 5, :]
        W.tmp = sv[:, 6, :]
        W.tmp2 = sv[:, 7, :]
        W.pv = sb("pair_vec", 10)
        W.lw = sb("lora_w", 2, P)
        W.masks = R.x[:, 6:8, NX:].rearrange("p z (q n) -> p z q n", n=P)
        W.lmask = R.x[:, 0:LEVELS, NX:].rearrange("p l (z n) -> p l z n", n=P)
        W.bk = sb("bk", NCH, P)
        W.ar = sb("ar", 2, NCH, P)
        W.A = sb("A", 2, 2, 4, 2, P)
        W.BK = sb("BK", 2, 2, 4, 2, HEAD)
        W.U = sb("U", 2, 2, 4, P)
        W.Tm = sb("Tm", 2, 4, P)
        W.Y = sb("Y", 2, 4, P)
        W.At = sb("At", 2, 4, P)
        W.pc = sb("pc", 2, NCH)
        W.H = sb("H", 2, 2, HEAD)
        W.HP = sb("HP", 2, 2, HEAD)
        W.Xs = sb("Xs", 2, 2, HEAD)
        W.Z = sb("Z", 2, 2, HEAD)
        W.st = sb("stats", 4, 4)
        W.coef = sb("coef", 4)
        W.yc = W.t0[:, 0:NX]
        W.reset = R.rstd
        with stage(nc, "loaded", "zeroed") as (block, s):
            @block.sync
            def _(sp):
                sp.dma_start(W.masks[:, :, :, :], I["masks"]).then_inc(s["loaded"], 16)
                sp.dma_start(W.lmask[:, :, :, :], I["level_masks"]).then_inc(s["loaded"], 16)
                sp.wait_ge(s["loaded"], 32)

            @block.vector
            def _(dve):
                step = Steps(dve, s["zeroed"])
                step(dve.memset(W.reset[:, :], 1.0))
                step.wait()
                step(dve.memset(W.reset[:, :].rearrange("p (c t) -> p c t", t=C)[:, :, 0:1], 0.0))
                step(dve.memset(W.At[:, :, :, :], 0.0))
                step(dve.memset(W.ar[:, :, :, :], 0.0))
        with nc.Fori(0, KE) as pair:
            rwkv_project(nc, R, W, I, pair)
            for z in range(2):
                rwkv_direction(nc, R, W, z)
                rwkv_inverse(nc, R, W, z)
            rwkv_scan(nc, R, W)
            rwkv_readout(nc, R, W, pair)
        uT = W.mix_k[:, :, :].rearrange("p a (b n) -> p (a b) n", n=NX)
        with stage(nc, "moved") as (block, s):
            @block.vector
            def _(dve):
                dve.tensor_copy(uT, W.u_pairs).then_inc(s["moved"], 1)
        dense(nc, R, I["w_out0"], KD, KE, NX, lambda k: uT[:, k, :], lambda m: R.h[:, ds(m, 1), 0:NX].rearrange("p a n -> p (a n)"))
    add_back(nc, R, R.h, R.mods[:, 0], R.vec[:, 5, 0:KD], NX)


def rwkv_project(nc, R, W, I, pair):
    with stage(nc, "w_loaded", "v_loaded", "k_done", "r_done", "g_done", "v_done", "k_out", "vt_out", "r_out", "g_out",
               "sq_out", "norm_sum", "root", "chain") as (block, s):
        wt = R.ring[:, 0:4, :].rearrange("p a (k n) -> p a k n", n=P)

        @block.sync
        def _(sp):
            for n in range(4):
                sp.dma_start(R.ring[:, n, :], I["w_rkvg"][ds(pair, 1), :, n * D:(n + 1) * D].rearrange("a p n -> p (a n)")).then_inc(s["w_loaded"], 16)
                if n == 0:
                    sp.wait_ge(s["w_loaded"], 16)

        @block.scalar
        def _(act):
            act.dma_start(W.pv[:, :], I["pair_vec"][ds(pair, 1)].rearrange("a p n -> p (a n)")).then_inc(s["v_loaded"], 16)
            act.dma_start(W.lw[:, :, :], I["lora"][ds(pair, 1)].rearrange("a p z n -> p (a z) n")).then_inc(s["v_loaded"], 16)
            act.wait_ge(s["v_loaded"], 32)
            act.wait_ge(s["k_out"], 1)
            act.activation(W.t0, W.k, ACT.Square, scale=W.pv[:, V_KK:V_KK + 1]).then_inc(s["sq_out"], 1)
            act.wait_ge(s["v_done"], 1)
            act.activation(W.vtok.rearrange("p j n -> p (j n)"), R.ps[:, 1, :], ACT.Copy).then_inc(s["vt_out"], 1)
            act.wait_ge(s["r_done"], 1)
            act.activation(W.r, R.ps[:, 2, 0:NX], ACT.Copy).then_inc(s["r_out"], 1)
            act.wait_ge(s["norm_sum"], 1)
            act.activation(W.t1, R.ps[:, 4, :], ACT.Sqrt).then_inc(s["root"], 1)
            act.wait_ge(s["g_done"], 1)
            act.activation(W.gate, R.ps[:, 3, 0:NX], ACT.Silu).then_inc(s["g_out"], 1)

        @block.tensor
        def _(pe):
            pe.wait_ge(s["w_loaded"], 16)
            for k in range(KD):
                mm = pe.matmul(R.ps[:, 0, :], wt[:, 0, k, :], W.mix_k[:, k, :], start=(k == 0), stop=(k == KD - 1))
            mm.then_inc(s["k_done"], 1)
            pe.wait_ge(s["w_loaded"], 64)
            for j in range(4):
                for k in range(KD):
                    mm = pe.matmul(R.ps[:, 1, j * P:(j + 1) * P], W.mix_v[:, k, j * P:(j + 1) * P], wt[:, 1, k, :],
                                   start=(k == 0), stop=(k == KD - 1))
            mm.then_inc(s["v_done"], 1)
            pe.wait_ge(s["sq_out"], 1)
            pe.matmul(R.ps[:, 4, :], R.head_ones[:, :], W.t0, start=True, stop=True).then_inc(s["norm_sum"], 1)
            for n, mix, bank, sem in ((2, W.mix_r, 2, s["r_done"]), (3, W.mix_g, 3, s["g_done"])):
                for k in range(KD):
                    mm = pe.matmul(R.ps[:, bank, 0:NX], wt[:, n, k, :], mix[:, k, :], start=(k == 0), stop=(k == KD - 1))
                mm.then_inc(sem, 1)

        @block.vector
        def _(dve):
            step = Steps(dve, s["chain"])
            dve.wait_ge(s["k_done"], 1)
            dve.tensor_copy(W.k, R.ps[:, 0, :]).then_inc(s["k_out"], 1)
            dve.wait_ge(s["k_out"], 1)
            dve.wait_ge(s["v_loaded"], 32)
            step(dve.tensor_scalar(W.k1, W.k, W.pv[:, V_KA:V_KA + 1], None, ALU.mult))
            step(dve.tensor_scalar(W.kk, W.k, W.pv[:, V_KK:V_KK + 1], None, ALU.mult))
            step.wait()
            step(dve.tensor_tensor(W.k2, W.k, W.k1, ALU.subtract))
            dve.wait_ge(s["root"], 1)
            step(dve.tensor_scalar(W.t1, W.t1, 1e-12, None, ALU.max))
            step.wait()
            step(dve.reciprocal(W.t1, W.t1))
            step.wait()
            step(dve.tensor_tensor(W.kk, W.kk, W.t1, ALU.mult))


def rwkv_direction(nc, R, W, z):
    with stage(nc, "low_done", "sig", "scan", "exps_in", "exps", "packed", "chain", "a_done", "a_out", "t_done", "t_out", "at_out") as (block, s):
        chunks = lambda ap: ap.rearrange("p (c t) -> p c t", t=C)
        par = lambda ap, p: ap.rearrange("p (j q t) -> p j q t", q=2, t=C)[:, :, p, :]

        @block.tensor
        def _(pe):
            for n in range(2):
                pe.matmul(R.ps[:, n, :], W.lw[z * 64:z * 64 + 64, n, :], W.low[z * 64:z * 64 + 64, n, :],
                          start=True, stop=True).then_inc(s["low_done"], 1)
            pe.wait_ge(s["packed"], 8)
            for g in range(4):
                h, jj = g // 2, g % 2
                for q in range(4):
                    j, p = 2 * jj + q // 2, q % 2
                    mm = pe.matmul(R.ps[:, 2 + g, q * P:(q + 1) * P], W.bk[h * 64:h * 64 + 64, 2 * j + p, :],
                                   W.ar[h * 64:h * 64 + 64, z, 2 * j + p, :], start=True, stop=True)
                mm.then_inc(s["a_done"], 1)
            for h in range(2):
                pe.wait_ge(s["a_done"], 4)
                pe.wait_ge(s["sig"], 2)
                for cch in range(NCH):
                    mm = pe.transpose(R.ps[:, 6 + h, cch * 64:(cch + 1) * 64], W.bk[h * 64:h * 64 + 64, cch, :],
                                      R.eye[h * 64:h * 64 + 64, h * 64:h * 64 + 64])
                mm.then_inc(s["t_done"], 1)

        @block.scalar
        def _(act):
            act.wait_ge(s["low_done"], 1)
            act.activation(W.sg, R.ps[:, 0, :], ACT.Sigmoid, bias=W.pv[:, V_W0 + z:V_W0 + z + 1]).then_inc(s["sig"], 1)
            act.wait_ge(s["low_done"], 2)
            act.activation(W.rate, R.ps[:, 1, :], ACT.Sigmoid, bias=W.pv[:, V_A0 + z:V_A0 + z + 1]).then_inc(s["sig"], 1)
            act.wait_ge(s["exps_in"], 1)
            act.activation(W.t0, W.cum, ACT.Exp, scale=-DECAY).then_inc(s["exps"], 1)
            act.activation(W.t2, W.cum, ACT.Exp, scale=DECAY).then_inc(s["exps"], 1)
            act.wait_ge(s["exps_in"], 2)
            act.activation(W.t1, W.t1, ACT.Exp, scale=-DECAY).then_inc(s["exps"], 1)
            act.activation(W.pc[:, z, :], W.pc[:, z, :], ACT.Exp, scale=-DECAY).then_inc(s["exps"], 1)
            for h in range(2):
                act.wait_ge(s["t_done"], h + 1)
                act.activation(W.BK[:, z, h].rearrange("p j q n -> p (j q n)"), R.ps[:, 6 + h, :], ACT.Copy).then_inc(s["t_out"], 1)

        @block.vector
        def _(dve):
            step = Steps(dve, s["chain"])
            dve.wait_ge(s["sig"], 1)
            step(dve.tensor_tensor_scan(W.cum, W.reset[:, :], W.sg, 0.0, ALU.mult, ALU.add))
            step.wait()
            tot = chunks(W.cum)[:, :, C - 1:C]
            step(dve.tensor_copy(W.pc[:, z, :], tot.rearrange("p c o -> p (c o)")))
            if z == 0:
                dve.tensor_tensor(W.t1, W.cum, W.sg, ALU.subtract).then_inc(s["exps_in"], 2)
                last = s["exps_in"]
            else:
                step(dve.tensor_tensor(chunks(W.t1), tot.broadcast_to([P, NCH, C]), chunks(W.cum), ALU.subtract))
                step.wait()
                dve.tensor_tensor(W.cum, W.t1, W.sg, ALU.add).then_inc(s["exps_in"], 2)
            dve.wait_ge(s["sig"], 2)
            step(dve.tensor_tensor(W.tmp, W.rate, W.k1, ALU.mult))
            step.wait()
            step(dve.tensor_tensor(W.tmp, W.tmp, W.k2, ALU.add))
            step(dve.tensor_tensor(W.tmp2, W.rate, W.kk, ALU.mult))
            step.wait()
            if z == 0:
                step(dve.tensor_copy(W.ksum, W.tmp))
            else:
                step(dve.tensor_tensor(W.ksum, W.ksum, W.tmp, ALU.add))
            bk = W.bk[:, :, :].rearrange("p (j q) n -> p j q n", q=2)
            ar = W.ar[:, z].rearrange("p (j q) n -> p j q n", q=2)
            dve.wait_ge(s["exps"], 2)
            for p in range(2):
                dve.tensor_tensor(bk[:, :, p, nat(p):nat(p) + 64], par(W.tmp, p), par(W.t2, p), ALU.mult).then_inc(s["packed"], 1)
                dve.tensor_tensor(bk[:, :, p, oth(p):oth(p) + 64], par(W.tmp2, p), par(W.t2, p), ALU.mult).then_inc(s["packed"], 1)
                dve.tensor_tensor(ar[:, 0:2, p, nat(p):nat(p) + 64], par(W.r, p), par(W.t0[:, 0:NX], p), ALU.mult).then_inc(s["packed"], 1)
            dve.wait_ge(s["exps"], 3)
            for p in range(2):
                dve.scalar_tensor_tensor(ar[:, :, p, oth(p):oth(p) + 64], par(W.t1, p), -1.0, par(W.kk, p), ALU.mult, ALU.mult).then_inc(s["packed"], 1)
            for g in range(4):
                h, jj = g // 2, g % 2
                dve.wait_ge(s["a_done"], g + 1)
                src = R.ps[:, 2 + g, :].rearrange("p (j q) -> p j q", q=2 * P)
                dst = W.A[:, z, h, 2 * jj:2 * jj + 2].rearrange("p j q n -> p j (q n)")
                mask = W.masks[:, z].rearrange("p q n -> p (q n)").unsqueeze(1).broadcast_to([P, 2, 2 * P])
                dve.tensor_tensor(dst, src, mask, ALU.mult).then_inc(s["a_out"], 1)
            for h in range(2):
                dve.wait_ge(s["a_out"], 2 * h + 2)
                dve.tensor_copy(W.At[0:64, h, :, 0:64], W.A[0:64, z, h, :, 1, 0:64]).then_inc(s["at_out"], 1)
                dve.tensor_copy(W.At[64:128, h, :, 64:128], W.A[64:128, z, h, :, 0, 64:128]).then_inc(s["at_out"], 1)


def rwkv_inverse(nc, R, W, z):
    with stage(nc, "y_done", "t_done", "y_out", "t_out", "u_out") as (block, s):
        lm = lambda l, zz: W.lmask[:, l, zz, :].unsqueeze(1).broadcast_to([P, 4, P])
        eye4 = R.eye[:, :].unsqueeze(1).broadcast_to([P, 4, P])
        bank = lambda n: R.ps[:, n, :].rearrange("p (j n) -> p j n", n=P)

        @block.tensor
        def _(pe):
            for l in range(LEVELS):
                for h in range(2):
                    n = 2 * l + h
                    if n >= 2:
                        pe.wait_ge(s["t_out"], n - 1)
                    for j in range(4):
                        mm = pe.matmul(R.ps[:, h, j * P:(j + 1) * P], W.At[:, h, j, :],
                                       R.eye[:, :] if l == 0 else W.Tm[:, h, j, :], start=True, stop=True)
                    mm.then_inc(s["y_done"], 1)
                if l == 0:
                    continue
                for h in range(2):
                    n = 2 * l + h
                    pe.wait_ge(s["y_out"], n + 1)
                    pe.wait_ge(s["u_out"], n + 1)
                    for j in range(4):
                        if l < LEVELS - 1:
                            pe.matmul(R.ps[:, 2 + h, j * P:(j + 1) * P], W.U[:, z, h, j, :], W.Y[:, h, j, :], start=True, stop=True)
                        mm = pe.matmul(R.ps[:, 4 + h, j * P:(j + 1) * P], W.Y[:, h, j, :], W.U[:, z, h, j, :], start=True, stop=True)
                    mm.then_inc(s["t_done"], 1)

        @block.vector
        def _(dve):
            for l in range(LEVELS):
                for h in range(2):
                    n = 2 * l + h
                    dve.wait_ge(s["y_done"], n + 1)
                    dve.tensor_tensor(W.Y[:, h], bank(h), lm(l, z), ALU.mult).then_inc(s["y_out"], 1)
                    if l == 0:
                        dve.tensor_tensor(W.U[:, z, h], W.At[:, h], lm(0, 1 - z), ALU.mult).then_inc(s["u_out"], 1)
                for h in range(2):
                    n = 2 * l + h
                    if l == 0:
                        dve.wait_ge(s["y_out"], h + 1)
                        dve.tensor_tensor(W.Tm[:, h], W.Y[:, h], eye4, ALU.add).then_inc(s["t_out"], 1)
                        dve.wait_ge(s["u_out"], 2)
                        dve.tensor_tensor(W.U[:, z, h], W.U[:, z, h], eye4, ALU.add).then_inc(s["u_out"], 1)
                    else:
                        dve.wait_ge(s["t_done"], 2 * (l - 1) + h + 1)
                        if l < LEVELS - 1:
                            dve.tensor_tensor(W.Tm[:, h], W.Tm[:, h], bank(2 + h), ALU.add).then_inc(s["t_out"], 1)
                        dve.tensor_tensor(W.U[:, z, h], W.U[:, z, h], bank(4 + h), ALU.add).then_inc(s["u_out"], 1)


ORDER = ([4, 5, 6, 7, 0, 1, 2, 3], [7, 6, 5, 4, 3, 2, 1, 0])


def rwkv_scan(nc, R, W):
    with stage(nc, "x_done", "u_done", "y_done", "h_done", "zeroed", "v_in", "x_out", "u_out", "h_scaled", "h_out", "y_out") as (block, s):
        first = {}
        for n in range(4, NCH):
            for z in range(2):
                first.setdefault(ORDER[z][n], (n, z))

        @block.tensor
        def _(pe):
            ny = 0
            for n in range(NCH):
                for z in range(2):
                    ch = ORDER[z][n]
                    j, p, x = ch // 2, ch % 2, ch < 4
                    a, r = oth(p), nat(p)
                    pe.wait_ge(s["h_out"], 2 * n + z + 1 if n else 2)
                    if n >= 5:
                        pe.wait_ge(s["y_out"], 2 * (n - 5) + z + 1)
                    pe.matmul(R.ps[:, z, 0:P], W.ar[:, z, ch, :], W.H[:, z].rearrange("p h n -> p (h n)"), start=True, stop=True)
                    for h in range(2):
                        g = h * 64
                        mm = pe.matmul(R.ps[a:a + 64, z, g:g + 64], W.A[r:r + 64, z, h, j, p, a:a + 64],
                                       W.vtok[r:r + 64, j, g:g + 64], start=False, stop=True, skip_group_check=True)
                    mm.then_inc(s["x_done"], 1)
                for z in range(2):
                    ch = ORDER[z][n]
                    j, p = ch // 2, ch % 2
                    a = oth(p)
                    pe.wait_ge(s["x_out"], 2 * n + z + 1)
                    for h in range(2):
                        mm = pe.matmul(R.ps[a:a + 64, 4 + z, h * 64:h * 64 + 64], W.U[a:a + 64, z, h, j, a:a + 64],
                                       W.Xs[a:a + 64, z, h, :], start=True, stop=True)
                    mm.then_inc(s["u_done"], 1)
                for z in range(2):
                    ch = ORDER[z][n]
                    j, p, x = ch // 2, ch % 2, ch < 4
                    r = nat(p)
                    pe.wait_ge(s["u_out"], 2 * n + z + 1)
                    pe.wait_ge(s["v_in"], 2 * n + z + 1)
                    for h in range(2):
                        mm = pe.matmul(R.ps[h * 64:h * 64 + 64, 6 + z, 0:64], W.BK[:, z, h, j, p, :], W.Z[:, z, h, :], start=True, stop=True)
                    mm.then_inc(s["h_done"], 1)
                    if x:
                        for h in range(2):
                            mm = pe.matmul(R.ps[r:r + 64, z, h * 64:h * 64 + 64], W.A[:, z, h, j, p, r:r + 64], W.Z[:, z, h, :],
                                           start=False, stop=True, skip_group_check=True)
                    else:
                        mm = pe.nop()
                    mm.then_inc(s["y_done"], 1)

        @block.scalar
        def _(act):
            for n in range(NCH):
                for z in range(2):
                    ch = ORDER[z][n]
                    j, p = ch // 2, ch % 2
                    a = oth(p)
                    act.wait_ge(s["x_done"], 2 * n + z + 1)
                    act.activation(W.Xs[a:a + 64, z].rearrange("p h n -> p (h n)"), R.ps[a:a + 64, z, 0:P], ACT.Copy).then_inc(s["x_out"], 1)
                for z in range(2):
                    ch = ORDER[z][n]
                    j, p = ch // 2, ch % 2
                    a = oth(p)
                    if n:
                        act.wait_ge(s["y_done"], 2 * (n - 1) + z + 1)
                        act.wait_ge(s["h_done"], 2 * (n - 1) + z + 1)
                    act.wait_ge(s["u_done"], 2 * n + z + 1)
                    act.activation(W.Z[a:a + 64, z].rearrange("p h n -> p (h n)"), R.ps[a:a + 64, 4 + z, 0:128], ACT.Copy).then_inc(s["u_out"], 1)

        @block.gpsimd
        def _(pool):
            for n in range(NCH):
                for z in range(2):
                    ch = ORDER[z][n]
                    j, r = ch // 2, nat(ch % 2)
                    if n:
                        pool.wait_ge(s["y_done"], 2 * (n - 1) + z + 1)
                        pool.wait_ge(s["h_done"], 2 * (n - 1) + z + 1)
                    pool.tensor_copy(W.Z[r:r + 64, z].rearrange("p h n -> p (h n)"), W.vtok[r:r + 64, j, :]).then_inc(s["v_in"], 1)

        @block.vector
        def _(dve):
            for z in range(2):
                dve.memset(W.H[:, z], 0.0).then_inc(s["h_out"], 1)
            dve.wait_ge(s["h_out"], 2)
            for n in range(NCH):
                for z in range(2):
                    ch = ORDER[z][n]
                    dve.wait_ge(s["h_out"], 2 * n + z + 1)
                    dve.tensor_scalar(W.HP[:, z], W.H[:, z], W.pc[:, z, ch:ch + 1], None, ALU.mult).then_inc(s["h_scaled"], 1)
                for z in range(2):
                    ch = ORDER[z][n]
                    j, p = ch // 2, ch % 2
                    r = nat(p)
                    dve.wait_ge(s["h_done"], 2 * n + z + 1)
                    dve.wait_ge(s["h_scaled"], 2 * n + z + 1)
                    for h in range(2):
                        g = slice(h * 64, h * 64 + 64)
                        up = dve.scalar_tensor_tensor(W.H[g, z, h], R.ps[g, 6 + z, 0:64], W.pc[g, z, ch:ch + 1], W.HP[g, z, h],
                                                      ALU.mult, ALU.add)
                    up.then_inc(s["h_out"], 1)
                for z in range(2):
                    ch = ORDER[z][n]
                    j, p = ch // 2, ch % 2
                    r = nat(p)
                    if ch < 4:
                        dve.wait_ge(s["y_done"], 2 * n + z + 1)
                        y = W.ytok[r:r + 64, j]
                        src = R.ps[r:r + 64, z, 0:P]
                        if first[ch] == (n, z):
                            dve.tensor_copy(y, src).then_inc(s["y_out"], 1)
                        else:
                            n0, z0 = first[ch]
                            dve.wait_ge(s["y_out"], 2 * (n0 - 4) + z0 + 1)
                            dve.tensor_tensor(y, y, src, ALU.add).then_inc(s["y_out"], 1)


def rwkv_readout(nc, R, W, pair):
    with stage(nc, "chain", "rk", "coef", "coef_out", "var", "root", "normed", "turned", "bonus_in", "out") as (block, s):
        y4 = W.ytok.rearrange("p j (h n) -> p (j h) n", n=64)
        yc = W.yc.rearrange("p (g n) -> p g n", n=64)
        sq = W.t1[:, 0:NX].rearrange("p (g n) -> p g n", n=64)
        st = lambda n: W.st[:, n, :]
        wide = lambda ap: ap.unsqueeze(2).broadcast_to([P, 4, 64])

        @block.tensor
        def _(pe):
            pe.wait_ge(s["rk"], 1)
            for j in range(2):
                mm = pe.matmul(R.ps[:, 0, 2 * j:2 * j + 2], W.tmp[:, j * P:(j + 1) * P], R.head_ones[:, 63:65], start=True, stop=True)
            mm.then_inc(s["coef"], 1)
            pe.wait_ge(s["bonus_in"], 1)
            for j in range(2):
                mm = pe.transpose(R.ps[:, 2, j * P:(j + 1) * P], W.bonus[:, j, :], R.eye[:, :])
            mm.then_inc(s["turned"], 1)
            pe.wait_ge(s["normed"], 1)
            for j in range(2):
                mm = pe.transpose(R.ps[:, 1, j * P:(j + 1) * P], yc[:, 2 * j:2 * j + 2, :].rearrange("p g n -> p (g n)"), R.eye[:, :])
            mm.then_inc(s["turned"], 1)

        @block.scalar
        def _(act):
            act.wait_ge(s["var"], 1)
            act.activation(st(1), st(1), ACT.Sqrt).then_inc(s["root"], 1)

        @block.vector
        def _(dve):
            step = Steps(dve, s["chain"])
            dve.scalar_tensor_tensor(W.tmp[:, 0:NX], W.ksum[:, 0:NX], W.pv[:, V_RK:V_RK + 1], W.r, ALU.mult, ALU.mult).then_inc(s["rk"], 1)
            step(dve.tensor_reduce(st(0), y4, AX_X, ALU.add))
            step.wait()
            step(dve.tensor_scalar(st(0), st(0), 1.0 / HEAD, None, ALU.mult))
            step.wait()
            step(dve.tensor_tensor(yc, y4, wide(st(0)), ALU.subtract))
            step.wait()
            step(dve.tensor_tensor(sq, yc, yc, ALU.mult))
            step.wait()
            step(dve.tensor_reduce(st(1), sq, AX_X, ALU.add))
            step.wait()
            dve.tensor_scalar(st(1), st(1), 1.0 / HEAD, GN_EPS, ALU.mult, ALU.add).then_inc(s["var"], 1)
            dve.wait_ge(s["coef"], 1)
            step(dve.tensor_copy(W.coef[:, :], R.ps[:, 0, 0:4]))
            step.wait()
            bonus = W.bonus.rearrange("p j (h n) -> p (j h) n", n=64)
            v4 = W.vtok[:, 0:2].rearrange("p j (h n) -> p (j h) n", n=64)
            dve.tensor_tensor(bonus, v4, wide(W.coef[:, :]), ALU.mult).then_inc(s["bonus_in"], 1)
            dve.wait_ge(s["root"], 1)
            step(dve.reciprocal(st(2), st(1)))
            step.wait()
            dve.tensor_tensor(yc, yc, wide(st(2)), ALU.mult).then_inc(s["normed"], 1)
            dve.wait_ge(s["turned"], 2)
            step(dve.tensor_scalar(W.t2[:, 0:NX], R.ps[:, 1, 0:NX], W.pv[:, V_LNW:V_LNW + 1], W.pv[:, V_LNB:V_LNB + 1], ALU.mult, ALU.add))
            step.wait()
            step(dve.tensor_tensor(W.t2[:, 0:NX], W.t2[:, 0:NX], R.ps[:, 2, 0:NX], ALU.add))
            step.wait()
            dve.tensor_tensor(W.u_pairs[:, ds(pair, 1), :].rearrange("p a n -> p (a n)"), W.t2[:, 0:NX], W.gate, ALU.mult).then_inc(s["out"], 1)



def hyena_layer(nc, R, I):
    with ExitStack() as c:
        def sb(name, *shape):
            return c.enter_context(nc.sbuf_tensor(name, [P, *shape], F32))

        W = Named()
        W.Kf = sb("filter_spectrum", 4, E)
        W.dft = sb("dft", 2, 4 * P)
        W.idft = sb("idft", 4, NX)
        W.hv = sb("hyena_vec", 5, 3 * KE)
        hyena_filters(nc, R, W, I)
        modulate(nc, R, R.mods[:, 1], R.vec[:, 4, KD:2 * KD], NX)
        W.proj = sb("hyena_proj", 4 * KE, NX)
        hyena_project(nc, R, W, I)
        hyena_convolve(nc, R, W)
        dense(nc, R, I["w_out1"], KD, KE, NX, lambda k: W.proj[:, k, :], lambda m: R.h[:, ds(m, 1), 0:NX].rearrange("p a n -> p (a n)"))
    add_back(nc, R, R.h, R.mods[:, 1], R.vec[:, 5, KD:2 * KD], NX)


def hyena_filters(nc, R, W, I):
    with ExitStack() as c:
        def sb(name, *shape):
            return c.enter_context(nc.sbuf_tensor(name, [P, *shape], F32))

        f1, f23, fb = sb("f_w1", 64), sb("f_w23", 2, 64), sb("f_vec", 4)
        zt, hid, arg, rnd = sb("z_t", NX), sb("hid", NX), sb("arg", NX), sb("rnd", NX)
        w4 = sb("f_w4", 2, E)
        sd = sb("sum_diff", 2, 2, E)
        win = sb("window", 2, E)
        with stage(nc, "loaded", "summed", "layer", "chain", "sine", "filt", "filt_out") as (block, s):
            loads = [(f1[0:33, :], I["f_w1"]), (f23[0:64, :, :], I["f_w23"]), (fb[0:64, :], I["f_vec"]), (zt[0:33, :], I["z_t"]),
                     (w4[0:64, :, :], I["f_w4"]), (win[:, :, :], I["window"]), (W.dft[:, :, :], I["dft"]),
                     (W.idft[:, :, :], I["idft"]), (W.hv[:, :, :], I["hyena_vec"])]

            @block.sync
            def _(sp):
                for dst, src in loads:
                    sp.dma_start(dst, src).then_inc(s["loaded"], 16)

            @block.tensor
            def _(pe):
                pe.wait_ge(s["loaded"], 16 * len(loads))
                for n in range(3):
                    if n:
                        pe.wait_ge(s["sine"], n)
                    w, x = (f1[0:33, :], zt[0:33, :]) if n == 0 else (f23[0:64, n - 1, :], hid[0:64, :])
                    pe.matmul(R.ps[0:64, 0, 0:NX], w, x, start=True, stop=True).then_inc(s["layer"], 1)
                pe.wait_ge(s["sine"], 3)
                pe.wait_ge(s["summed"], 3)
                for n in range(16):
                    t, q, ch = n // 8, n // 4 % 2, n % 4
                    if n >= 7:
                        pe.wait_ge(s["filt_out"], n - 6)
                    pe.matmul(R.ps[:, 1 + n % 7, :], hid[0:64, t * P:(t + 1) * P], w4[0:64, q, ch * 512:(ch + 1) * 512],
                              start=True, stop=True).then_inc(s["filt"], 1)

            @block.scalar
            def _(act):
                for n in range(3):
                    act.wait_ge(s["chain"], 6 * n + 6)
                    act.activation(hid[0:64, :], arg[0:64, :], ACT.Sin).then_inc(s["sine"], 1)

            @block.vector
            def _(dve):
                dve.wait_ge(s["loaded"], 16 * len(loads))
                step = Steps(dve, s["chain"])
                for n in range(3):
                    dve.wait_ge(s["layer"], n + 1)
                    a, r = arg[0:64, :], rnd[0:64, :]
                    step(dve.tensor_scalar(a, R.ps[0:64, 0, 0:NX], fb[0:64, n:n + 1], fb[0:64, 3:4], ALU.add, ALU.mult))
                    step.wait()
                    step(dve.tensor_scalar(r, a, 1 / (2 * math.pi), BIG, ALU.mult, ALU.add))
                    step.wait()
                    step(dve.tensor_scalar(r, r, -BIG, None, ALU.add))
                    step.wait()
                    step(dve.scalar_tensor_tensor(a, r, -6.28125, a, ALU.mult, ALU.add))
                    step.wait()
                    step(dve.scalar_tensor_tensor(a, r, -(2 * math.pi - 6.28125), a, ALU.mult, ALU.add))
                    step.wait()
                    step(dve.tensor_scalar(a, a, 3.1415925, -3.1415925, ALU.min, ALU.max))
                    if n == 0:
                        tmp = sd[0:64, 0, 0, :]
                        dve.tensor_tensor(tmp, w4[0:64, 0, :], w4[0:64, 1, :], ALU.subtract).then_inc(s["summed"], 1)
                        dve.wait_ge(s["summed"], 1)
                        dve.tensor_tensor(w4[0:64, 0, :], w4[0:64, 0, :], w4[0:64, 1, :], ALU.add).then_inc(s["summed"], 1)
                        dve.wait_ge(s["summed"], 2)
                        dve.tensor_copy(w4[0:64, 1, :], tmp).then_inc(s["summed"], 1)
                        dve.wait_ge(s["summed"], 3)
                for n in range(16):
                    t, q, ch = n // 8, n // 4 % 2, n % 4
                    cols = slice(ch * 512, (ch + 1) * 512)
                    dve.wait_ge(s["filt"], n + 1)
                    dve.tensor_tensor(sd[:, q, t, cols], R.ps[:, 1 + n % 7, :], win[:, t, cols], ALU.mult).then_inc(s["filt_out"], 1)

        with stage(nc, "done", "copied") as (block, s):
            @block.tensor
            def _(pe):
                for n in range(16):
                    f, ch = n // 4, n % 4
                    if n >= 8:
                        pe.wait_ge(s["copied"], n - 7)
                    for t in range(2):
                        mm = pe.matmul(R.ps[:, n % 8, :], W.dft[:, t, f * P:(f + 1) * P], sd[:, f // 2, t, ch * 512:(ch + 1) * 512],
                                       start=(t == 0), stop=(t == 1))
                    mm.then_inc(s["done"], 1)

            @block.vector
            def _(dve):
                for n in range(16):
                    f, ch = n // 4, n % 4
                    dve.wait_ge(s["done"], n + 1)
                    dve.tensor_copy(W.Kf[:, f, ch * 512:(ch + 1) * 512], R.ps[:, n % 8, :]).then_inc(s["copied"], 1)


def hyena_project(nc, R, W, I):
    conv = 3 * KE

    def evac(dve, s, n, m, bank):
        out = W.proj[:, ds(m, 1), :].rearrange("p a n -> p (a n)")
        vec = lambda q: W.hv[:, q, ds(m, 1)]
        dve.tensor_scalar(out, R.ps[:, bank, 0:NX], vec(1), vec(3), ALU.mult, ALU.add).then_inc(s["part"], 1)
        dve.wait_ge(s["part"], n * 2 + 1)
        dve.scalar_tensor_tensor(out[:, 1:], R.ps[:, bank, 0:NX - 1], vec(0), out[:, 1:], ALU.mult, ALU.add).then_inc(s["part"], 1)
        dve.wait_ge(s["part"], n * 2 + 2)
        return dve.scalar_tensor_tensor(out[:, :-1], R.ps[:, bank, 1:NX], vec(2), out[:, :-1], ALU.mult, ALU.add)

    dense(nc, R, I["w_in1"], conv, KD, NX, lambda k: R.h[:, k, 0:NX], None, evac)
    dense(nc, R, I["w_gate1"], KE, KD, NX, lambda k: R.h[:, k, 0:NX], lambda m: W.proj[:, ds(m + conv, 1), :].rearrange("p a n -> p (a n)"))


def hyena_convolve(nc, R, W):
    x0, u, v, gate = (W.proj[:, q * KE:(q + 1) * KE, :] for q in range(4))
    utok = R.sq[:, :, :].rearrange("p a b -> p (a b)").rearrange("p (t n) -> p t n", n=E)
    with stage(nc, "u", "gate", "turned", "utok", "spec", "spec_out", "chain", "mult", "conv", "out") as (block, s):
        @block.scalar
        def _(act):
            for q in range(4):
                act.activation(gate[:, 4 * q:4 * q + 4, :], gate[:, 4 * q:4 * q + 4, :], ACT.Silu).then_inc(s["gate"], 1)
            for n in range(8):
                t, q = n % 2, n // 2
                act.wait_ge(s["turned"], n + 1)
                act.activation(utok[:, t, q * 512:(q + 1) * 512], R.ps[:, n % 2, :], ACT.Copy).then_inc(s["utok"], 1)
            for q in range(4):
                for f in range(4):
                    act.wait_ge(s["spec"], 4 * q + f + 1)
                    if q >= 2:
                        act.wait_ge(s["mult"], q - 1)
                    act.activation(R.h[:, 4 * (q % 2) + f, :], R.ps[:, 2 + f, :], ACT.Copy).then_inc(s["spec_out"], 1)

        @block.tensor
        def _(pe):
            for n in range(8):
                t, q = n % 2, n // 2
                pe.wait_ge(s["u"], q + 1)
                if n >= 2:
                    pe.wait_ge(s["utok"], n - 1)
                for b in range(4):
                    mm = pe.transpose(R.ps[:, n % 2, b * P:(b + 1) * P], u[:, 4 * q + b, t * P:(t + 1) * P], R.eye[:, :])
                mm.then_inc(s["turned"], 1)
            for q in range(4):
                pe.wait_ge(s["utok"], 2 * q + 2)
                for f in range(4):
                    if q:
                        pe.wait_ge(s["spec_out"], 4 * (q - 1) + f + 1)
                    for t in range(2):
                        mm = pe.matmul(R.ps[:, 2 + f, :], W.dft[:, t, f * P:(f + 1) * P], utok[:, t, q * 512:(q + 1) * 512],
                                       start=(t == 0), stop=(t == 1))
                    mm.then_inc(s["spec"], 1)
            for m in range(KE):
                pe.wait_ge(s["mult"], m // 4 + 1)
                if m >= 2:
                    pe.wait_ge(s["out"], 3 * (m - 2) + 1)
                for f in range(4):
                    mm = pe.matmul(R.ps[:, 6 + m % 2, 0:NX], W.Kf[:, f, m * P:(m + 1) * P], W.idft[:, f, :],
                                   start=(f == 0), stop=(f == 3))
                mm.then_inc(s["conv"], 1)

        @block.vector
        def _(dve):
            step = Steps(dve, s["chain"])
            for q in range(4):
                a = slice(4 * q, 4 * q + 4)
                dve.tensor_tensor(u[:, a, :], v[:, a, :], u[:, a, :], ALU.mult).then_inc(s["u"], 1)
            dve.wait_ge(s["u"], 4)
            ta = v[:, 0:4, :].rearrange("p (a b) n -> p a (b n)", a=2)
            tb = v[:, 4:8, :].rearrange("p (a b) n -> p a (b n)", a=2)
            for q in range(4):
                dve.wait_ge(s["spec_out"], 4 * q + 4)
                cols = slice(q * 512, (q + 1) * 512)
                b = 4 * (q % 2)
                ure, uim = R.h[:, b:b + 2, :], R.h[:, b + 2:b + 4, :]
                kre, kim = W.Kf[:, 0:2, cols], W.Kf[:, 2:4, cols]
                step(dve.tensor_tensor(ta, uim, kim, ALU.mult))
                step(dve.tensor_tensor(tb, ure, kim, ALU.mult))
                step.wait()
                step(dve.tensor_tensor(kim, uim, kre, ALU.mult))
                step.wait()
                step(dve.tensor_tensor(kre, ure, kre, ALU.mult))
                step.wait()
                step(dve.tensor_tensor(kre, kre, ta, ALU.subtract))
                step(dve.tensor_tensor(kim, kim, tb, ALU.add))
                step.wait()
                dve.sem_inc(s["mult"], 1)
            dve.wait_ge(s["gate"], 4)
            for m in range(KE):
                dve.wait_ge(s["conv"], m + 1)
                n = 3 * m
                dve.scalar_tensor_tensor(u[:, m, :], u[:, m, :], W.hv[:, 4, m:m + 1], R.ps[:, 6 + m % 2, 0:NX], ALU.mult, ALU.add).then_inc(s["out"], 1)
                dve.wait_ge(s["out"], n + 1)
                dve.tensor_tensor(x0[:, m, :], x0[:, m, :], u[:, m, :], ALU.mult).then_inc(s["out"], 1)
                dve.wait_ge(s["out"], n + 2)
                dve.tensor_tensor(x0[:, m, :], x0[:, m, :], gate[:, m, :], ALU.mult).then_inc(s["out"], 1)



RK, DK, RQ, DQ, RG, DG, MU, MG = range(8)


def second_layer(nc, R, I, l):
    last = l == 1
    NQ = NX if last else NT
    w_feature, w_token, w_merge, w_last = ((I["w_feature0"], I["w_token0"], I["w_merge0"], I["w_last0"]),
                                           (I["w_feature1"], I["w_token1"], I["w_merge1"], I["w_last1"]))[l]
    modulate(nc, R, R.mods[:, 2 + l], R.vec[:, 6, l * 8:l * 8 + 8], NT)
    with ExitStack() as c:
        def sb(name, *shape):
            return c.enter_context(nc.sbuf_tensor(f"{name}_{l}", [P, *shape], F32))

        W = Named()
        W.F, W.D, W.sc = sb("features", 32, NT), sb("decays", HEADS, 4, NX), sb("scalars", 64)
        W.rv, W.dv, W.mv = sb("ret_v", 4, BW), sb("diff_v", 4, BW), sb("mlp_v", 4, BW)
        dense(nc, R, w_feature[0:8], 8, KD, NT, lambda k: R.h[:, k, :], lambda m: W.F[:, ds(m, 1), :].rearrange("p a n -> p (a n)"))
        dense(nc, R, w_feature[8:32], 24, KD, NQ, lambda k: R.h[:, k, 0:NQ], lambda m: W.F[:, ds(m + 8, 1), 0:NQ].rearrange("p a n -> p (a n)"))
        rhs = lambda k, t: R.h[:, k, t * P:(t + 1) * P]
        token_major(nc, R, w_token[0], rhs, 4, lambda t: W.rv[:, t, :])
        token_major(nc, R, w_token[1], rhs, 4, lambda t: W.dv[:, t, :])
        token_major(nc, R, w_token[2], rhs, NQ // P, lambda t: W.mv[:, t, :])
        decays(nc, R, W, I, l)
        rotate(nc, R, W, I)
        retention(nc, R, W, NQ)
        diff_attention(nc, R, W, NQ)
        lam_init = 0.8 - 0.6 * math.exp(-0.3 * l)
        head_norms(nc, R, W, RQ, RG, NQ, 1.0)
        head_norms(nc, R, W, DQ, DG, NQ, 1.0 - lam_init)
        mlp(nc, R, W, I, l, NQ)
        merge(nc, R, W, w_merge, NQ)
        dense(nc, R, w_last, KD, KD, NQ, lambda k: R.sq[:, k, 0:NQ], lambda m: R.h[:, ds(m, 1), 0:NQ].rearrange("p a n -> p (a n)"))
    add_back(nc, R, R.h, R.mods[:, 2 + l], R.vec[:, 7, l * 8:l * 8 + 8], NQ)


def decays(nc, R, W, I, l):
    lam_init = 0.8 - 0.6 * math.exp(-0.3 * l)
    sc = W.sc
    logit, lg, ax, y, sd, s1, s2, poly = (sc[:, 8 * n:8 * n + 8] for n in range(8))
    W.lam = sc[:, 56:57]
    lamk = R.ring[:, 0, 0:256].rearrange("p (a b n) -> p a b n", a=2, b=2)
    prod = R.ring[:, 1, 0:128].rearrange("p (b n) -> p b n", b=2)
    lsum = R.ring[:, 2, 0:2]
    dist = R.ring[:, 4:6, :].rearrange("p a (b n) -> p (a b) n", n=2 * NX)
    same = R.ring[:, 6, 0:2 * NX]
    with stage(nc, "loaded", "chain", "act") as (block, s):
        loads = [(logit, I["ret_logit"][l]), (lamk, I["lambdas"][l]), (dist, I["distances"]), (same, I["same"])]

        @block.sync
        def _(sp):
            for dst, src in loads:
                sp.dma_start(dst, src).then_inc(s["loaded"], 16)

        @block.vector
        def _(dve):
            dve.wait_ge(s["loaded"], 16 * len(loads))
            step = Steps(dve, s["chain"])

            def seq(ins):
                step(ins)
                step.wait()

            seq(dve.tensor_scalar(ax, logit, -1.0, None, ALU.mult))
            seq(dve.tensor_tensor(ax, ax, logit, ALU.max))
            seq(dve.tensor_tensor(prod, lamk[:, 0], lamk[:, 1], ALU.mult))
            seq(dve.tensor_reduce(lsum, prod, AX_X, ALU.add))
            dve.wait_ge(s["act"], 2)
            seq(dve.tensor_scalar(sd, y, 2.0, None, ALU.add))
            seq(dve.reciprocal(sd, sd))
            seq(dve.tensor_tensor(s1, y, sd, ALU.mult))
            seq(dve.tensor_tensor(s2, s1, s1, ALU.mult))
            seq(dve.tensor_scalar(poly, s2, 1 / 19, 1 / 17, ALU.mult, ALU.add))
            for q in (15, 13, 11, 9, 7, 5, 3, 1):
                seq(dve.tensor_tensor(poly, poly, s2, ALU.mult))
                seq(dve.tensor_scalar(poly, poly, 1 / q, None, ALU.add))
            seq(dve.tensor_tensor(poly, poly, s1, ALU.mult))
            seq(dve.tensor_scalar(lg, logit, 0.0, None, ALU.min))
            seq(dve.scalar_tensor_tensor(lg, poly, -2.0, lg, ALU.mult, ALU.add))
            seq(dve.tensor_tensor(W.lam, lsum[:, 0:1], lsum[:, 1:2], ALU.subtract))
            seq(dve.tensor_scalar(W.lam, W.lam, lam_init, None, ALU.add))
            for h in range(HEADS):
                d = W.D[:, h, 0:2, :].rearrange("p a n -> p (a n)")
                seq(dve.tensor_scalar(d, dist[:, 0, :], lg[:, h:h + 1], None, ALU.mult))
                seq(dve.scalar_tensor_tensor(d, dist[:, 1, :], lg[:, 4 + h:5 + h], d, ALU.mult, ALU.add))
            dve.sem_inc(s["chain"], 1)
            step.n += 1
            self_n = step.n
            for h in range(HEADS):
                dve.wait_ge(s["act"], 3 + h)
                d = W.D[:, h, 0:2, :].rearrange("p a n -> p (a n)")
                step(dve.tensor_tensor(d, d, same, ALU.add))
            for h in range(HEADS):
                dve.wait_ge(s["act"], 2 + HEADS + 2 * h + 2)
                d = W.D[:, h, 2:4, :].rearrange("p a n -> p (a n)")
                other = R.sq[:, h, :]
                step(dve.tensor_tensor(d, d, other, ALU.add))

        ready = 4 + 4 + 1 + 16 + 3 + 2 + 2 * HEADS + 1

        @block.scalar
        def _(act):
            act.wait_ge(s["chain"], 4)
            act.activation(y, ax, ACT.Exp, scale=-1.0).then_inc(s["act"], 1)
            act.activation(lsum, lsum, ACT.Exp).then_inc(s["act"], 1)
            act.wait_ge(s["chain"], ready)
            for h in range(HEADS):
                d = W.D[:, h, 0:2, :].rearrange("p a n -> p (a n)")
                act.activation(d, d, ACT.Exp).then_inc(s["act"], 1)
            for h in range(HEADS):
                d = W.D[:, h, 2:4, :].rearrange("p a n -> p (a n)")
                act.activation(d, dist[:, 2, :], ACT.Exp, scale=lg[:, h:h + 1]).then_inc(s["act"], 1)
                act.activation(R.sq[:, h, :], dist[:, 3, :], ACT.Exp, scale=lg[:, 4 + h:5 + h]).then_inc(s["act"], 1)


def rotate(nc, R, W, I):
    tab = R.ring[:, 0, :].rearrange("p (q n) -> p q n", n=NX)
    swap = R.ring[:, 1, 0:2 * P].rearrange("p (q n) -> p q n", n=P)
    with stage(nc, "loaded", "swapped", "term", "scaled", "out") as (block, s):
        @block.sync
        def _(sp):
            sp.dma_start(tab, I["rope"]).then_inc(s["loaded"], 16)
            sp.dma_start(swap, I["swaps"]).then_inc(s["loaded"], 16)

        order = [(g, h) for h in range(4) for g in (RK, RQ, DK, DQ)]

        @block.tensor
        def _(pe):
            pe.wait_ge(s["loaded"], 32)
            for n, (g, h) in enumerate(order):
                if n >= 4:
                    pe.wait_ge(s["term"], n - 3)
                pe.matmul(R.ps[:, n % 4, 0:NX], swap[:, int(g in (DK, DQ)), :], W.F[:, 4 * g + h, 0:NX], start=True, stop=True).then_inc(s["swapped"], 1)

        @block.vector
        def _(dve):
            dve.wait_ge(s["loaded"], 32)
            for n, (g, h) in enumerate(order):
                q = 2 * int(g in (DK, DQ))
                x, t = W.F[:, 4 * g + h, 0:NX], R.sq[:, n % 4, 0:NX]
                dve.wait_ge(s["swapped"], n + 1)
                if n >= 4:
                    dve.wait_ge(s["out"], n - 3)
                dve.tensor_tensor(t, R.ps[:, n % 4, 0:NX], tab[:, q + 1, :], ALU.mult).then_inc(s["term"], 1)
                dve.tensor_tensor(x, x, tab[:, q, :], ALU.mult).then_inc(s["scaled"], 1)
                dve.wait_ge(s["term"], n + 1)
                dve.wait_ge(s["scaled"], n + 1)
                dve.tensor_tensor(x, x, t, ALU.add).then_inc(s["out"], 1)


def retention(nc, R, W, NQ):
    jobs = [(h, side) for h in range(HEADS) for side in range(NQ // NX)]
    with stage(nc, "scores", "decayed", "out", "out_copied") as (block, s):
        score = R.ring[:, 0:2, :].rearrange("p a (b n) -> p (a b) n", n=NX)

        def keys(side):
            return [(0, 0), (1, 1), (2, 2), (3, 3)] if side == 0 else [(2, 0), (3, 1)]

        first = [0]
        for _, side in jobs:
            first.append(first[-1] + len(keys(side)))

        @block.tensor
        def _(pe):
            for n, (h, side) in enumerate(jobs):
                q = W.F[:, 4 * RQ + h, side * NX:(side + 1) * NX]
                for i, (kt, _) in enumerate(keys(side)):
                    if n:
                        pe.wait_ge(s["decayed"], first[n])
                    pe.matmul(R.ps[:, i, 0:NX], W.F[:, 4 * RK + h, kt * P:(kt + 1) * P], q, start=True, stop=True).then_inc(s["scores"], 1)
                if n >= 2:
                    pe.wait_ge(s["out_copied"], n - 1)
                for i, (kt, _) in enumerate(keys(side)):
                    pe.wait_ge(s["decayed"], first[n] + i + 1)
                    mm = pe.matmul(R.ps[:, 4 + n % 2, 0:NX], W.rv[:, kt, h * P:(h + 1) * P], score[:, 4 * (n % 2) + i, :],
                                   start=(i == 0), stop=(i == len(keys(side)) - 1))
                mm.then_inc(s["out"], 1)

        @block.vector
        def _(dve):
            for n, (h, side) in enumerate(jobs):
                for i, (_, dt) in enumerate(keys(side)):
                    dve.wait_ge(s["scores"], first[n] + i + 1)
                    if n >= 2:
                        dve.wait_ge(s["out"], n - 1)
                    dve.scalar_tensor_tensor(score[:, 4 * (n % 2) + i, :], R.ps[:, i, 0:NX], float(P) ** -0.5,
                                             W.D[:, h, dt, :], ALU.mult, ALU.mult).then_inc(s["decayed"], 1)

        @block.scalar
        def _(act):
            for n, (h, side) in enumerate(jobs):
                act.wait_ge(s["out"], n + 1)
                act.activation(W.F[:, 4 * RQ + h, side * NX:(side + 1) * NX], R.ps[:, 4 + n % 2, 0:NX], ACT.Copy).then_inc(s["out_copied"], 1)


def diff_attention(nc, R, W, NQ):
    jobs = [(h, t) for h in range(HEADS) for t in range(NQ // P)]
    prob = R.ring[:, 0:4, :].rearrange("p (b a) (c n) -> p b (a c) n", b=2, n=512)
    st = R.rstd
    with stage(nc, "scores", "top", "expd", "chain", "mixed", "turned", "turned_out", "out", "out_copied") as (block, s):
        def span(t):
            return (0, 4) if t < 2 else (2, 4)

        @block.tensor
        def _(pe):
            def scores(n):
                h, t = jobs[n]
                a, b = span(t)
                for m in range(2):
                    r = slice(64 * m, 64 * m + 64)
                    if n >= 2:
                        pe.wait_ge(s["expd"], 2 * (n - 2) + m + 1)
                    pe.matmul(R.ps[:, 2 * (n % 2) + m, 0:(b - a) * P], W.F[r, 4 * DQ + h, t * P:(t + 1) * P],
                              W.F[r, 4 * DK + h, a * P:b * P], start=True, stop=True).then_inc(s["scores"], 1)

            def values(n):
                h, t = jobs[n]
                a, b = span(t)
                pe.wait_ge(s["mixed"], n + 1)
                if n >= 1:
                    pe.wait_ge(s["turned_out"], n)
                for i in range(b - a):
                    mm = pe.transpose(R.ps[:, 4, i * P:(i + 1) * P], prob[:, n % 2, 2, i * P:(i + 1) * P], R.eye[:, :])
                mm.then_inc(s["turned"], 1)
                pe.wait_ge(s["turned_out"], n + 1)
                if n >= 2:
                    pe.wait_ge(s["out_copied"], n - 1)
                for i in range(b - a):
                    mm = pe.matmul(R.ps[:, 5 + n % 2, 0:P], W.dv[:, a + i, h * P:(h + 1) * P], prob[:, n % 2, 3, i * P:(i + 1) * P],
                                   start=(i == 0), stop=(i == b - a - 1))
                mm.then_inc(s["out"], 1)

            scores(0)
            for n in range(len(jobs)):
                if n + 1 < len(jobs):
                    scores(n + 1)
                values(n)

        @block.scalar
        def _(act):
            def exps(n):
                h, t = jobs[n]
                a, b = span(t)
                for m in range(2):
                    act.wait_ge(s["top"], 2 * n + m + 1)
                    if n >= 2:
                        act.wait_ge(s["mixed"], n - 1)
                    c = 16 * (n % 2) + m
                    act.activation(prob[:, n % 2, m, 0:(b - a) * P], R.ps[:, 2 * (n % 2) + m, 0:(b - a) * P], ACT.Exp,
                                   bias=st[:, c:c + 1], scale=0.125, accum_out=st[:, c + 2:c + 3]).then_inc(s["expd"], 1)

            exps(0)
            for n, (h, t) in enumerate(jobs):
                if n + 1 < len(jobs):
                    exps(n + 1)
                a, b = span(t)
                act.wait_ge(s["turned"], n + 1)
                if n >= 2:
                    act.wait_ge(s["out"], n - 1)
                act.activation(prob[:, n % 2, 3, 0:(b - a) * P], R.ps[:, 4, 0:(b - a) * P], ACT.Copy).then_inc(s["turned_out"], 1)
                act.wait_ge(s["out"], n + 1)
                act.activation(W.F[:, 4 * DQ + h, t * P:(t + 1) * P], R.ps[:, 5 + n % 2, 0:P], ACT.Copy).then_inc(s["out_copied"], 1)

        @block.vector
        def _(dve):
            step = Steps(dve, s["chain"])

            def tops(n):
                h, t = jobs[n]
                a, b = span(t)
                for m in range(2):
                    c = 16 * (n % 2) + m
                    dve.wait_ge(s["scores"], 2 * n + m + 1)
                    step(dve.tensor_reduce(st[:, c:c + 1], R.ps[:, 2 * (n % 2) + m, 0:(b - a) * P], AX_X, ALU.max))
                    step.wait()
                    dve.tensor_scalar(st[:, c:c + 1], st[:, c:c + 1], -0.125, None, ALU.mult).then_inc(s["top"], 1)

            tops(0)
            for n, (h, t) in enumerate(jobs):
                a, b = span(t)
                c = 16 * (n % 2)
                if n + 1 < len(jobs):
                    tops(n + 1)
                dve.wait_ge(s["expd"], 2 * n + 2)
                step(dve.reciprocal(st[:, c + 4:c + 6], st[:, c + 2:c + 4]))
                step.wait()
                step(dve.scalar_tensor_tensor(st[:, c + 6:c + 7], st[:, c + 5:c + 6], -1.0, W.lam, ALU.mult, ALU.mult))
                step.wait()
                w = (b - a) * P
                step(dve.tensor_scalar(prob[:, n % 2, 1, 0:w], prob[:, n % 2, 1, 0:w], st[:, c + 6:c + 7], None, ALU.mult))
                step.wait()
                if n >= 2:
                    dve.wait_ge(s["turned"], n - 1)
                dve.scalar_tensor_tensor(prob[:, n % 2, 2, 0:w], prob[:, n % 2, 0, 0:w], st[:, c + 4:c + 5], prob[:, n % 2, 1, 0:w],
                                         ALU.mult, ALU.add).then_inc(s["mixed"], 1)


def head_norms(nc, R, W, O, G, NQ, factor):
    with stage(nc, "squared", "summed", "log", "rstd", "gate", "scaled", "out") as (block, s):
        @block.tensor
        def _(pe):
            for h in range(HEADS):
                pe.wait_ge(s["squared"], h + 1)
                pe.matmul(R.ps[:, h, 0:NQ], R.ones[:, :], R.sq[:, h, 0:NQ], start=True, stop=True).then_inc(s["summed"], 1)

        @block.scalar
        def _(act):
            for h in range(HEADS):
                act.activation(R.sq[:, h, 0:NQ], W.F[:, 4 * O + h, 0:NQ], ACT.Square).then_inc(s["squared"], 1)
            for h in range(HEADS):
                act.activation(W.F[:, 4 * G + h, 0:NQ], W.F[:, 4 * G + h, 0:NQ], ACT.Silu).then_inc(s["gate"], 1)
            for h in range(HEADS):
                act.wait_ge(s["summed"], h + 1)
                act.activation(R.sq[:, h, 0:NQ], R.ps[:, h, 0:NQ], ACT.Ln, bias=R.eps[:, 0:1], scale=1.0 / P).then_inc(s["log"], 1)
            for h in range(HEADS):
                act.wait_ge(s["log"], h + 1)
                act.activation(R.sq[:, h, 0:NQ], R.sq[:, h, 0:NQ], ACT.Exp, scale=-0.5).then_inc(s["rstd"], 1)

        @block.vector
        def _(dve):
            for h in range(HEADS):
                dve.wait_ge(s["rstd"], h + 1)
                o, g = W.F[:, 4 * O + h, 0:NQ], W.F[:, 4 * G + h, 0:NQ]
                dve.tensor_tensor(o, o, R.sq[:, h, 0:NQ], ALU.mult).then_inc(s["scaled"], 1)
                dve.wait_ge(s["scaled"], h + 1)
                dve.wait_ge(s["gate"], h + 1)
                dve.scalar_tensor_tensor(g, o, factor, g, ALU.mult, ALU.mult).then_inc(s["out"], 1)


def mlp(nc, R, W, I, l, NQ):
    wst = R.ring[:, 0, 0:4 * P].rearrange("p (g n) -> p g n", n=P)
    bs = R.ring[:, 1, 0:4 * P].rearrange("p (g n) -> p g n", n=P)
    stats, mv = R.ring[:, 2, 0:24].rearrange("p (t n) -> p t n", n=6), R.ring[:, 3, 0:8].rearrange("p (t n) -> p t n", n=2)
    T = NQ // P
    with stage(nc, "loaded", "chain", "var", "root", "normed", "mixed", "gate", "out") as (block, s):
        @block.sync
        def _(sp):
            sp.dma_start(wst, I["mlp_w"][l]).then_inc(s["loaded"], 16)
            sp.dma_start(bs, I["mlp_b"][l]).then_inc(s["loaded"], 16)

        @block.scalar
        def _(act):
            for g in range(4):
                act.activation(W.F[:, 4 * MG + g, 0:NQ], W.F[:, 4 * MG + g, 0:NQ], ACT.Silu).then_inc(s["gate"], 1)
            act.wait_ge(s["var"], 1)
            act.activation(mv[:, 0:T, 1], mv[:, 0:T, 1], ACT.Sqrt, bias=R.eps[:, 0:1]).then_inc(s["root"], 1)

        @block.tensor
        def _(pe):
            pe.wait_ge(s["loaded"], 32)
            pe.wait_ge(s["normed"], T)
            for g in range(4):
                for t in range(T):
                    mm = pe.matmul(R.ps[:, g, t * P:(t + 1) * P], W.mv[:, t, g * P:(g + 1) * P], wst[:, g, :], start=True, stop=True)
                mm.then_inc(s["mixed"], 1)

        @block.vector
        def _(dve):
            step = Steps(dve, s["chain"])
            for t in range(T):
                step(dve.bn_stats(stats[:, t, :], W.mv[:, t, :]))
            for t in range(T):
                step.wait(t + 1)
                step(dve.bn_aggr(mv[:, t, :], stats[:, t, :]))
            step.wait()
            dve.sem_inc(s["var"], 1)
            dve.wait_ge(s["root"], 1)
            step(dve.reciprocal(mv[:, 0:T, 1], mv[:, 0:T, 1]))
            step.wait()
            for t in range(T):
                dve.tensor_scalar(W.mv[:, t, :], W.mv[:, t, :], mv[:, t, 0:1], mv[:, t, 1:2], ALU.subtract, ALU.mult).then_inc(s["normed"], 1)
            dve.wait_ge(s["loaded"], 32)
            for g in range(4):
                dve.wait_ge(s["mixed"], g + 1)
                u, gate = W.F[:, 4 * MU + g, 0:NQ], W.F[:, 4 * MG + g, 0:NQ]
                x = R.sq[:, g, 0:NQ]
                step(dve.tensor_tensor(x.rearrange("p (t n) -> p t n", n=P), R.ps[:, g, 0:NQ].rearrange("p (t n) -> p t n", n=P),
                                       bs[:, g, :].unsqueeze(1).broadcast_to([P, T, P]), ALU.add))
                step.wait()
                step(dve.tensor_tensor(x, x, u, ALU.mult))
                step.wait()
                dve.wait_ge(s["gate"], g + 1)
                dve.tensor_tensor(gate, x, gate, ALU.mult).then_inc(s["out"], 1)


def merge(nc, R, W, w, NQ):
    names = [f"w_loaded{b}" for b in range(3)]
    with stage(nc, *names, "logit_done", "branch_done", "sig", "mult", "out") as (block, s):
        loaded = [s[n] for n in names]
        wt = R.ring[:, 0:6, :].rearrange("p (b a) n -> p b (a n)", b=3)[:, :, 0:12 * P].rearrange("p b (k n) -> p b k n", n=P)
        sig = R.ring[:, 6:8, :].rearrange("p a (b n) -> p (a b) n", n=512)

        @block.sync
        def _(sp):
            with sp.Fori(0, KD) as m:
                for b in range(3):
                    sp.wait_ge(s["branch_done"], m * 3 + (b + 1))
                    sp.dma_start(wt[:, b].rearrange("p k n -> p (k n)"), w[ds(m, 1), b].rearrange("a p n -> p (a n)")).then_inc(loaded[b], 16)

        @block.tensor
        def _(pe):
            pe.sem_inc(s["branch_done"], 3)
            with pe.Fori(0, KD) as m:
                for b, G in enumerate((RG, MG, DG)):
                    pe.wait_ge(loaded[b], m * 16 + 16)
                    pe.wait_ge(s["sig"], m * 3 + (b + 1))
                    for k in range(KD):
                        mm = pe.matmul(R.ps[:, 2 * b, 0:NQ], wt[:, b, k, :], R.h[:, k, 0:NQ], start=(k == 0), stop=(k == KD - 1))
                    mm.then_inc(s["logit_done"], 1)
                    pe.wait_ge(s["mult"], m * 3 + (b + 1))
                    for k in range(KB):
                        mm = pe.matmul(R.ps[:, 2 * b + 1, 0:NQ], wt[:, b, KD + k, :], W.F[:, 4 * G + k, 0:NQ], start=(k == 0), stop=(k == KB - 1))
                    mm.then_inc(s["branch_done"], 1)

        @block.scalar
        def _(act):
            act.sem_inc(s["sig"], 3)
            with act.Fori(0, KD) as m:
                for b in range(3):
                    act.wait_ge(s["logit_done"], m * 3 + (b + 1))
                    act.wait_ge(s["mult"], m * 3 + (b + 1))
                    act.activation(sig[:, b, 0:NQ], R.ps[:, 2 * b, 0:NQ], ACT.Sigmoid).then_inc(s["sig"], 1)

        @block.vector
        def _(dve):
            dve.sem_inc(s["mult"], 3)
            with dve.Fori(0, KD) as m:
                y = R.sq[:, ds(m, 1), 0:NQ].rearrange("p a n -> p (a n)")
                for b in range(3):
                    dve.wait_ge(s["sig"], m * 3 + (b + 4))
                    dve.wait_ge(s["branch_done"], m * 3 + (b + 4))
                    if b == 0:
                        dve.tensor_tensor(y, R.ps[:, 1, 0:NQ], sig[:, 0, 0:NQ], ALU.mult).then_inc(s["mult"], 1)
                    else:
                        t = sig[:, b, 0:NQ]
                        dve.tensor_tensor(t, R.ps[:, 2 * b + 1, 0:NQ], t, ALU.mult).then_inc(s["out"], 1)
                        dve.wait_ge(s["out"], m * 2 + b)
                        if b == 1:
                            dve.wait_ge(s["mult"], m * 3 + 4)
                        else:
                            dve.wait_ge(s["mult"], m * 3 + 5)
                        dve.tensor_tensor(y, y, t, ALU.add).then_inc(s["mult"], 1)


def program(nc, I, out):
    with ExitStack() as c:
        R = Named()
        alloc(nc, R, lambda name, *shape: c.enter_context(nc.sbuf_tensor(name, [P, *shape], F32)), c)
        setup(nc, R, I)
        modulate(nc, R, R.mods[:, 0], R.vec[:, 4, 0:KD], NT)
        rwkv_layer(nc, R, I)
        hyena_layer(nc, R, I)
        with stage(nc, "loaded") as (block, s):
            @block.sync
            def _(sp):
                sp.dma_start(R.x[:, :, NX:], I["ctx_t"]).then_inc(s["loaded"], 16)
                sp.wait_ge(s["loaded"], 16)
        for l in range(2):
            second_layer(nc, R, I, l)
        with stage(nc, "stored") as (block, s):
            @block.sync
            def _(sp):
                sp.dma_start(out, R.x[:, :, 0:NX]).then_inc(s["stored"], 16)
                sp.wait_ge(s["stored"], 16)



def tiles(w):
    K, N = w.shape
    return np.ascontiguousarray(w.reshape(K // P, P, N // P, P).transpose(2, 1, 0, 3)).reshape(N // P, P, K)


def columns(v):
    return v.reshape(-1, P).T


def layouts(a):
    f = np.float32
    out = {}
    out["x_t"] = np.concatenate([a["x"][0].T, a["ctx"][0].T], 1).reshape(KD, P, NT).transpose(1, 0, 2)
    out["eye"] = np.eye(P, dtype=f)
    half = np.arange(P) // 64
    out["head_ones"] = (half[:, None] == half[None, :]).astype(f)
    out["cond"] = np.stack([a["c"][0], a["c_ctx"], a["c_2"][0], a["c_ctx_2"]], 1).reshape(KD, P, 4).transpose(1, 0, 2)
    vec = np.zeros((P, 9, 24), f)
    for n, b in enumerate((a["ada_b"][0], a["ada_b"][1], a["b_mod_2"][0], a["b_mod_2"][1])):
        vec[:, n, :] = columns(b)
    for l in range(2):
        vec[:, 4, l * 8:l * 8 + 8] = columns(a["norm_pre"][l])
        vec[:, 5, l * 8:l * 8 + 8] = columns(a["norm_post"][l])
        vec[:, 6, l * 8:l * 8 + 8] = columns(a["g_pre_2"][l])
        vec[:, 7, l * 8:l * 8 + 8] = columns(a["g_post_2"][l])
    out["vectors"] = vec
    for n, w in (("ada0", a["ada_w"][0]), ("ada1", a["ada_w"][1]), ("mod0", a["w_mod_2"][0]), ("mod1", a["w_mod_2"][1]),
                 ("w_out0", a["w_out"][0])):
        out[n] = tiles(w)
    out["mu"] = a["l0_mu"].reshape(6, KD, P).transpose(2, 0, 1)
    w = a["l0_w_in"]
    out["w_rkvg"] = np.concatenate([tiles(w[:, g * E:(g + 1) * E]) for g in (1, 2, 0, 3)], 2)
    out["w_low"] = np.concatenate(list(tiles(w[:, 4 * E:])), 1)
    pv = np.zeros((KE, P, 10), f)
    for n, v in enumerate((a["l0_w0"][0], a["l0_w0"][1], a["l0_a0"][0], a["l0_a0"][1], a["l0_k_k"], a["l0_k_a"],
                           a["l0_r_k"].reshape(-1), a["l0_ln_w"], a["l0_ln_b"])):
        pv[:, :, n] = v.reshape(KE, P)
    out["pair_vec"] = pv
    out["lora"] = np.stack([a["l0_w2"].reshape(P, KE, P), a["l0_a2"].reshape(P, KE, P)], 1).transpose(2, 0, 1, 3)
    t = np.arange(64)
    strict = [t[:, None] < t[None, :], t[:, None] > t[None, :]]
    incl = [t[:, None] <= t[None, :], t[:, None] >= t[None, :]]
    masks = np.zeros((P, 2, 2, P), f)
    for z in range(2):
        for p in range(2):
            for rows in (0, 64):
                masks[rows:rows + 64, z, p, oth(p):oth(p) + 64] = strict[z]
                masks[rows:rows + 64, z, p, nat(p):nat(p) + 64] = incl[z]
    out["masks"] = masks
    lm = np.zeros((P, LEVELS, 2, P), f)
    q = np.arange(P)
    for l in range(LEVELS):
        b = q >> l
        low = (b[:, None] == b[None, :] + 1) & (b[:, None] % 2 == 1)
        lm[:, l, 0, :] = low
        lm[:, l, 1, :] = low.T
    out["level_masks"] = lm
    out["ctx_t"] = a["ctx_2"][0].T.reshape(KD, P, NX).transpose(1, 0, 2)
    w = a["l1_w_in"]
    out["w_in1"], out["w_gate1"], out["w_out1"] = tiles(w[:, :3 * E]), tiles(w[:, 3 * E:]), tiles(a["w_out"][1])
    hv = np.zeros((P, 5, 3 * KE), f)
    for q in range(3):
        hv[:, q, :] = columns(a["l1_conv_w"][q])
    hv[:, 3, :] = columns(a["l1_conv_b"])
    hv[:, 4, 0:KE] = columns(a["l1_filter_bias"])
    out["hyena_vec"] = hv
    out["f_w1"] = a["l1_f_w1"]
    out["f_w23"] = np.stack([a["l1_f_w2"], a["l1_f_w3"]], 1)
    out["f_vec"] = np.stack([a["l1_f_b1"], a["l1_f_b2"], a["l1_f_b3"], a["l1_sin_freq"]], 1)
    out["f_w4"] = a["l1_f_w4"].reshape(64, 2, E)
    out.update(hyena_constants())
    for l in range(2):
        w = a["w_in_2"][l]
        col = lambda n: w[:, n * BW:(n + 1) * BW]
        out[f"w_feature{l}"] = np.concatenate([tiles(col(n)) for n in (0, 2, 4, 6, 5, 7, 8, 10)])
        out[f"w_token{l}"] = np.stack([col(n).reshape(KD, P, BW).transpose(1, 0, 2) for n in (1, 3, 9)])
        logits = tiles(w[:, 11 * BW:]).reshape(3, KD, P, D).transpose(1, 0, 2, 3)
        branch = np.stack([tiles(a["w_branch_out_2"][l, b]) for b in range(3)], 1)
        out[f"w_merge{l}"] = np.concatenate([logits, branch], 3)
        out[f"w_last{l}"] = tiles(a["w_out_2"][l])
    every = lambda v: np.broadcast_to(v[:, None], (v.shape[0], P) + v.shape[1:])
    out["ret_logit"] = every(a["ret_decay_logit_2"].reshape(2, 8))
    out["lambdas"] = every(np.stack([a["diff_lambda_q_2"], a["diff_lambda_k_2"]], 1))
    out["mlp_w"] = a["mlp_w_s_2"].transpose(0, 3, 1, 2)
    out["mlp_b"] = every(a["mlp_b_s_2"])
    out.update(attention_constants())
    return {k: np.ascontiguousarray(v) for k, v in out.items()}


def hyena_constants():
    f = np.float32
    L, bands = NX, 16
    t = np.linspace(0.0, 1.0, L, dtype=f)[:, None]
    freqs = np.linspace(1e-4, bands - 1, bands, dtype=f)[None, :]
    ang = f(2.0 * math.pi / L) * np.arange(L, dtype=f)[:, None] * freqs
    z = np.concatenate([t, np.cos(ang), -np.sin(ang)], 1)
    deltas = np.abs(np.linspace(math.log(1e-2) / 1.5, math.log(1e-2) / 0.3, E, dtype=f))
    window = np.exp(-t * deltas).astype(f)
    w = math.pi * (2 * np.arange(L) + 1) / (2 * L)
    ph = np.arange(L)[:, None] * w[None, :]
    dft = np.concatenate([np.cos(ph), -np.sin(ph)], 1)
    idft = np.concatenate([np.cos(ph).T, -np.sin(ph).T], 0) / L
    return {"z_t": z.T.astype(f), "window": window.reshape(2, P, E).transpose(1, 0, 2),
            "dft": dft.reshape(2, P, 4 * P).transpose(1, 0, 2).astype(f),
            "idft": idft.reshape(4, P, NX).transpose(1, 0, 2).astype(f)}


def attention_constants():
    f = np.float32
    j = np.arange(NX).reshape(2, P).T[:, :, None]
    i = np.arange(NX)[None, None, :]
    dist = np.stack([np.maximum(i - j, 0), np.maximum(j - i, 0), NX + i - j, NX - i + j], 1).astype(f)
    out = {"distances": dist.reshape(P, 4, 2 * NX), "same": (i == j).astype(f).reshape(P, 2 * NX)}
    row, col = np.arange(NX) // GRID, np.arange(NX) % GRID
    rope = []
    for dim in (128, 64):
        n = dim // 4
        inv = (f(10000.0) ** (-np.arange(n, dtype=f) / n)).astype(f)
        ang = np.concatenate([row.astype(f)[:, None] * inv, col.astype(f)[:, None] * inv], 1).T
        q = np.arange(P)
        sign = np.where(q % dim < dim // 2, -1.0, 1.0).astype(f)
        rope += [np.cos(ang)[q % (dim // 2)], np.sin(ang)[q % (dim // 2)] * sign[:, None]]
    out["rope"] = np.stack(rope, 1).astype(f)
    q = np.arange(P)
    out["swaps"] = np.stack([(q[:, None] == (q[None, :] ^ s)) for s in (64, 32)], 1).astype(f)
    return out


def kernel(**inputs):
    import concourse.bacc as bacc
    from concourse.bass_utils import run_bass_kernel_spmd

    nc = bacc.Bacc("TRN2", target_bir_lowering=False, num_devices=1)
    arrays = {f"in_{k}": v for k, v in layouts({k: np.asarray(v) for k, v in inputs.items()}).items()}
    aps = {k[3:]: nc.dram_tensor(k, v.shape, mybir.dt.from_np(v.dtype), kind="ExternalInput").ap() for k, v in arrays.items()}
    out = nc.dram_tensor("out_x", (P, KD, NX), F32, kind="ExternalOutput").ap()
    program(nc, aps, out)
    got = run_bass_kernel_spmd(nc, [arrays], core_ids=[0]).results[0]["out_x"]
    return np.ascontiguousarray(got.transpose(2, 1, 0)).reshape(1, NX, D)
```

```python
import math
from contextlib import ExitStack, contextmanager

import numpy as np

import concourse.bass as bass
from concourse import mybir

F32 = mybir.dt.float32
ALU = mybir.AluOpType
ACT = mybir.ActivationFunctionType
AX_X = mybir.AxisListType.X
ds = bass.ds

P = 128
D = 1024
KD = D // P
E = 2048
KE = E // P
NX = 256
NT = 2 * NX
GRID = 64
HEAD = 64
C = 64
NCH = NT // C
LORA = 64
LEVELS = 6
EPS = 1e-6
GN_EPS = 64e-5
DECAY = math.exp(-0.5)
BW = 512
KB = BW // P
HEADS = 4
V_W0, V_A0, V_KK, V_KA, V_RK, V_LNW, V_LNB = 0, 2, 4, 5, 6, 7, 8
RING = 8
BIG = float(2 ** 23) * 1.5


class Named:
    pass


class Steps:

    def __init__(self, eng, sem):
        self.eng, self.sem, self.n = eng, sem, 0

    def __call__(self, ins):
        self.n += 1
        ins.then_inc(self.sem, 1)
        return self.n

    def wait(self, n=None):
        self.eng.wait_ge(self.sem, self.n if n is None else n)


STAGES = [0]


@contextmanager
def stage(nc, *names):
    with ExitStack() as c:
        STAGES[0] += 1
        sems = [c.enter_context(nc.semaphore(f"{n}_{STAGES[0]}")) for n in names]
        with nc.Block() as block:
            yield block, dict(zip(names, sems))
        for s in sems:
            nc.gpsimd.sem_clear(s)
        nc.all_engine_barrier()


@contextmanager
def repeat(eng, n):
    if n == 1:
        yield 0
    else:
        with eng.Fori(0, n) as i:
            yield i


def dense(nc, R, w, M, K, N, rhs, out, evac=None):
    S = max(1, K // 8)
    width = K * P // S
    G = min(M, RING // S)
    assert M % G == 0 and (G % 4 == 0)
    with stage(nc, *[f"w_loaded{s}" for s in range(RING)], "tile_done", "bank_free", "part") as (block, s):
        loaded = [s[f"w_loaded{j}"] for j in range(RING)]

        @block.sync
        def _(sp):
            with repeat(sp, M // G) as i:
                for j in range(G):
                    sp.wait_ge(s["tile_done"], i * G + (j + 1))
                    for h in range(S):
                        src = w[ds(i * G + j, 1), :, h * width:(h + 1) * width].rearrange("a p n -> p (a n)")
                        sp.dma_start(R.ring[:, j * S + h, 0:width], src).then_inc(loaded[j * S + h], 16)

        @block.tensor
        def _(pe):
            pe.sem_inc(s["tile_done"], G)
            with repeat(pe, M // G) as i:
                for j in range(G):
                    pe.wait_ge(s["bank_free"], i * G + (j + 1))
                    for k in range(K):
                        if k % 8 == 0:
                            pe.wait_ge(loaded[j * S + k // 8], i * 16 + 16)
                        a = (k % 8) * P
                        mm = pe.matmul(R.ps[:, j % 4, 0:N], R.ring[:, j * S + k // 8, a:a + P], rhs(k),
                                       start=(k == 0), stop=(k == K - 1))
                    mm.then_inc(s["tile_done"], 1)

        @block.vector
        def _(dve):
            dve.sem_inc(s["bank_free"], 4)
            with repeat(dve, M // G) as i:
                for j in range(G):
                    dve.wait_ge(s["tile_done"], i * G + (G + j + 1))
                    if evac is None:
                        last = dve.tensor_copy(out(i * G + j), R.ps[:, j % 4, 0:N])
                    else:
                        last = evac(dve, s, i * G + j, i * G + j, j % 4)
                    last.then_inc(s["bank_free"], 1)


def token_major(nc, R, w, rhs, ntiles, out):
    with stage(nc, "w_loaded", "done", "copied") as (block, s):
        wt = R.ring[:, 0:4, :].rearrange("p a (b n) -> p (a b) n", n=512)

        @block.sync
        def _(sp):
            sp.dma_start(wt, w).then_inc(s["w_loaded"], 16)

        @block.tensor
        def _(pe):
            pe.wait_ge(s["w_loaded"], 16)
            for t in range(ntiles):
                for k in range(KD):
                    mm = pe.matmul(R.ps[:, t, :], rhs(k, t), wt[:, k, :], start=(k == 0), stop=(k == KD - 1))
                mm.then_inc(s["done"], 1)

        @block.vector
        def _(dve):
            for t in range(ntiles):
                dve.wait_ge(s["done"], t + 1)
                dve.tensor_copy(out(t), R.ps[:, t, :]).then_inc(s["copied"], 1)


def inverse_rms(nc, R, src, rstd, N, width, tiles):
    with stage(nc, "squared", "summed", "mean", "root", "used") as (block, s):
        @block.scalar
        def _(act):
            for t in range(tiles):
                act.activation(R.sq[:, t, 0:N], src(t), ACT.Square).then_inc(s["squared"], 1)
            act.wait_ge(s["mean"], 1)
            act.activation(rstd, rstd, ACT.Sqrt).then_inc(s["root"], 1)

        @block.tensor
        def _(pe):
            for t in range(tiles):
                pe.wait_ge(s["squared"], t + 1)
                mm = pe.matmul(R.ps[:, 0, 0:N], R.ones[:, :], R.sq[:, t, 0:N], start=(t == 0), stop=(t == tiles - 1))
            mm.then_inc(s["summed"], 1)

        @block.vector
        def _(dve):
            dve.wait_ge(s["summed"], 1)
            dve.tensor_scalar(rstd, R.ps[:, 0, 0:N], 1.0 / width, EPS, ALU.mult, ALU.add).then_inc(s["mean"], 1)
            dve.wait_ge(s["root"], 1)
            dve.reciprocal(rstd, rstd).then_inc(s["used"], 1)


def modulate(nc, R, mods, g, N):
    inverse_rms(nc, R, lambda t: R.x[:, t, 0:N], R.rstd[:, 0:N], N, D, KD)
    with stage(nc, "gain", "scaled", "shifted") as (block, s):
        @block.vector
        def _(dve):
            for c in range(N // NX):
                dve.scalar_tensor_tensor(R.gain[:, c, :], mods[:, c, KD:2 * KD], 1.0, g, ALU.add, ALU.mult).then_inc(s["gain"], 1)
            for k in range(KD):
                dve.tensor_tensor(R.h[:, k, 0:N], R.x[:, k, 0:N], R.rstd[:, 0:N], ALU.mult).then_inc(s["scaled"], 1)

        @block.scalar
        def _(act):
            act.wait_ge(s["gain"], N // NX)
            for k in range(KD):
                act.wait_ge(s["scaled"], k + 1)
                for c in range(N // NX):
                    cols = slice(c * NX, (c + 1) * NX)
                    act.activation(R.h[:, k, cols], R.h[:, k, cols], ACT.Identity, bias=mods[:, c, k:k + 1],
                                   scale=R.gain[:, c, k:k + 1]).then_inc(s["shifted"], 1)


def add_back(nc, R, o, mods, g, N):
    inverse_rms(nc, R, lambda t: o[:, t, 0:N], R.rstd[:, 0:N], N, D, KD)
    with stage(nc, "gain", "scaled", "added") as (block, s):
        @block.vector
        def _(dve):
            for c in range(N // NX):
                dve.tensor_tensor(R.gain[:, c, :], mods[:, c, 2 * KD:3 * KD], g, ALU.mult).then_inc(s["gain"], 1)
            for k in range(KD):
                dve.tensor_tensor(o[:, k, 0:N], o[:, k, 0:N], R.rstd[:, 0:N], ALU.mult).then_inc(s["scaled"], 1)
            dve.wait_ge(s["gain"], N // NX)
            for k in range(KD):
                dve.wait_ge(s["scaled"], k + 1)
                for c in range(N // NX):
                    cols = slice(c * NX, (c + 1) * NX)
                    dve.scalar_tensor_tensor(R.x[:, k, cols], o[:, k, cols], R.gain[:, c, k:k + 1],
                                             R.x[:, k, cols], ALU.mult, ALU.add).then_inc(s["added"], 1)


def alloc(nc, R, sb, c):
    R.x = sb("x", KD, NT)
    R.h = sb("h", KD, NT)
    R.sq = sb("sq", KD, NT)
    R.ring = sb("ring", RING, D)
    R.eye, R.ones, R.head_ones = sb("eye", P), sb("ones", P), sb("head_ones", P)
    R.cond, R.vec = sb("cond", KD, 4), sb("vec", 9, 24)
    R.mods = sb("mods", 4, 2, 24)
    R.rstd, R.gain, R.eps = sb("rstd", NT), sb("gain", 2, KD), sb("eps", 1)
    R.ps = c.enter_context(nc.psum_tensor("ps", [P, 8, 512], F32))


def setup(nc, R, I):
    with stage(nc, "loaded", "silu", "ones") as (block, s):
        loads = [(R.x[:, :, :], I["x_t"]), (R.eye[:, :], I["eye"]), (R.head_ones[:, :], I["head_ones"]),
                 (R.cond[:, :, :], I["cond"]), (R.vec[:, :, :], I["vectors"])]

        @block.sync
        def _(sp):
            for dst, src in loads:
                sp.dma_start(dst, src).then_inc(s["loaded"], 16)

        @block.gpsimd
        def _(pool):
            pool.memset(R.ones[:, :], 1.0).then_inc(s["ones"], 1)
            pool.memset(R.eps[:, :], EPS).then_inc(s["ones"], 1)

        @block.scalar
        def _(act):
            act.wait_ge(s["loaded"], 16 * len(loads))
            act.activation(R.cond[:, :, :], R.cond[:, :, :], ACT.Silu).then_inc(s["silu"], 1)
    modulations(nc, R, I)


def modulations(nc, R, I):
    CH = 4
    steps = 4 * 3 * D // 512 // CH
    with ExitStack() as c:
        rows = c.enter_context(nc.sbuf_tensor("mod_rows", [4, CH, 512], F32))
        with stage(nc, *[f"w_loaded{n}" for n in range(RING)], "used", "copied", "turned", "bias") as (block, s):
            loaded = [s[f"w_loaded{n}"] for n in range(RING)]

            @block.sync
            def _(sp):
                with sp.Fori(0, steps) as i:
                    for q in range(CH):
                        for piece in range(4):
                            slot = 4 * (q % 2) + piece
                            sp.wait_ge(s["used"], i * (4 * CH) + (4 * q + piece + 1))
                            sp.dma_start(R.ring[:, slot, :], I["w_mods"][ds(i * CH + q, 1), piece].rearrange("a p n -> p (a n)")).then_inc(loaded[slot], 16)

            @block.tensor
            def _(pe):
                pe.sem_inc(s["used"], RING)
                with pe.Fori(0, steps) as i:
                    for q in range(CH):
                        pe.wait_ge(s["copied"], i * CH + (q + 1))
                        for k in range(KD):
                            slot = 4 * (q % 2) + k // 2
                            if k % 2 == 0:
                                pe.wait_ge(loaded[slot], i * (16 * CH // 2) + 16 * (q // 2 + 1))
                            mm = pe.matmul(R.ps[0:4, q, :], R.cond[:, k, :], R.ring[:, slot, (k % 2) * 512:(k % 2) * 512 + 512],
                                           start=(k == 0), stop=(k == KD - 1))
                            if k % 2:
                                mm.then_inc(s["used"], 1)
                    for q in range(CH):
                        pe.wait_ge(s["copied"], i * CH + (CH + q + 1))
                        for t in range(4):
                            mm = pe.matmul(R.ps[:, 6, ds(i * (16 * CH) + (4 * q + t) * 4, 4)], rows[:, q, t * P:(t + 1) * P], R.eye[0:4, 0:4], start=True, stop=True)
                        mm.then_inc(s["turned"], 1)

            @block.scalar
            def _(act):
                act.sem_inc(s["copied"], CH)
                with act.Fori(0, steps) as i:
                    for q in range(CH):
                        act.wait_ge(s["used"], i * (4 * CH) + (RING + 4 * q + 4))
                        act.wait_ge(s["turned"], i * CH + (q + 1))
                        act.activation(rows[:, q, :], R.ps[0:4, q, :], ACT.Copy).then_inc(s["copied"], 1)

            @block.vector
            def _(dve):
                dve.sem_inc(s["turned"], CH)
                dve.wait_ge(s["turned"], CH + 4 * 3 * D // 512)
                turned = R.ps[:, 6, 0:4 * 4 * 24].rearrange("p (n m c) -> p n m c", m=24, c=4)
                for n in range(4):
                    for c in range(2):
                        dve.tensor_tensor(R.mods[:, n, c, :], turned[:, n, :, 2 * (n // 2) + c], R.vec[:, n, 0:24], ALU.add).then_inc(s["bias"], 1)



def shift_mix(nc, R, W, I):
    with stage(nc, "diff", "loaded") as (block, s):
        @block.sync
        def _(sp):
            sp.dma_start(W.mu[:, :, :], I["mu"]).then_inc(s["loaded"], 16)
            sp.wait_ge(s["loaded"], 16)

        @block.vector
        def _(dve):
            step = Steps(dve, s["diff"])
            h, d = R.h, R.sq
            for q in range(4):
                ks = slice(2 * q, 2 * q + 2)
                for k in (2 * q, 2 * q + 1):
                    hg = h[:, k, 0:NX].rearrange("p (r c) -> p r c", c=GRID)
                    dg = d[:, k, 0:NX].rearrange("p (r c) -> p r c", c=GRID)
                    if q == 0:
                        step(dve.tensor_tensor(dg[:, :, 1:], hg[:, :, :-1], hg[:, :, 1:], ALU.subtract))
                        step(dve.tensor_scalar(dg[:, :, 0:1], hg[:, :, 0:1], -1.0, None, ALU.mult))
                    elif q == 1:
                        step(dve.tensor_tensor(dg[:, :, :-1], hg[:, :, 1:], hg[:, :, :-1], ALU.subtract))
                        step(dve.tensor_scalar(dg[:, :, GRID - 1:], hg[:, :, GRID - 1:], -1.0, None, ALU.mult))
                    elif q == 2:
                        step(dve.tensor_tensor(dg[:, 1:, :], hg[:, :-1, :], hg[:, 1:, :], ALU.subtract))
                        step(dve.tensor_scalar(dg[:, 0:1, :], hg[:, 0:1, :], -1.0, None, ALU.mult))
                    else:
                        step(dve.tensor_tensor(dg[:, :-1, :], hg[:, 1:, :], hg[:, :-1, :], ALU.subtract))
                        step(dve.tensor_scalar(dg[:, 3:4, :], hg[:, 3:4, :], -1.0, None, ALU.mult))
            a, b = h[:, 0:4, NX:], d[:, 0:4, NX:]
            step(dve.tensor_tensor(b[:, :, 1:], a[:, :, :-1], a[:, :, 1:], ALU.subtract))
            step(dve.tensor_scalar(b[:, :, 0:1], a[:, :, 0:1], -1.0, None, ALU.mult))
            a, b = h[:, 4:8, NX:], d[:, 4:8, NX:]
            step(dve.tensor_tensor(b[:, :, :-1], a[:, :, 1:], a[:, :, :-1], ALU.subtract))
            step(dve.tensor_scalar(b[:, :, NX - 1:], a[:, :, NX - 1:], -1.0, None, ALU.mult))

    def mixes(groups):
        with stage(nc, "mixed") as (block, s):
            @block.vector
            def _(dve):
                for g, dst, N in groups:
                    for k in range(KD):
                        dve.scalar_tensor_tensor(dst[:, k, 0:N], R.sq[:, k, 0:N], W.mu[:, g, k:k + 1],
                                                 R.h[:, k, 0:N], ALU.mult, ALU.add).then_inc(s["mixed"], 1)

    mixes([(4, W.mix_k, NT), (5, W.mix_v, NT)])
    with stage(nc, "loaded", "done", "tanh") as (block, s):
        wt = R.ring[:, 0:2, :].rearrange("p a (k n) -> p a k n", n=P)

        @block.sync
        def _(sp):
            sp.dma_start(R.ring[:, 0:2, :], I["w_low"]).then_inc(s["loaded"], 16)

        @block.tensor
        def _(pe):
            pe.wait_ge(s["loaded"], 16)
            for n, mix in enumerate((W.mix_k, W.mix_v)):
                for k in range(KD):
                    mm = pe.matmul(R.ps[:, n, :], wt[:, n, k, :], mix[:, k, :], start=(k == 0), stop=(k == KD - 1))
                mm.then_inc(s["done"], 1)

        @block.scalar
        def _(act):
            act.wait_ge(s["done"], 1)
            act.activation(W.low[:, 0, :], R.ps[:, 0, :], ACT.Tanh).then_inc(s["tanh"], 1)
            act.wait_ge(s["done"], 2)
            act.activation(W.low[:, 1, :], R.ps[:, 1, :], ACT.Copy).then_inc(s["tanh"], 1)

    mixes([(0, W.mix_r, NX), (1, W.mix_k, NT), (2, W.mix_v, NT), (3, W.mix_g, NX)])


def nat(p):
    return 64 * p


def oth(p):
    return 64 - 64 * p


def rwkv_layer(nc, R, I):
    with ExitStack() as c:
        def sb(name, *shape):
            return c.enter_context(nc.sbuf_tensor(name, [P, *shape], F32))

        W = Named()
        W.mix_r, W.mix_g = sb("mix_r", KD, NX), sb("mix_g", KD, NX)
        W.mix_k, W.mix_v = sb("mix_k", KD, NT), sb("mix_v", KD, NT)
        W.low = sb("low", 2, NT)
        with ExitStack() as c2:
            W.mu = c2.enter_context(nc.sbuf_tensor("mu", [P, 6, KD], F32))
            shift_mix(nc, R, W, I)
        W.u_pairs = R.ring[:, 4:8, :].rearrange("p a (k n) -> p (a k) n", n=NX)
        hv = R.h[:, :, :]
        W.r, W.gate = hv[:, 0, 0:NX], hv[:, 0, NX:]
        W.k, W.kk, W.ksum, W.k1, W.k2, W.cum = (hv[:, n, :] for n in range(1, 7))
        W.sg = hv[:, 7, :]
        sv = R.sq[:, :, :]
        W.t0, W.t1, W.t2 = sv[:, 0, :], sv[:, 1, :], sv[:, 2, :]
        W.vtok = sv[:, 3, :].rearrange("p (j n) -> p j n", n=P)
        W.ytok = sv[:, 4, 0:NX].rearrange("p (j n) -> p j n", n=P)
        W.bonus = sv[:, 4, NX:].rearrange("p (j n) -> p j n", n=P)
        W.rate = sv[:, 5, :]
        W.tmp = sv[:, 6, :]
        W.tmp2 = sv[:, 7, :]
        W.pv = sb("pair_vec", 10)
        W.lw = sb("lora_w", 2, P)
        W.masks = R.x[:, 6:8, NX:].rearrange("p z (q n) -> p z q n", n=P)
        W.lmask = R.x[:, 0:LEVELS, NX:].rearrange("p l (z n) -> p l z n", n=P)
        W.bk = sb("bk", NCH, P)
        W.ar = sb("ar", 2, NCH, P)
        W.A = sb("A", 2, 2, 4, 2, P)
        W.BK = sb("BK", 2, 2, 4, 2, HEAD)
        W.U = sb("U", 2, 2, 4, P)
        W.Tm = sb("Tm", 2, 4, P)
        W.Y = sb("Y", 2, 4, P)
        W.At = sb("At", 2, 2, 4, P)
        W.vnext, W.gnext, W.ln, W.yt = sb("v_next", NT), sb("gate_next", NX), sb("ln", 2), sb("y_turned", NX)
        W.pc = sb("pc", 2, NCH)
        W.H = sb("H", 2, 2, HEAD)
        W.HP = sb("HP", 2, 2, HEAD)
        W.Xs = sb("Xs", 2, 2, HEAD)
        W.Z = sb("Z", 2, 2, HEAD)
        W.st = sb("stats", 4, 4)
        W.coef = sb("coef", 4)
        W.reset = R.rstd
        with stage(nc, "loaded", "zeroed") as (block, s):
            @block.sync
            def _(sp):
                sp.dma_start(W.masks[:, :, :, :], I["masks"]).then_inc(s["loaded"], 16)
                sp.dma_start(W.lmask[:, :, :, :], I["level_masks"]).then_inc(s["loaded"], 16)
                sp.wait_ge(s["loaded"], 32)

            @block.vector
            def _(dve):
                step = Steps(dve, s["zeroed"])
                step(dve.memset(W.reset[:, :], 1.0))
                step.wait()
                step(dve.memset(W.reset[:, :].rearrange("p (c t) -> p c t", t=C)[:, :, 0:1], 0.0))
                step(dve.memset(W.At[:, :, :, :, :], 0.0))
                step(dve.memset(W.ar[:, :, :, :], 0.0))
        rwkv_project_first(nc, R, W, I)
        rwkv_pair(nc, R, W, I, 0, True, False)
        with nc.Fori(1, KE - 1) as pair:
            rwkv_pair(nc, R, W, I, pair, False, False)
        rwkv_pair(nc, R, W, I, KE - 1, False, True)
        with stage(nc, *READOUT_SEMS) as (block, s):
            @block.tensor
            def _(pe):
                for _ in readout_pe(pe, R, W, s):
                    pass

            @block.scalar
            def _(act):
                readout_act(act, R, W, s)

            @block.vector
            def _(dve):
                for _ in readout_dve(dve, R, W, s, KE - 1):
                    pass

        uT = W.mix_k[:, :, :].rearrange("p a (b n) -> p (a b) n", n=NX)
        with stage(nc, "moved") as (block, s):
            @block.vector
            def _(dve):
                dve.tensor_copy(uT, W.u_pairs).then_inc(s["moved"], 1)
        dense(nc, R, I["w_out0"], KD, KE, NX, lambda k: uT[:, k, :], lambda m: R.h[:, ds(m, 1), 0:NX].rearrange("p a n -> p (a n)"))
    add_back(nc, R, R.h, R.mods[:, 0], R.vec[:, 5, 0:KD], NX)


def at(i, n):
    return ds(i + n, 1)


def rwkv_pair(nc, R, W, I, pair, first, last):
    first_direction(nc, R, W, I, pair, first, last)
    inverse_and_direction(nc, R, W)
    with stage(nc, *INVERSE_SEMS) as (block, s):
        @block.tensor
        def _(pe):
            for _ in inverse_pe(pe, R, W, s, 1):
                pass

        @block.vector
        def _(dve):
            for _ in inverse_dve(dve, R, W, s, 1):
                pass

    rwkv_scan(nc, R, W, I, pair, last)



PROJECT_SEMS = ("v_loaded", "k_done", "r_done", "g_done", "v_done", "k_out", "vt_out", "r_out", "g_out",
                "sq_out", "norm_sum", "root", "p_chain")


def project_pe(pe, R, W, s):
    wt = R.ring[:, 0:4, :].rearrange("p a (k n) -> p a k n", n=P)
    for k in range(KD):
        mm = pe.matmul(R.ps[:, 2, :], wt[:, 0, k, :], W.mix_k[:, k, :], start=(k == 0), stop=(k == KD - 1))
        if k == KD - 1:
            mm.then_inc(s["k_done"], 1)
        yield
    for j in range(4):
        for k in range(KD):
            mm = pe.matmul(R.ps[:, 3, j * P:(j + 1) * P], W.mix_v[:, k, j * P:(j + 1) * P], wt[:, 1, k, :],
                           start=(k == 0), stop=(k == KD - 1))
            if k == KD - 1 and j == 3:
                mm.then_inc(s["v_done"], 1)
            if k % 4 == 3:
                yield
    pe.wait_ge(s["sq_out"], 1)
    pe.matmul(R.ps[:, 2, :], R.head_ones[:, :], W.t0, start=True, stop=True).then_inc(s["norm_sum"], 1)
    yield
    for n, mix, bank, done, read in ((2, W.mix_r, 3, "r_done", "vt_out"), (3, W.mix_g, 2, "g_done", "root")):
        pe.wait_ge(s[read], 1)
        for k in range(KD):
            mm = pe.matmul(R.ps[:, bank, 0:NX], wt[:, n, k, :], mix[:, k, :], start=(k == 0), stop=(k == KD - 1))
            if k == KD - 1:
                mm.then_inc(s[done], 1)
            if k % 2:
                yield


def project_act(act, R, W, s, I, pair):
    act.dma_start(W.pv[:, :], I["pair_vec"][ds(pair, 1)].rearrange("a p n -> p (a n)")).then_inc(s["v_loaded"], 16)
    act.dma_start(W.lw[:, :, :], I["lora"][ds(pair, 1)].rearrange("a p z n -> p (a z) n")).then_inc(s["v_loaded"], 16)
    yield
    act.wait_ge(s["v_loaded"], 32)
    act.wait_ge(s["k_out"], 1)
    act.activation(W.t0, W.k, ACT.Square, scale=W.pv[:, V_KK:V_KK + 1]).then_inc(s["sq_out"], 1)
    yield
    act.wait_ge(s["v_done"], 1)
    act.activation(W.vnext[:, :], R.ps[:, 3, :], ACT.Copy).then_inc(s["vt_out"], 1)
    yield
    act.wait_ge(s["norm_sum"], 1)
    act.activation(W.t1, R.ps[:, 2, :], ACT.Sqrt).then_inc(s["root"], 1)
    yield
    act.wait_ge(s["r_done"], 1)
    act.activation(W.r, R.ps[:, 3, 0:NX], ACT.Copy).then_inc(s["r_out"], 1)
    act.wait_ge(s["g_done"], 1)
    act.activation(W.gnext[:, :], R.ps[:, 2, 0:NX], ACT.Silu).then_inc(s["g_out"], 1)
    yield


def project_dve(dve, R, W, s):
    step = Steps(dve, s["p_chain"])
    dve.wait_ge(s["k_done"], 1)
    dve.tensor_copy(W.k, R.ps[:, 2, :]).then_inc(s["k_out"], 1)
    yield
    dve.wait_ge(s["k_out"], 1)
    dve.wait_ge(s["v_loaded"], 32)
    step(dve.tensor_scalar(W.k1, W.k, W.pv[:, V_KA:V_KA + 1], None, ALU.mult))
    step(dve.tensor_scalar(W.kk, W.k, W.pv[:, V_KK:V_KK + 1], None, ALU.mult))
    yield
    step.wait()
    step(dve.tensor_tensor(W.k2, W.k, W.k1, ALU.subtract))
    yield
    dve.wait_ge(s["root"], 1)
    step(dve.tensor_scalar(W.t1, W.t1, 1e-12, None, ALU.max))
    step.wait()
    step(dve.reciprocal(W.t1, W.t1))
    step.wait()
    step(dve.tensor_tensor(W.kk, W.kk, W.t1, ALU.mult))
    yield


def rwkv_project_first(nc, R, W, I):
    with stage(nc, "w_loaded", *PROJECT_SEMS) as (block, s):
        @block.sync
        def _(sp):
            for n in range(4):
                sp.dma_start(R.ring[:, n, :], I["w_rkvg"][0, :, n * D:(n + 1) * D]).then_inc(s["w_loaded"], 16)

        @block.tensor
        def _(pe):
            pe.wait_ge(s["w_loaded"], 64)
            for _ in project_pe(pe, R, W, s):
                pass

        @block.scalar
        def _(act):
            for _ in project_act(act, R, W, s, I, 0):
                pass

        @block.vector
        def _(dve):
            for _ in project_dve(dve, R, W, s):
                pass


DIRECTION_SEMS = ("low_done", "sig", "exps_in", "exps", "packed", "d_chain", "a_done", "a_out", "bk_done", "bk_out", "at_out")


def direction_pe_low(pe, R, W, s, z, banks):
    for n in range(2):
        pe.matmul(R.ps[:, banks[n], :], W.lw[z * 64:z * 64 + 64, n, :], W.low[z * 64:z * 64 + 64, n, :],
                  start=True, stop=True).then_inc(s["low_done"], 1)


def direction_pe(pe, R, W, s, z, banks):
    pe.wait_ge(s["packed"], 8)
    nb = len(banks)
    for g in range(4):
        h, jj = g // 2, g % 2
        if g >= nb:
            pe.wait_ge(s["a_out"], g - nb + 1)
        for q in range(4):
            c = 2 * (2 * jj + q // 2) + q % 2
            mm = pe.matmul(R.ps[:, banks[g % nb], q * P:(q + 1) * P], W.bk[h * 64:h * 64 + 64, c, :],
                           W.ar[h * 64:h * 64 + 64, z, c, :], start=True, stop=True)
        mm.then_inc(s["a_done"], 1)
        yield
    for h in range(2):
        pe.wait_ge(s["a_out"], 3 + h if nb == 2 else 1 + h)
        for c in range(NCH):
            mm = pe.transpose(R.ps[:, banks[h], c * 64:(c + 1) * 64], W.bk[h * 64:h * 64 + 64, c, :],
                              R.eye[h * 64:h * 64 + 64, h * 64:h * 64 + 64])
        mm.then_inc(s["bk_done"], 1)
        yield


def direction_act(act, R, W, s, z, low_banks, banks):
    act.wait_ge(s["low_done"], 1)
    act.activation(W.sg, R.ps[:, low_banks[0], :], ACT.Sigmoid, bias=W.pv[:, V_W0 + z:V_W0 + z + 1]).then_inc(s["sig"], 1)
    act.wait_ge(s["low_done"], 2)
    act.activation(W.rate, R.ps[:, low_banks[1], :], ACT.Sigmoid, bias=W.pv[:, V_A0 + z:V_A0 + z + 1]).then_inc(s["sig"], 1)
    act.wait_ge(s["exps_in"], 1)
    act.activation(W.t0, W.cum, ACT.Exp, scale=-DECAY).then_inc(s["exps"], 1)
    act.activation(W.t2, W.cum, ACT.Exp, scale=DECAY).then_inc(s["exps"], 1)
    act.activation(W.t1, W.t1, ACT.Exp, scale=-DECAY).then_inc(s["exps"], 1)
    act.activation(W.pc[:, z, :], W.pc[:, z, :], ACT.Exp, scale=-DECAY).then_inc(s["exps"], 1)
    yield
    for h in range(2):
        act.wait_ge(s["bk_done"], h + 1)
        act.activation(W.BK[:, z, h].rearrange("p j q n -> p (j q n)"), R.ps[:, banks[h], :], ACT.Copy).then_inc(s["bk_out"], 1)
    yield


def direction_dve(dve, R, W, s, z, banks):
    chunks = lambda ap: ap.rearrange("p (c t) -> p c t", t=C)
    par = lambda ap, p: ap.rearrange("p (j q t) -> p j q t", q=2, t=C)[:, :, p, :]
    step = Steps(dve, s["d_chain"])
    dve.wait_ge(s["sig"], 1)
    step(dve.tensor_tensor_scan(W.cum, W.reset[:, :], W.sg, 0.0, ALU.mult, ALU.add))
    step.wait()
    tot = chunks(W.cum)[:, :, C - 1:C]
    step(dve.tensor_copy(W.pc[:, z, :], tot.rearrange("p c o -> p (c o)")))
    if z == 0:
        dve.tensor_tensor(W.t1, W.cum, W.sg, ALU.subtract).then_inc(s["exps_in"], 1)
    else:
        step(dve.tensor_tensor(chunks(W.t1), tot.broadcast_to([P, NCH, C]), chunks(W.cum), ALU.subtract))
        step.wait()
        dve.tensor_tensor(W.cum, W.t1, W.sg, ALU.add).then_inc(s["exps_in"], 1)
    yield
    dve.wait_ge(s["sig"], 2)
    step(dve.tensor_tensor(W.tmp, W.rate, W.k1, ALU.mult))
    step(dve.tensor_tensor(W.tmp2, W.rate, W.kk, ALU.mult))
    yield
    step.wait()
    step(dve.tensor_tensor(W.tmp, W.tmp, W.k2, ALU.add))
    step.wait()
    if z == 0:
        step(dve.tensor_copy(W.ksum, W.tmp))
    else:
        step(dve.tensor_tensor(W.ksum, W.ksum, W.tmp, ALU.add))
    yield
    bk = W.bk[:, :, :].rearrange("p (j q) n -> p j q n", q=2)
    ar = W.ar[:, z].rearrange("p (j q) n -> p j q n", q=2)
    dve.wait_ge(s["exps"], 2)
    for p in range(2):
        dve.tensor_tensor(bk[:, :, p, nat(p):nat(p) + 64], par(W.tmp, p), par(W.t2, p), ALU.mult).then_inc(s["packed"], 1)
        dve.tensor_tensor(bk[:, :, p, oth(p):oth(p) + 64], par(W.tmp2, p), par(W.t2, p), ALU.mult).then_inc(s["packed"], 1)
        dve.tensor_tensor(ar[:, 0:2, p, nat(p):nat(p) + 64], par(W.r, p), par(W.t0[:, 0:NX], p), ALU.mult).then_inc(s["packed"], 1)
        yield
    dve.wait_ge(s["exps"], 3)
    for p in range(2):
        dve.scalar_tensor_tensor(ar[:, :, p, oth(p):oth(p) + 64], par(W.t1, p), -1.0, par(W.kk, p), ALU.mult, ALU.mult).then_inc(s["packed"], 1)
    yield
    for g in range(4):
        h, jj = g // 2, g % 2
        dve.wait_ge(s["a_done"], g + 1)
        src = R.ps[:, banks[g % len(banks)], :].rearrange("p (j q) -> p j q", q=2 * P)
        dst = W.A[:, z, h, 2 * jj:2 * jj + 2].rearrange("p j q n -> p j (q n)")
        mask = W.masks[:, z].rearrange("p q n -> p (q n)").unsqueeze(1).broadcast_to([P, 2, 2 * P])
        dve.tensor_tensor(dst, src, mask, ALU.mult).then_inc(s["a_out"], 1)
        yield
    for h in range(2):
        dve.wait_ge(s["a_out"], 2 * h + 2)
        dve.tensor_copy(W.At[0:64, z, h, :, 0:64], W.A[0:64, z, h, :, 1, 0:64]).then_inc(s["at_out"], 1)
        dve.tensor_copy(W.At[64:128, z, h, :, 64:128], W.A[64:128, z, h, :, 0, 64:128]).then_inc(s["at_out"], 1)
    yield


def first_direction(nc, R, W, I, pair, first, last):
    with stage(nc, "w_loaded", *DIRECTION_SEMS, *READOUT_SEMS) as (block, s):
        if not last:
            @block.sync
            def _(sp):
                for n in range(4):
                    sp.dma_start(R.ring[:, n, :], I["w_rkvg"][at(pair, 1), :, n * D:(n + 1) * D].rearrange("a p n -> p (a n)")).then_inc(s["w_loaded"], 16)
                sp.wait_ge(s["w_loaded"], 64)

        @block.tensor
        def _(pe):
            direction_pe_low(pe, R, W, s, 0, (2, 3))
            if not first:
                for _ in readout_pe(pe, R, W, s):
                    pass
            pe.wait_ge(s["sig"], 2)
            for _ in direction_pe(pe, R, W, s, 0, (2, 3, 4, 5)):
                pass

        @block.scalar
        def _(act):
            part = direction_act(act, R, W, s, 0, (2, 3), (2, 3))
            next(part)
            if not first:
                readout_act(act, R, W, s)
            next(part)

        @block.vector
        def _(dve):
            part = direction_dve(dve, R, W, s, 0, (2, 3, 4, 5))
            if first:
                for _ in part:
                    pass
            else:
                out = readout_dve(dve, R, W, s, pair - 1)
                next(out)
                next(part)
                next(out)
                for _ in range(5):
                    next(part)
                for _ in range(9):
                    next(out, None)
                    next(part, None)
                for _ in part:
                    pass


def inverse_and_direction(nc, R, W):
    with stage(nc, *INVERSE_SEMS, *DIRECTION_SEMS, "rk", "coef", "coef_out", "bonus_out", "moved") as (block, s):
        @block.tensor
        def _(pe):
            direction_pe_low(pe, R, W, s, 1, (6, 7))
            inverse = inverse_pe(pe, R, W, s, 0)
            for _ in range(6):
                next(inverse)
            pe.wait_ge(s["sig"], 2)
            part = direction_pe(pe, R, W, s, 1, (6, 7))
            while next(inverse, "end") != "end":
                next(part, None)
            for _ in part:
                pass
            pe.wait_ge(s["rk"], 1)
            pe.wait_ge(s["bk_out"], 1)
            for j in range(2):
                mm = pe.matmul(R.ps[:, 6, 2 * j:2 * j + 2], W.t0[:, j * P:(j + 1) * P], R.head_ones[:, 63:65], start=True, stop=True)
            mm.then_inc(s["coef"], 1)

        @block.scalar
        def _(act):
            for _ in direction_act(act, R, W, s, 1, (6, 7), (6, 7)):
                pass

        @block.gpsimd
        def _(pool):
            pool.tensor_copy(W.vtok.rearrange("p j n -> p (j n)"), W.vnext[:, :]).then_inc(s["moved"], 1)
            pool.tensor_copy(W.gate, W.gnext[:, :]).then_inc(s["moved"], 1)
            pool.tensor_copy(W.ln[:, :], W.pv[:, V_LNW:V_LNB + 1]).then_inc(s["moved"], 1)

        @block.vector
        def _(dve):
            part = direction_dve(dve, R, W, s, 1, (6, 7))
            for n, _ in enumerate(inverse_dve(dve, R, W, s, 0)):
                if n in (0, 1, 3, 4, 6, 7, 10, 12, 13):
                    next(part)
            for _ in part:
                pass
            dve.scalar_tensor_tensor(W.t0[:, 0:NX], W.ksum[:, 0:NX], W.pv[:, V_RK:V_RK + 1], W.r, ALU.mult, ALU.mult).then_inc(s["rk"], 1)
            dve.wait_ge(s["coef"], 1)
            dve.tensor_copy(W.coef[:, :], R.ps[:, 6, 0:4]).then_inc(s["coef_out"], 1)
            dve.wait_ge(s["coef_out"], 1)
            bonus = W.bonus.rearrange("p j (h n) -> p (j h) n", n=64)
            v4 = W.vnext[:, 0:NX].rearrange("p (g n) -> p g n", n=64)
            dve.tensor_tensor(bonus, v4, W.coef[:, :].unsqueeze(2).broadcast_to([P, 4, 64]), ALU.mult).then_inc(s["bonus_out"], 1)


INVERSE_SEMS = ("y_done", "t_done", "y_out", "t_out", "u_out")



def inverse_pe(pe, R, W, s, z):
    for l in range(LEVELS):
        for h in range(2):
            n = 2 * l + h
            if n >= 2:
                pe.wait_ge(s["t_out"], n - 1)
            for j in range(4):
                mm = pe.matmul(R.ps[:, h, j * P:(j + 1) * P], W.At[:, z, h, j, :],
                               R.eye[:, :] if l == 0 else W.Tm[:, h, j, :], start=True, stop=True)
            mm.then_inc(s["y_done"], 1)
        yield
        if l == 0:
            continue
        for h in range(2):
            n = 2 * l + h
            pe.wait_ge(s["y_out"], n + 1)
            pe.wait_ge(s["u_out"], n + 1)
            for j in range(4):
                if l < LEVELS - 1:
                    pe.matmul(R.ps[:, 2 + h, j * P:(j + 1) * P], W.U[:, z, h, j, :], W.Y[:, h, j, :], start=True, stop=True)
                mm = pe.matmul(R.ps[:, 4 + h, j * P:(j + 1) * P], W.Y[:, h, j, :], W.U[:, z, h, j, :], start=True, stop=True)
            mm.then_inc(s["t_done"], 1)
        yield


def inverse_dve(dve, R, W, s, z):
    lm = lambda l, zz: W.lmask[:, l, zz, :].unsqueeze(1).broadcast_to([P, 4, P])
    eye4 = R.eye[:, :].unsqueeze(1).broadcast_to([P, 4, P])
    bank = lambda n: R.ps[:, n, :].rearrange("p (j n) -> p j n", n=P)
    for l in range(LEVELS):
        for h in range(2):
            n = 2 * l + h
            if l == 0:
                dve.tensor_tensor(W.U[:, z, h], W.At[:, z, h], lm(0, 1 - z), ALU.mult).then_inc(s["u_out"], 1)
            dve.wait_ge(s["y_done"], n + 1)
            dve.tensor_tensor(W.Y[:, h], bank(h), lm(l, z), ALU.mult).then_inc(s["y_out"], 1)
        yield
        for h in range(2):
            if l == 0:
                dve.wait_ge(s["y_out"], h + 1)
                dve.tensor_tensor(W.Tm[:, h], W.Y[:, h], eye4, ALU.add).then_inc(s["t_out"], 1)
                dve.wait_ge(s["u_out"], 2)
                dve.tensor_tensor(W.U[:, z, h], W.U[:, z, h], eye4, ALU.add).then_inc(s["u_out"], 1)
            else:
                dve.wait_ge(s["t_done"], 2 * (l - 1) + h + 1)
                if l < LEVELS - 1:
                    dve.tensor_tensor(W.Tm[:, h], W.Tm[:, h], bank(2 + h), ALU.add).then_inc(s["t_out"], 1)
                dve.tensor_tensor(W.U[:, z, h], W.U[:, z, h], bank(4 + h), ALU.add).then_inc(s["u_out"], 1)
                yield


ORDER = ([4, 5, 6, 7, 0, 1, 2, 3], [7, 6, 5, 4, 3, 2, 1, 0])


def rwkv_scan(nc, R, W, I, pair, last):
    with stage(nc, "x_done", "u_done", "y_done", "h_done", "v_in", "x_out", "u_out", "h_scaled", "h_out", "y_out",
               *PROJECT_SEMS) as (block, s):
        first = {}
        for n in range(4, NCH):
            for z in range(2):
                first.setdefault(ORDER[z][n], (n, z))

        @block.tensor
        def _(pe):
            part = iter(()) if last else project_pe(pe, R, W, s)
            for n in range(NCH):
                for z in range(2):
                    ch = ORDER[z][n]
                    j, p, x = ch // 2, ch % 2, ch < 4
                    a, r = oth(p), nat(p)
                    pe.wait_ge(s["h_out"], 2 * n + z + 1 if n else 2)
                    if n >= 5:
                        pe.wait_ge(s["y_out"], 2 * (n - 5) + z + 1)
                    pe.matmul(R.ps[:, z, 0:P], W.ar[:, z, ch, :], W.H[:, z].rearrange("p h n -> p (h n)"), start=True, stop=True)
                    for h in range(2):
                        g = h * 64
                        mm = pe.matmul(R.ps[a:a + 64, z, g:g + 64], W.A[r:r + 64, z, h, j, p, a:a + 64],
                                       W.vtok[r:r + 64, j, g:g + 64], start=False, stop=True, skip_group_check=True)
                    mm.then_inc(s["x_done"], 1)
                next(part, None)
                for z in range(2):
                    ch = ORDER[z][n]
                    j, p = ch // 2, ch % 2
                    a = oth(p)
                    pe.wait_ge(s["x_out"], 2 * n + z + 1)
                    for h in range(2):
                        mm = pe.matmul(R.ps[a:a + 64, 4 + z, h * 64:h * 64 + 64], W.U[a:a + 64, z, h, j, a:a + 64],
                                       W.Xs[a:a + 64, z, h, :], start=True, stop=True)
                    mm.then_inc(s["u_done"], 1)
                next(part, None)
                for z in range(2):
                    ch = ORDER[z][n]
                    j, p, x = ch // 2, ch % 2, ch < 4
                    r = nat(p)
                    pe.wait_ge(s["u_out"], 2 * n + z + 1)
                    pe.wait_ge(s["v_in"], 2 * n + z + 1)
                    for h in range(2):
                        mm = pe.matmul(R.ps[h * 64:h * 64 + 64, 6 + z, 0:64], W.BK[:, z, h, j, p, :], W.Z[:, z, h, :], start=True, stop=True)
                    mm.then_inc(s["h_done"], 1)
                    if x:
                        for h in range(2):
                            mm = pe.matmul(R.ps[r:r + 64, z, h * 64:h * 64 + 64], W.A[:, z, h, j, p, r:r + 64], W.Z[:, z, h, :],
                                           start=False, stop=True, skip_group_check=True)
                    else:
                        mm = pe.nop()
                    mm.then_inc(s["y_done"], 1)
                next(part, None)
            for _ in part:
                pass

        @block.scalar
        def _(act):
            part = iter(()) if last else project_act(act, R, W, s, I, pair + 1)
            next(part, None)
            for n in range(NCH):
                if n in (4, 6, 7):
                    next(part, None)
                for z in range(2):
                    ch = ORDER[z][n]
                    j, p = ch // 2, ch % 2
                    a = oth(p)
                    act.wait_ge(s["x_done"], 2 * n + z + 1)
                    act.activation(W.Xs[a:a + 64, z].rearrange("p h n -> p (h n)"), R.ps[a:a + 64, z, 0:P], ACT.Copy).then_inc(s["x_out"], 1)
                for z in range(2):
                    ch = ORDER[z][n]
                    j, p = ch // 2, ch % 2
                    a = oth(p)
                    if n:
                        act.wait_ge(s["y_done"], 2 * (n - 1) + z + 1)
                        act.wait_ge(s["h_done"], 2 * (n - 1) + z + 1)
                    act.wait_ge(s["u_done"], 2 * n + z + 1)
                    act.activation(W.Z[a:a + 64, z].rearrange("p h n -> p (h n)"), R.ps[a:a + 64, 4 + z, 0:128], ACT.Copy).then_inc(s["u_out"], 1)
            for _ in part:
                pass

        @block.gpsimd
        def _(pool):
            for n in range(NCH):
                for z in range(2):
                    ch = ORDER[z][n]
                    j, r = ch // 2, nat(ch % 2)
                    if n:
                        pool.wait_ge(s["y_done"], 2 * (n - 1) + z + 1)
                        pool.wait_ge(s["h_done"], 2 * (n - 1) + z + 1)
                    pool.tensor_copy(W.Z[r:r + 64, z].rearrange("p h n -> p (h n)"), W.vtok[r:r + 64, j, :]).then_inc(s["v_in"], 1)

        @block.vector
        def _(dve):
            for z in range(2):
                dve.memset(W.H[:, z], 0.0).then_inc(s["h_out"], 1)
            dve.wait_ge(s["h_out"], 2)
            part = iter(()) if last else project_dve(dve, R, W, s)
            for n in range(NCH):
                if n in (3, 4, 5):
                    next(part, None)
                for z in range(2):
                    ch = ORDER[z][n]
                    dve.wait_ge(s["h_out"], 2 * n + z + 1)
                    dve.tensor_scalar(W.HP[:, z], W.H[:, z], W.pc[:, z, ch:ch + 1], None, ALU.mult).then_inc(s["h_scaled"], 1)
                for z in range(2):
                    ch = ORDER[z][n]
                    j, p = ch // 2, ch % 2
                    r = nat(p)
                    dve.wait_ge(s["h_done"], 2 * n + z + 1)
                    dve.wait_ge(s["h_scaled"], 2 * n + z + 1)
                    for h in range(2):
                        g = slice(h * 64, h * 64 + 64)
                        up = dve.scalar_tensor_tensor(W.H[g, z, h], R.ps[g, 6 + z, 0:64], W.pc[g, z, ch:ch + 1], W.HP[g, z, h],
                                                      ALU.mult, ALU.add)
                    up.then_inc(s["h_out"], 1)
                for z in range(2):
                    ch = ORDER[z][n]
                    j, p = ch // 2, ch % 2
                    r = nat(p)
                    if ch < 4:
                        dve.wait_ge(s["y_done"], 2 * n + z + 1)
                        y = W.ytok[r:r + 64, j]
                        src = R.ps[r:r + 64, z, 0:P]
                        if first[ch] == (n, z):
                            dve.tensor_copy(y, src).then_inc(s["y_out"], 1)
                        else:
                            n0, z0 = first[ch]
                            dve.wait_ge(s["y_out"], 2 * (n0 - 4) + z0 + 1)
                            dve.tensor_tensor(y, y, src, ALU.add).then_inc(s["y_out"], 1)
            for _ in part:
                pass


READOUT_SEMS = ("o_chain", "var", "root_out", "normed", "turned", "out")


def readout_pe(pe, R, W, s):
    for j in range(2):
        mm = pe.transpose(R.ps[:, 0, j * P:(j + 1) * P], W.bonus[:, j, :], R.eye[:, :])
    mm.then_inc(s["turned"], 1)
    yield
    pe.wait_ge(s["normed"], 1)
    for j in range(2):
        mm = pe.transpose(R.ps[:, 1, j * P:(j + 1) * P], W.ytok[:, j, :], R.eye[:, :])
    mm.then_inc(s["turned"], 1)
    yield


def readout_act(act, R, W, s):
    act.wait_ge(s["var"], 1)
    act.activation(W.st[:, 1, :], W.st[:, 1, :], ACT.Sqrt).then_inc(s["root_out"], 1)


def readout_dve(dve, R, W, s, pair):
    y4 = W.ytok.rearrange("p j (h n) -> p (j h) n", n=64)
    sq = W.yt[:, :].rearrange("p (g n) -> p g n", n=64)
    st = lambda n: W.st[:, n, :]
    wide = lambda ap: ap.unsqueeze(2).broadcast_to([P, 4, 64])
    step = Steps(dve, s["o_chain"])
    step(dve.tensor_reduce(st(0), y4, AX_X, ALU.add))
    step.wait()
    step(dve.tensor_scalar(st(0), st(0), 1.0 / HEAD, None, ALU.mult))
    step.wait()
    step(dve.tensor_tensor(y4, y4, wide(st(0)), ALU.subtract))
    yield
    step.wait()
    step(dve.tensor_tensor(sq, y4, y4, ALU.mult))
    step.wait()
    step(dve.tensor_reduce(st(1), sq, AX_X, ALU.add))
    step.wait()
    dve.tensor_scalar(st(1), st(1), 1.0 / HEAD, GN_EPS, ALU.mult, ALU.add).then_inc(s["var"], 1)
    yield
    dve.wait_ge(s["root_out"], 1)
    step(dve.reciprocal(st(2), st(1)))
    step.wait()
    dve.tensor_tensor(y4, y4, wide(st(2)), ALU.mult).then_inc(s["normed"], 1)
    yield
    y = W.yt[:, :]
    dve.wait_ge(s["turned"], 2)
    step(dve.tensor_scalar(y, R.ps[:, 1, 0:NX], W.ln[:, 0:1], W.ln[:, 1:2], ALU.mult, ALU.add))
    step.wait()
    step(dve.tensor_tensor(y, y, R.ps[:, 0, 0:NX], ALU.add))
    step.wait()
    dve.tensor_tensor(W.u_pairs[:, ds(pair, 1), :].rearrange("p a n -> p (a n)"), y, W.gate, ALU.mult).then_inc(s["out"], 1)
    yield



def hyena_layer(nc, R, I):
    with ExitStack() as c:
        def sb(name, *shape):
            return c.enter_context(nc.sbuf_tensor(name, [P, *shape], F32))

        W = Named()
        W.Kf = sb("filter_spectrum", 4, E)
        W.dft = sb("dft", 2, 4 * P)
        W.idft = sb("idft", 4, NX)
        W.hv = sb("hyena_vec", 5, 3 * KE)
        hyena_filters(nc, R, W, I)
        modulate(nc, R, R.mods[:, 1], R.vec[:, 4, KD:2 * KD], NX)
        W.proj = sb("hyena_proj", 4 * KE, NX)
        hyena_project(nc, R, W, I)
        hyena_convolve(nc, R, W)
        dense(nc, R, I["w_out1"], KD, KE, NX, lambda k: W.proj[:, k, :], lambda m: R.h[:, ds(m, 1), 0:NX].rearrange("p a n -> p (a n)"))
    add_back(nc, R, R.h, R.mods[:, 1], R.vec[:, 5, KD:2 * KD], NX)


def hyena_filters(nc, R, W, I):
    with ExitStack() as c:
        def sb(name, *shape):
            return c.enter_context(nc.sbuf_tensor(name, [P, *shape], F32))

        f1, f23, fb = sb("f_w1", 64), sb("f_w23", 2, 64), sb("f_vec", 4)
        zt, hid, arg, rnd = sb("z_t", NX), sb("hid", NX), sb("arg", NX), sb("rnd", NX)
        w4 = sb("f_w4", 2, E)
        sd = sb("sum_diff", 2, 2, E)
        win = sb("window", 2, E)
        with stage(nc, "loaded", "summed", "layer", "chain", "sine", "filt", "filt_out") as (block, s):
            loads = [(f1[0:33, :], I["f_w1"]), (f23[0:64, :, :], I["f_w23"]), (fb[0:64, :], I["f_vec"]), (zt[0:33, :], I["z_t"]),
                     (w4[0:64, :, :], I["f_w4"]), (win[:, :, :], I["window"]), (W.dft[:, :, :], I["dft"]),
                     (W.idft[:, :, :], I["idft"]), (W.hv[:, :, :], I["hyena_vec"])]

            @block.sync
            def _(sp):
                for dst, src in loads:
                    sp.dma_start(dst, src).then_inc(s["loaded"], 16)

            @block.tensor
            def _(pe):
                pe.wait_ge(s["loaded"], 16 * len(loads))
                for n in range(3):
                    if n:
                        pe.wait_ge(s["sine"], n)
                    w, x = (f1[0:33, :], zt[0:33, :]) if n == 0 else (f23[0:64, n - 1, :], hid[0:64, :])
                    pe.matmul(R.ps[0:64, 0, 0:NX], w, x, start=True, stop=True).then_inc(s["layer"], 1)
                pe.wait_ge(s["sine"], 3)
                pe.wait_ge(s["summed"], 3)
                for n in range(16):
                    t, q, ch = n // 8, n // 4 % 2, n % 4
                    if n >= 7:
                        pe.wait_ge(s["filt_out"], n - 6)
                    pe.matmul(R.ps[:, 1 + n % 7, :], hid[0:64, t * P:(t + 1) * P], w4[0:64, q, ch * 512:(ch + 1) * 512],
                              start=True, stop=True).then_inc(s["filt"], 1)

            @block.scalar
            def _(act):
                for n in range(3):
                    act.wait_ge(s["chain"], 6 * n + 6)
                    act.activation(hid[0:64, :], arg[0:64, :], ACT.Sin).then_inc(s["sine"], 1)

            @block.vector
            def _(dve):
                dve.wait_ge(s["loaded"], 16 * len(loads))
                step = Steps(dve, s["chain"])
                for n in range(3):
                    dve.wait_ge(s["layer"], n + 1)
                    a, r = arg[0:64, :], rnd[0:64, :]
                    step(dve.tensor_scalar(a, R.ps[0:64, 0, 0:NX], fb[0:64, n:n + 1], fb[0:64, 3:4], ALU.add, ALU.mult))
                    step.wait()
                    step(dve.tensor_scalar(r, a, 1 / (2 * math.pi), BIG, ALU.mult, ALU.add))
                    step.wait()
                    step(dve.tensor_scalar(r, r, -BIG, None, ALU.add))
                    step.wait()
                    step(dve.scalar_tensor_tensor(a, r, -6.28125, a, ALU.mult, ALU.add))
                    step.wait()
                    step(dve.scalar_tensor_tensor(a, r, -(2 * math.pi - 6.28125), a, ALU.mult, ALU.add))
                    step.wait()
                    step(dve.tensor_scalar(a, a, 3.1415925, -3.1415925, ALU.min, ALU.max))
                    if n == 0:
                        tmp = sd[0:64, 0, 0, :]
                        dve.tensor_tensor(tmp, w4[0:64, 0, :], w4[0:64, 1, :], ALU.subtract).then_inc(s["summed"], 1)
                        dve.wait_ge(s["summed"], 1)
                        dve.tensor_tensor(w4[0:64, 0, :], w4[0:64, 0, :], w4[0:64, 1, :], ALU.add).then_inc(s["summed"], 1)
                        dve.wait_ge(s["summed"], 2)
                        dve.tensor_copy(w4[0:64, 1, :], tmp).then_inc(s["summed"], 1)
                        dve.wait_ge(s["summed"], 3)
                for n in range(16):
                    t, q, ch = n // 8, n // 4 % 2, n % 4
                    cols = slice(ch * 512, (ch + 1) * 512)
                    dve.wait_ge(s["filt"], n + 1)
                    dve.tensor_tensor(sd[:, q, t, cols], R.ps[:, 1 + n % 7, :], win[:, t, cols], ALU.mult).then_inc(s["filt_out"], 1)

        with stage(nc, "done", "copied") as (block, s):
            @block.tensor
            def _(pe):
                for n in range(16):
                    f, ch = n // 4, n % 4
                    if n >= 8:
                        pe.wait_ge(s["copied"], n - 7)
                    for t in range(2):
                        mm = pe.matmul(R.ps[:, n % 8, :], W.dft[:, t, f * P:(f + 1) * P], sd[:, f // 2, t, ch * 512:(ch + 1) * 512],
                                       start=(t == 0), stop=(t == 1))
                    mm.then_inc(s["done"], 1)

            @block.vector
            def _(dve):
                for n in range(16):
                    f, ch = n // 4, n % 4
                    dve.wait_ge(s["done"], n + 1)
                    dve.tensor_copy(W.Kf[:, f, ch * 512:(ch + 1) * 512], R.ps[:, n % 8, :]).then_inc(s["copied"], 1)


def hyena_project(nc, R, W, I):
    conv = 3 * KE

    def evac(dve, s, n, m, bank):
        out = W.proj[:, ds(m, 1), :].rearrange("p a n -> p (a n)")
        vec = lambda q: W.hv[:, q, ds(m, 1)]
        dve.tensor_scalar(out, R.ps[:, bank, 0:NX], vec(1), vec(3), ALU.mult, ALU.add).then_inc(s["part"], 1)
        dve.wait_ge(s["part"], n * 2 + 1)
        dve.scalar_tensor_tensor(out[:, 1:], R.ps[:, bank, 0:NX - 1], vec(0), out[:, 1:], ALU.mult, ALU.add).then_inc(s["part"], 1)
        dve.wait_ge(s["part"], n * 2 + 2)
        return dve.scalar_tensor_tensor(out[:, :-1], R.ps[:, bank, 1:NX], vec(2), out[:, :-1], ALU.mult, ALU.add)

    dense(nc, R, I["w_in1"], conv, KD, NX, lambda k: R.h[:, k, 0:NX], None, evac)
    dense(nc, R, I["w_gate1"], KE, KD, NX, lambda k: R.h[:, k, 0:NX], lambda m: W.proj[:, ds(m + conv, 1), :].rearrange("p a n -> p (a n)"))


def hyena_convolve(nc, R, W):
    x0, u, v, gate = (W.proj[:, q * KE:(q + 1) * KE, :] for q in range(4))
    utok = R.sq[:, :, :].rearrange("p a b -> p (a b)").rearrange("p (t n) -> p t n", n=E)
    with stage(nc, "u", "gate", "turned", "utok", "spec", "spec_out", "chain", "mult", "conv", "out") as (block, s):
        @block.scalar
        def _(act):
            for q in range(4):
                act.activation(gate[:, 4 * q:4 * q + 4, :], gate[:, 4 * q:4 * q + 4, :], ACT.Silu).then_inc(s["gate"], 1)
            for n in range(8):
                t, q = n % 2, n // 2
                act.wait_ge(s["turned"], n + 1)
                act.activation(utok[:, t, q * 512:(q + 1) * 512], R.ps[:, n % 2, :], ACT.Copy).then_inc(s["utok"], 1)
            for q in range(4):
                for f in range(4):
                    act.wait_ge(s["spec"], 4 * q + f + 1)
                    if q >= 2:
                        act.wait_ge(s["mult"], q - 1)
                    act.activation(R.h[:, 4 * (q % 2) + f, :], R.ps[:, 2 + f, :], ACT.Copy).then_inc(s["spec_out"], 1)

        @block.tensor
        def _(pe):
            for n in range(8):
                t, q = n % 2, n // 2
                pe.wait_ge(s["u"], q + 1)
                if n >= 2:
                    pe.wait_ge(s["utok"], n - 1)
                for b in range(4):
                    mm = pe.transpose(R.ps[:, n % 2, b * P:(b + 1) * P], u[:, 4 * q + b, t * P:(t + 1) * P], R.eye[:, :])
                mm.then_inc(s["turned"], 1)
            for q in range(4):
                pe.wait_ge(s["utok"], 2 * q + 2)
                for f in range(4):
                    if q:
                        pe.wait_ge(s["spec_out"], 4 * (q - 1) + f + 1)
                    for t in range(2):
                        mm = pe.matmul(R.ps[:, 2 + f, :], W.dft[:, t, f * P:(f + 1) * P], utok[:, t, q * 512:(q + 1) * 512],
                                       start=(t == 0), stop=(t == 1))
                    mm.then_inc(s["spec"], 1)
            for m in range(KE):
                pe.wait_ge(s["mult"], m // 4 + 1)
                if m >= 2:
                    pe.wait_ge(s["out"], 3 * (m - 2) + 1)
                for f in range(4):
                    mm = pe.matmul(R.ps[:, 6 + m % 2, 0:NX], W.Kf[:, f, m * P:(m + 1) * P], W.idft[:, f, :],
                                   start=(f == 0), stop=(f == 3))
                mm.then_inc(s["conv"], 1)

        @block.vector
        def _(dve):
            step = Steps(dve, s["chain"])
            for q in range(4):
                a = slice(4 * q, 4 * q + 4)
                dve.tensor_tensor(u[:, a, :], v[:, a, :], u[:, a, :], ALU.mult).then_inc(s["u"], 1)
            dve.wait_ge(s["u"], 4)
            ta = v[:, 0:4, :].rearrange("p (a b) n -> p a (b n)", a=2)
            tb = v[:, 4:8, :].rearrange("p (a b) n -> p a (b n)", a=2)
            for q in range(4):
                dve.wait_ge(s["spec_out"], 4 * q + 4)
                cols = slice(q * 512, (q + 1) * 512)
                b = 4 * (q % 2)
                ure, uim = R.h[:, b:b + 2, :], R.h[:, b + 2:b + 4, :]
                kre, kim = W.Kf[:, 0:2, cols], W.Kf[:, 2:4, cols]
                step(dve.tensor_tensor(ta, uim, kim, ALU.mult))
                step(dve.tensor_tensor(tb, ure, kim, ALU.mult))
                step.wait()
                step(dve.tensor_tensor(kim, uim, kre, ALU.mult))
                step.wait()
                step(dve.tensor_tensor(kre, ure, kre, ALU.mult))
                step.wait()
                step(dve.tensor_tensor(kre, kre, ta, ALU.subtract))
                step(dve.tensor_tensor(kim, kim, tb, ALU.add))
                step.wait()
                dve.sem_inc(s["mult"], 1)
            dve.wait_ge(s["gate"], 4)
            for m in range(KE):
                dve.wait_ge(s["conv"], m + 1)
                n = 3 * m
                dve.scalar_tensor_tensor(u[:, m, :], u[:, m, :], W.hv[:, 4, m:m + 1], R.ps[:, 6 + m % 2, 0:NX], ALU.mult, ALU.add).then_inc(s["out"], 1)
                dve.wait_ge(s["out"], n + 1)
                dve.tensor_tensor(x0[:, m, :], x0[:, m, :], u[:, m, :], ALU.mult).then_inc(s["out"], 1)
                dve.wait_ge(s["out"], n + 2)
                dve.tensor_tensor(x0[:, m, :], x0[:, m, :], gate[:, m, :], ALU.mult).then_inc(s["out"], 1)



RK, DK, RQ, DQ, RG, DG, MU, MG = range(8)


def second_layer(nc, R, I, l):
    last = l == 1
    NQ = NX if last else NT
    w_feature, w_token, w_merge, w_last = ((I["w_feature0"], I["w_token0"], I["w_merge0"], I["w_last0"]),
                                           (I["w_feature1"], I["w_token1"], I["w_merge1"], I["w_last1"]))[l]
    modulate(nc, R, R.mods[:, 2 + l], R.vec[:, 6, l * 8:l * 8 + 8], NT)
    with ExitStack() as c:
        def sb(name, *shape):
            return c.enter_context(nc.sbuf_tensor(f"{name}_{l}", [P, *shape], F32))

        W = Named()
        W.F, W.D, W.sc = sb("features", 32, NT), sb("decays", HEADS, 4, NX), sb("scalars", 64)
        W.rv, W.dv, W.mv = sb("ret_v", 4, BW), sb("diff_v", 4, BW), sb("mlp_v", 4, BW)
        dense(nc, R, w_feature[0:8], 8, KD, NT, lambda k: R.h[:, k, :], lambda m: W.F[:, ds(m, 1), :].rearrange("p a n -> p (a n)"))
        dense(nc, R, w_feature[8:32], 24, KD, NQ, lambda k: R.h[:, k, 0:NQ], lambda m: W.F[:, ds(m + 8, 1), 0:NQ].rearrange("p a n -> p (a n)"))
        rhs = lambda k, t: R.h[:, k, t * P:(t + 1) * P]
        token_major(nc, R, w_token[0], rhs, 4, lambda t: W.rv[:, t, :])
        token_major(nc, R, w_token[1], rhs, 4, lambda t: W.dv[:, t, :])
        token_major(nc, R, w_token[2], rhs, NQ // P, lambda t: W.mv[:, t, :])
        decays(nc, R, W, I, l)
        rotate(nc, R, W, I)
        retention(nc, R, W, NQ)
        diff_attention(nc, R, W, NQ)
        lam_init = 0.8 - 0.6 * math.exp(-0.3 * l)
        head_norms(nc, R, W, RQ, RG, NQ, 1.0)
        head_norms(nc, R, W, DQ, DG, NQ, 1.0 - lam_init)
        mlp(nc, R, W, I, l, NQ)
        merge(nc, R, W, w_merge, NQ)
        dense(nc, R, w_last, KD, KD, NQ, lambda k: R.sq[:, k, 0:NQ], lambda m: R.h[:, ds(m, 1), 0:NQ].rearrange("p a n -> p (a n)"))
    add_back(nc, R, R.h, R.mods[:, 2 + l], R.vec[:, 7, l * 8:l * 8 + 8], NQ)


def decays(nc, R, W, I, l):
    lam_init = 0.8 - 0.6 * math.exp(-0.3 * l)
    sc = W.sc
    logit, lg, ax, y, sd, s1, s2, poly = (sc[:, 8 * n:8 * n + 8] for n in range(8))
    W.lam = sc[:, 56:57]
    lamk = R.ring[:, 0, 0:256].rearrange("p (a b n) -> p a b n", a=2, b=2)
    prod = R.ring[:, 1, 0:128].rearrange("p (b n) -> p b n", b=2)
    lsum = R.ring[:, 2, 0:2]
    dist = R.ring[:, 4:6, :].rearrange("p a (b n) -> p (a b) n", n=2 * NX)
    same = R.ring[:, 6, 0:2 * NX]
    with stage(nc, "loaded", "chain", "act") as (block, s):
        loads = [(logit, I["ret_logit"][l]), (lamk, I["lambdas"][l]), (dist, I["distances"]), (same, I["same"])]

        @block.sync
        def _(sp):
            for dst, src in loads:
                sp.dma_start(dst, src).then_inc(s["loaded"], 16)

        @block.vector
        def _(dve):
            dve.wait_ge(s["loaded"], 16 * len(loads))
            step = Steps(dve, s["chain"])

            def seq(ins):
                step(ins)
                step.wait()

            seq(dve.tensor_scalar(ax, logit, -1.0, None, ALU.mult))
            seq(dve.tensor_tensor(ax, ax, logit, ALU.max))
            seq(dve.tensor_tensor(prod, lamk[:, 0], lamk[:, 1], ALU.mult))
            seq(dve.tensor_reduce(lsum, prod, AX_X, ALU.add))
            dve.wait_ge(s["act"], 2)
            seq(dve.tensor_scalar(sd, y, 2.0, None, ALU.add))
            seq(dve.reciprocal(sd, sd))
            seq(dve.tensor_tensor(s1, y, sd, ALU.mult))
            seq(dve.tensor_tensor(s2, s1, s1, ALU.mult))
            seq(dve.tensor_scalar(poly, s2, 1 / 19, 1 / 17, ALU.mult, ALU.add))
            for q in (15, 13, 11, 9, 7, 5, 3, 1):
                seq(dve.tensor_tensor(poly, poly, s2, ALU.mult))
                seq(dve.tensor_scalar(poly, poly, 1 / q, None, ALU.add))
            seq(dve.tensor_tensor(poly, poly, s1, ALU.mult))
            seq(dve.tensor_scalar(lg, logit, 0.0, None, ALU.min))
            seq(dve.scalar_tensor_tensor(lg, poly, -2.0, lg, ALU.mult, ALU.add))
            seq(dve.tensor_tensor(W.lam, lsum[:, 0:1], lsum[:, 1:2], ALU.subtract))
            seq(dve.tensor_scalar(W.lam, W.lam, lam_init, None, ALU.add))
            for h in range(HEADS):
                d = W.D[:, h, 0:2, :].rearrange("p a n -> p (a n)")
                seq(dve.tensor_scalar(d, dist[:, 0, :], lg[:, h:h + 1], None, ALU.mult))
                seq(dve.scalar_tensor_tensor(d, dist[:, 1, :], lg[:, 4 + h:5 + h], d, ALU.mult, ALU.add))
            dve.sem_inc(s["chain"], 1)
            step.n += 1
            self_n = step.n
            for h in range(HEADS):
                dve.wait_ge(s["act"], 3 + h)
                d = W.D[:, h, 0:2, :].rearrange("p a n -> p (a n)")
                step(dve.tensor_tensor(d, d, same, ALU.add))
            for h in range(HEADS):
                dve.wait_ge(s["act"], 2 + HEADS + 2 * h + 2)
                d = W.D[:, h, 2:4, :].rearrange("p a n -> p (a n)")
                other = R.sq[:, h, :]
                step(dve.tensor_tensor(d, d, other, ALU.add))

        ready = 4 + 4 + 1 + 16 + 3 + 2 + 2 * HEADS + 1

        @block.scalar
        def _(act):
            act.wait_ge(s["chain"], 4)
            act.activation(y, ax, ACT.Exp, scale=-1.0).then_inc(s["act"], 1)
            act.activation(lsum, lsum, ACT.Exp).then_inc(s["act"], 1)
            act.wait_ge(s["chain"], ready)
            for h in range(HEADS):
                d = W.D[:, h, 0:2, :].rearrange("p a n -> p (a n)")
                act.activation(d, d, ACT.Exp).then_inc(s["act"], 1)
            for h in range(HEADS):
                d = W.D[:, h, 2:4, :].rearrange("p a n -> p (a n)")
                act.activation(d, dist[:, 2, :], ACT.Exp, scale=lg[:, h:h + 1]).then_inc(s["act"], 1)
                act.activation(R.sq[:, h, :], dist[:, 3, :], ACT.Exp, scale=lg[:, 4 + h:5 + h]).then_inc(s["act"], 1)


def rotate(nc, R, W, I):
    tab = R.ring[:, 0, :].rearrange("p (q n) -> p q n", n=NX)
    swap = R.ring[:, 1, 0:2 * P].rearrange("p (q n) -> p q n", n=P)
    with stage(nc, "loaded", "swapped", "term", "scaled", "out") as (block, s):
        @block.sync
        def _(sp):
            sp.dma_start(tab, I["rope"]).then_inc(s["loaded"], 16)
            sp.dma_start(swap, I["swaps"]).then_inc(s["loaded"], 16)

        order = [(g, h) for h in range(4) for g in (RK, RQ, DK, DQ)]

        @block.tensor
        def _(pe):
            pe.wait_ge(s["loaded"], 32)
            for n, (g, h) in enumerate(order):
                if n >= 4:
                    pe.wait_ge(s["term"], n - 3)
                pe.matmul(R.ps[:, n % 4, 0:NX], swap[:, int(g in (DK, DQ)), :], W.F[:, 4 * g + h, 0:NX], start=True, stop=True).then_inc(s["swapped"], 1)

        @block.vector
        def _(dve):
            dve.wait_ge(s["loaded"], 32)
            for n, (g, h) in enumerate(order):
                q = 2 * int(g in (DK, DQ))
                x, t = W.F[:, 4 * g + h, 0:NX], R.sq[:, n % 4, 0:NX]
                dve.wait_ge(s["swapped"], n + 1)
                if n >= 4:
                    dve.wait_ge(s["out"], n - 3)
                dve.tensor_tensor(t, R.ps[:, n % 4, 0:NX], tab[:, q + 1, :], ALU.mult).then_inc(s["term"], 1)
                dve.tensor_tensor(x, x, tab[:, q, :], ALU.mult).then_inc(s["scaled"], 1)
                dve.wait_ge(s["term"], n + 1)
                dve.wait_ge(s["scaled"], n + 1)
                dve.tensor_tensor(x, x, t, ALU.add).then_inc(s["out"], 1)


def retention(nc, R, W, NQ):
    jobs = [(h, side) for h in range(HEADS) for side in range(NQ // NX)]
    with stage(nc, "scores", "decayed", "out", "out_copied") as (block, s):
        score = R.ring[:, 0:2, :].rearrange("p a (b n) -> p (a b) n", n=NX)

        def keys(side):
            return [(0, 0), (1, 1), (2, 2), (3, 3)] if side == 0 else [(2, 0), (3, 1)]

        first = [0]
        for _, side in jobs:
            first.append(first[-1] + len(keys(side)))

        @block.tensor
        def _(pe):
            for n, (h, side) in enumerate(jobs):
                q = W.F[:, 4 * RQ + h, side * NX:(side + 1) * NX]
                for i, (kt, _) in enumerate(keys(side)):
                    if n:
                        pe.wait_ge(s["decayed"], first[n])
                    pe.matmul(R.ps[:, i, 0:NX], W.F[:, 4 * RK + h, kt * P:(kt + 1) * P], q, start=True, stop=True).then_inc(s["scores"], 1)
                if n >= 2:
                    pe.wait_ge(s["out_copied"], n - 1)
                for i, (kt, _) in enumerate(keys(side)):
                    pe.wait_ge(s["decayed"], first[n] + i + 1)
                    mm = pe.matmul(R.ps[:, 4 + n % 2, 0:NX], W.rv[:, kt, h * P:(h + 1) * P], score[:, 4 * (n % 2) + i, :],
                                   start=(i == 0), stop=(i == len(keys(side)) - 1))
                mm.then_inc(s["out"], 1)

        @block.vector
        def _(dve):
            for n, (h, side) in enumerate(jobs):
                for i, (_, dt) in enumerate(keys(side)):
                    dve.wait_ge(s["scores"], first[n] + i + 1)
                    if n >= 2:
                        dve.wait_ge(s["out"], n - 1)
                    dve.scalar_tensor_tensor(score[:, 4 * (n % 2) + i, :], R.ps[:, i, 0:NX], float(P) ** -0.5,
                                             W.D[:, h, dt, :], ALU.mult, ALU.mult).then_inc(s["decayed"], 1)

        @block.scalar
        def _(act):
            for n, (h, side) in enumerate(jobs):
                act.wait_ge(s["out"], n + 1)
                act.activation(W.F[:, 4 * RQ + h, side * NX:(side + 1) * NX], R.ps[:, 4 + n % 2, 0:NX], ACT.Copy).then_inc(s["out_copied"], 1)


def diff_attention(nc, R, W, NQ):
    jobs = [(h, t) for h in range(HEADS) for t in range(NQ // P)]
    J, DEPTH = len(jobs), 3
    prob = R.ring[:, 0:6, :].rearrange("p (b a) (c n) -> p b (a c) n", b=3, n=512)
    st = R.rstd
    with stage(nc, "scores", "top", "expd", "chain", "mixed", "turned", "turned_out", "out", "out_copied") as (block, s):
        def span(n):
            return (0, 4) if jobs[n][1] < 2 else (2, 4)

        @block.tensor
        def _(pe):
            def scores(n):
                h, t = jobs[n]
                a, b = span(n)
                if n >= DEPTH:
                    pe.wait_ge(s["expd"], 2 * (n - DEPTH) + 2)
                for m in range(2):
                    r = slice(64 * m, 64 * m + 64)
                    mm = pe.matmul(R.ps[:, 2 * (n % DEPTH) + m, 0:(b - a) * P], W.F[r, 4 * DQ + h, t * P:(t + 1) * P],
                                   W.F[r, 4 * DK + h, a * P:b * P], start=True, stop=True)
                mm.then_inc(s["scores"], 1)

            def turn(n):
                a, b = span(n)
                pe.wait_ge(s["mixed"], n + 1)
                if n:
                    pe.wait_ge(s["turned_out"], n)
                for i in range(b - a):
                    mm = pe.transpose(R.ps[:, 6, i * P:(i + 1) * P], prob[:, n % DEPTH, 2, i * P:(i + 1) * P], R.eye[:, :])
                mm.then_inc(s["turned"], 1)

            def values(n):
                h, t = jobs[n]
                a, b = span(n)
                pe.wait_ge(s["turned_out"], n + 1)
                if n >= 2:
                    pe.wait_ge(s["out_copied"], n - 1)
                o = 256 * (n % 2)
                for i in range(b - a):
                    mm = pe.matmul(R.ps[:, 7, o:o + P], W.dv[:, a + i, h * P:(h + 1) * P], prob[:, n % DEPTH, 3, i * P:(i + 1) * P],
                                   start=(i == 0), stop=(i == b - a - 1))
                mm.then_inc(s["out"], 1)

            scores(0)
            scores(1)
            for n in range(J):
                if n + 2 < J:
                    scores(n + 2)
                if n:
                    values(n - 1)
                turn(n)
            values(J - 1)

        @block.scalar
        def _(act):
            def exps(n):
                a, b = span(n)
                act.wait_ge(s["top"], n + 1)
                if n >= DEPTH:
                    act.wait_ge(s["mixed"], n - DEPTH + 1)
                c = 16 * (n % DEPTH)
                for m in range(2):
                    act.activation(prob[:, n % DEPTH, m, 0:(b - a) * P], R.ps[:, 2 * (n % DEPTH) + m, 0:(b - a) * P], ACT.Exp,
                                   bias=st[:, c + m:c + m + 1], scale=0.125, accum_out=st[:, c + 2 + m:c + 3 + m]).then_inc(s["expd"], 1)

            def out_copy(n):
                h, t = jobs[n]
                act.wait_ge(s["out"], n + 1)
                o = 256 * (n % 2)
                act.activation(W.F[:, 4 * DQ + h, t * P:(t + 1) * P], R.ps[:, 7, o:o + P], ACT.Copy).then_inc(s["out_copied"], 1)

            exps(0)
            exps(1)
            for n in range(J):
                a, b = span(n)
                if n:
                    out_copy(n - 1)
                act.wait_ge(s["turned"], n + 1)
                if n >= DEPTH:
                    act.wait_ge(s["out"], n - DEPTH + 1)
                act.activation(prob[:, n % DEPTH, 3, 0:(b - a) * P], R.ps[:, 6, 0:(b - a) * P], ACT.Copy).then_inc(s["turned_out"], 1)
                if n + 2 < J:
                    exps(n + 2)
            out_copy(J - 1)

        @block.vector
        def _(dve):
            step = Steps(dve, s["chain"])

            def tops(n):
                a, b = span(n)
                c = 16 * (n % DEPTH)
                dve.wait_ge(s["scores"], n + 1)
                bank = 2 * (n % DEPTH)
                step(dve.tensor_reduce(st[:, c:c + 2], R.ps[:, bank:bank + 2, 0:(b - a) * P], AX_X, ALU.max))
                step.wait()
                dve.tensor_scalar(st[:, c:c + 2], st[:, c:c + 2], -0.125, None, ALU.mult).then_inc(s["top"], 1)

            tops(0)
            tops(1)
            for n in range(J):
                a, b = span(n)
                c = 16 * (n % DEPTH)
                p = prob[:, n % DEPTH]
                w = (b - a) * P
                dve.wait_ge(s["expd"], 2 * n + 2)
                step(dve.reciprocal(st[:, c + 4:c + 6], st[:, c + 2:c + 4]))
                step.wait()
                step(dve.scalar_tensor_tensor(st[:, c + 6:c + 7], st[:, c + 5:c + 6], -1.0, W.lam, ALU.mult, ALU.mult))
                step.wait()
                step(dve.tensor_scalar(p[:, 1, 0:w], p[:, 1, 0:w], st[:, c + 6:c + 7], None, ALU.mult))
                step.wait()
                if n >= DEPTH:
                    dve.wait_ge(s["turned"], n - DEPTH + 1)
                dve.scalar_tensor_tensor(p[:, 2, 0:w], p[:, 0, 0:w], st[:, c + 4:c + 5], p[:, 1, 0:w],
                                         ALU.mult, ALU.add).then_inc(s["mixed"], 1)
                if n + 2 < J:
                    tops(n + 2)


def head_norms(nc, R, W, O, G, NQ, factor):
    with stage(nc, "squared", "summed", "log", "rstd", "gate", "scaled", "out") as (block, s):
        @block.tensor
        def _(pe):
            for h in range(HEADS):
                pe.wait_ge(s["squared"], h + 1)
                pe.matmul(R.ps[:, h, 0:NQ], R.ones[:, :], R.sq[:, h, 0:NQ], start=True, stop=True).then_inc(s["summed"], 1)

        @block.scalar
        def _(act):
            for h in range(HEADS):
                act.activation(R.sq[:, h, 0:NQ], W.F[:, 4 * O + h, 0:NQ], ACT.Square).then_inc(s["squared"], 1)
            for h in range(HEADS):
                act.activation(W.F[:, 4 * G + h, 0:NQ], W.F[:, 4 * G + h, 0:NQ], ACT.Silu).then_inc(s["gate"], 1)
            for h in range(HEADS):
                act.wait_ge(s["summed"], h + 1)
                act.activation(R.sq[:, h, 0:NQ], R.ps[:, h, 0:NQ], ACT.Ln, bias=R.eps[:, 0:1], scale=1.0 / P).then_inc(s["log"], 1)
            for h in range(HEADS):
                act.wait_ge(s["log"], h + 1)
                act.activation(R.sq[:, h, 0:NQ], R.sq[:, h, 0:NQ], ACT.Exp, scale=-0.5).then_inc(s["rstd"], 1)

        @block.vector
        def _(dve):
            for h in range(HEADS):
                dve.wait_ge(s["rstd"], h + 1)
                o, g = W.F[:, 4 * O + h, 0:NQ], W.F[:, 4 * G + h, 0:NQ]
                dve.tensor_tensor(o, o, R.sq[:, h, 0:NQ], ALU.mult).then_inc(s["scaled"], 1)
                dve.wait_ge(s["scaled"], h + 1)
                dve.wait_ge(s["gate"], h + 1)
                dve.scalar_tensor_tensor(g, o, factor, g, ALU.mult, ALU.mult).then_inc(s["out"], 1)


def mlp(nc, R, W, I, l, NQ):
    wst = R.ring[:, 0, 0:4 * P].rearrange("p (g n) -> p g n", n=P)
    bs = R.ring[:, 1, 0:4 * P].rearrange("p (g n) -> p g n", n=P)
    stats, mv = R.ring[:, 2, 0:24].rearrange("p (t n) -> p t n", n=6), R.ring[:, 3, 0:8].rearrange("p (t n) -> p t n", n=2)
    T = NQ // P
    with stage(nc, "loaded", "chain", "var", "root", "normed", "mixed", "gate", "out") as (block, s):
        @block.sync
        def _(sp):
            sp.dma_start(wst, I["mlp_w"][l]).then_inc(s["loaded"], 16)
            sp.dma_start(bs, I["mlp_b"][l]).then_inc(s["loaded"], 16)

        @block.scalar
        def _(act):
            for g in range(4):
                act.activation(W.F[:, 4 * MG + g, 0:NQ], W.F[:, 4 * MG + g, 0:NQ], ACT.Silu).then_inc(s["gate"], 1)
            act.wait_ge(s["var"], 1)
            act.activation(mv[:, 0:T, 1], mv[:, 0:T, 1], ACT.Sqrt, bias=R.eps[:, 0:1]).then_inc(s["root"], 1)

        @block.tensor
        def _(pe):
            pe.wait_ge(s["loaded"], 32)
            pe.wait_ge(s["normed"], T)
            for g in range(4):
                for t in range(T):
                    mm = pe.matmul(R.ps[:, g, t * P:(t + 1) * P], W.mv[:, t, g * P:(g + 1) * P], wst[:, g, :], start=True, stop=True)
                mm.then_inc(s["mixed"], 1)

        @block.vector
        def _(dve):
            step = Steps(dve, s["chain"])
            for t in range(T):
                step(dve.bn_stats(stats[:, t, :], W.mv[:, t, :]))
            for t in range(T):
                step.wait(t + 1)
                step(dve.bn_aggr(mv[:, t, :], stats[:, t, :]))
            step.wait()
            dve.sem_inc(s["var"], 1)
            dve.wait_ge(s["root"], 1)
            step(dve.reciprocal(mv[:, 0:T, 1], mv[:, 0:T, 1]))
            step.wait()
            for t in range(T):
                dve.tensor_scalar(W.mv[:, t, :], W.mv[:, t, :], mv[:, t, 0:1], mv[:, t, 1:2], ALU.subtract, ALU.mult).then_inc(s["normed"], 1)
            dve.wait_ge(s["loaded"], 32)
            for g in range(4):
                dve.wait_ge(s["mixed"], g + 1)
                u, gate = W.F[:, 4 * MU + g, 0:NQ], W.F[:, 4 * MG + g, 0:NQ]
                x = R.sq[:, g, 0:NQ]
                step(dve.tensor_tensor(x.rearrange("p (t n) -> p t n", n=P), R.ps[:, g, 0:NQ].rearrange("p (t n) -> p t n", n=P),
                                       bs[:, g, :].unsqueeze(1).broadcast_to([P, T, P]), ALU.add))
                step.wait()
                step(dve.tensor_tensor(x, x, u, ALU.mult))
                step.wait()
                dve.wait_ge(s["gate"], g + 1)
                dve.tensor_tensor(gate, x, gate, ALU.mult).then_inc(s["out"], 1)


def merge(nc, R, W, w, NQ):
    names = [f"w_loaded{b}" for b in range(3)]
    with stage(nc, *names, "logit_done", "branch_done", "sig", "mult", "out") as (block, s):
        loaded = [s[n] for n in names]
        wt = R.ring[:, 0:6, :].rearrange("p (b a) n -> p b (a n)", b=3)[:, :, 0:12 * P].rearrange("p b (k n) -> p b k n", n=P)
        sig = R.ring[:, 6:8, :].rearrange("p a (b n) -> p (a b) n", n=512)

        @block.sync
        def _(sp):
            with sp.Fori(0, KD) as m:
                for b in range(3):
                    sp.wait_ge(s["branch_done"], m * 3 + (b + 1))
                    sp.dma_start(wt[:, b].rearrange("p k n -> p (k n)"), w[ds(m, 1), b].rearrange("a p n -> p (a n)")).then_inc(loaded[b], 16)

        @block.tensor
        def _(pe):
            pe.sem_inc(s["branch_done"], 3)
            with pe.Fori(0, KD) as m:
                for b, G in enumerate((RG, MG, DG)):
                    pe.wait_ge(loaded[b], m * 16 + 16)
                    pe.wait_ge(s["sig"], m * 3 + (b + 1))
                    for k in range(KD):
                        mm = pe.matmul(R.ps[:, 2 * b, 0:NQ], wt[:, b, k, :], R.h[:, k, 0:NQ], start=(k == 0), stop=(k == KD - 1))
                    mm.then_inc(s["logit_done"], 1)
                    pe.wait_ge(s["mult"], m * 3 + (b + 1))
                    for k in range(KB):
                        mm = pe.matmul(R.ps[:, 2 * b + 1, 0:NQ], wt[:, b, KD + k, :], W.F[:, 4 * G + k, 0:NQ], start=(k == 0), stop=(k == KB - 1))
                    mm.then_inc(s["branch_done"], 1)

        @block.scalar
        def _(act):
            act.sem_inc(s["sig"], 3)
            with act.Fori(0, KD) as m:
                for b in range(3):
                    act.wait_ge(s["logit_done"], m * 3 + (b + 1))
                    act.wait_ge(s["mult"], m * 3 + (b + 1))
                    act.activation(sig[:, b, 0:NQ], R.ps[:, 2 * b, 0:NQ], ACT.Sigmoid).then_inc(s["sig"], 1)

        @block.vector
        def _(dve):
            dve.sem_inc(s["mult"], 3)
            with dve.Fori(0, KD) as m:
                y = R.sq[:, ds(m, 1), 0:NQ].rearrange("p a n -> p (a n)")
                for b in range(3):
                    dve.wait_ge(s["sig"], m * 3 + (b + 4))
                    dve.wait_ge(s["branch_done"], m * 3 + (b + 4))
                    if b == 0:
                        dve.tensor_tensor(y, R.ps[:, 1, 0:NQ], sig[:, 0, 0:NQ], ALU.mult).then_inc(s["mult"], 1)
                    else:
                        t = sig[:, b, 0:NQ]
                        dve.tensor_tensor(t, R.ps[:, 2 * b + 1, 0:NQ], t, ALU.mult).then_inc(s["out"], 1)
                        dve.wait_ge(s["out"], m * 2 + b)
                        if b == 1:
                            dve.wait_ge(s["mult"], m * 3 + 4)
                        else:
                            dve.wait_ge(s["mult"], m * 3 + 5)
                        dve.tensor_tensor(y, y, t, ALU.add).then_inc(s["mult"], 1)


def program(nc, I, out):
    with ExitStack() as c:
        R = Named()
        alloc(nc, R, lambda name, *shape: c.enter_context(nc.sbuf_tensor(name, [P, *shape], F32)), c)
        setup(nc, R, I)
        modulate(nc, R, R.mods[:, 0], R.vec[:, 4, 0:KD], NT)
        rwkv_layer(nc, R, I)
        hyena_layer(nc, R, I)
        with stage(nc, "loaded") as (block, s):
            @block.sync
            def _(sp):
                sp.dma_start(R.x[:, :, NX:], I["ctx_t"]).then_inc(s["loaded"], 16)
                sp.wait_ge(s["loaded"], 16)
        for l in range(2):
            second_layer(nc, R, I, l)
        with stage(nc, "stored") as (block, s):
            @block.sync
            def _(sp):
                sp.dma_start(out, R.x[:, :, 0:NX]).then_inc(s["stored"], 16)
                sp.wait_ge(s["stored"], 16)



def tiles(w):
    K, N = w.shape
    return np.ascontiguousarray(w.reshape(K // P, P, N // P, P).transpose(2, 1, 0, 3)).reshape(N // P, P, K)


def columns(v):
    return v.reshape(-1, P).T


def layouts(a):
    f = np.float32
    out = {}
    out["x_t"] = np.concatenate([a["x"][0].T, a["ctx"][0].T], 1).reshape(KD, P, NT).transpose(1, 0, 2)
    out["eye"] = np.eye(P, dtype=f)
    half = np.arange(P) // 64
    out["head_ones"] = (half[:, None] == half[None, :]).astype(f)
    out["cond"] = np.stack([a["c"][0], a["c_ctx"], a["c_2"][0], a["c_ctx_2"]], 1).reshape(KD, P, 4).transpose(1, 0, 2)
    vec = np.zeros((P, 9, 24), f)
    for n, b in enumerate((a["ada_b"][0], a["ada_b"][1], a["b_mod_2"][0], a["b_mod_2"][1])):
        vec[:, n, :] = columns(b)
    for l in range(2):
        vec[:, 4, l * 8:l * 8 + 8] = columns(a["norm_pre"][l])
        vec[:, 5, l * 8:l * 8 + 8] = columns(a["norm_post"][l])
        vec[:, 6, l * 8:l * 8 + 8] = columns(a["g_pre_2"][l])
        vec[:, 7, l * 8:l * 8 + 8] = columns(a["g_post_2"][l])
    out["vectors"] = vec
    mods = np.concatenate([a["ada_w"], a["w_mod_2"]]).reshape(4, 4, 2, P, 6, 512)
    out["w_mods"] = mods.transpose(0, 4, 1, 3, 2, 5).reshape(24, 4, P, D)
    out["w_out0"] = tiles(a["w_out"][0])
    out["mu"] = a["l0_mu"].reshape(6, KD, P).transpose(2, 0, 1)
    w = a["l0_w_in"]
    out["w_rkvg"] = np.concatenate([tiles(w[:, g * E:(g + 1) * E]) for g in (1, 2, 0, 3)], 2)
    out["w_low"] = np.concatenate(list(tiles(w[:, 4 * E:])), 1)
    pv = np.zeros((KE, P, 10), f)
    for n, v in enumerate((a["l0_w0"][0], a["l0_w0"][1], a["l0_a0"][0], a["l0_a0"][1], a["l0_k_k"], a["l0_k_a"],
                           a["l0_r_k"].reshape(-1), a["l0_ln_w"], a["l0_ln_b"])):
        pv[:, :, n] = v.reshape(KE, P)
    out["pair_vec"] = pv
    out["lora"] = np.stack([a["l0_w2"].reshape(P, KE, P), a["l0_a2"].reshape(P, KE, P)], 1).transpose(2, 0, 1, 3)
    t = np.arange(64)
    strict = [t[:, None] < t[None, :], t[:, None] > t[None, :]]
    incl = [t[:, None] <= t[None, :], t[:, None] >= t[None, :]]
    masks = np.zeros((P, 2, 2, P), f)
    for z in range(2):
        for p in range(2):
            for rows in (0, 64):
                masks[rows:rows + 64, z, p, oth(p):oth(p) + 64] = strict[z]
                masks[rows:rows + 64, z, p, nat(p):nat(p) + 64] = incl[z]
    out["masks"] = masks
    lm = np.zeros((P, LEVELS, 2, P), f)
    q = np.arange(P)
    for l in range(LEVELS):
        b = q >> l
        low = (b[:, None] == b[None, :] + 1) & (b[:, None] % 2 == 1)
        lm[:, l, 0, :] = low
        lm[:, l, 1, :] = low.T
    out["level_masks"] = lm
    out["ctx_t"] = a["ctx_2"][0].T.reshape(KD, P, NX).transpose(1, 0, 2)
    w = a["l1_w_in"]
    out["w_in1"], out["w_gate1"], out["w_out1"] = tiles(w[:, :3 * E]), tiles(w[:, 3 * E:]), tiles(a["w_out"][1])
    hv = np.zeros((P, 5, 3 * KE), f)
    for q in range(3):
        hv[:, q, :] = columns(a["l1_conv_w"][q])
    hv[:, 3, :] = columns(a["l1_conv_b"])
    hv[:, 4, 0:KE] = columns(a["l1_filter_bias"])
    out["hyena_vec"] = hv
    out["f_w1"] = a["l1_f_w1"]
    out["f_w23"] = np.stack([a["l1_f_w2"], a["l1_f_w3"]], 1)
    out["f_vec"] = np.stack([a["l1_f_b1"], a["l1_f_b2"], a["l1_f_b3"], a["l1_sin_freq"]], 1)
    out["f_w4"] = a["l1_f_w4"].reshape(64, 2, E)
    out.update(hyena_constants())
    for l in range(2):
        w = a["w_in_2"][l]
        col = lambda n: w[:, n * BW:(n + 1) * BW]
        out[f"w_feature{l}"] = np.concatenate([tiles(col(n)) for n in (0, 2, 4, 6, 5, 7, 8, 10)])
        out[f"w_token{l}"] = np.stack([col(n).reshape(KD, P, BW).transpose(1, 0, 2) for n in (1, 3, 9)])
        logits = tiles(w[:, 11 * BW:]).reshape(3, KD, P, D).transpose(1, 0, 2, 3)
        branch = np.stack([tiles(a["w_branch_out_2"][l, b]) for b in range(3)], 1)
        out[f"w_merge{l}"] = np.concatenate([logits, branch], 3)
        out[f"w_last{l}"] = tiles(a["w_out_2"][l])
    every = lambda v: np.broadcast_to(v[:, None], (v.shape[0], P) + v.shape[1:])
    out["ret_logit"] = every(a["ret_decay_logit_2"].reshape(2, 8))
    out["lambdas"] = every(np.stack([a["diff_lambda_q_2"], a["diff_lambda_k_2"]], 1))
    out["mlp_w"] = a["mlp_w_s_2"].transpose(0, 3, 1, 2)
    out["mlp_b"] = every(a["mlp_b_s_2"])
    out.update(attention_constants())
    return {k: np.ascontiguousarray(v) for k, v in out.items()}


def hyena_constants():
    f = np.float32
    L, bands = NX, 16
    t = np.linspace(0.0, 1.0, L, dtype=f)[:, None]
    freqs = np.linspace(1e-4, bands - 1, bands, dtype=f)[None, :]
    ang = f(2.0 * math.pi / L) * np.arange(L, dtype=f)[:, None] * freqs
    z = np.concatenate([t, np.cos(ang), -np.sin(ang)], 1)
    deltas = np.abs(np.linspace(math.log(1e-2) / 1.5, math.log(1e-2) / 0.3, E, dtype=f))
    window = np.exp(-t * deltas).astype(f)
    w = math.pi * (2 * np.arange(L) + 1) / (2 * L)
    ph = np.arange(L)[:, None] * w[None, :]
    dft = np.concatenate([np.cos(ph), -np.sin(ph)], 1)
    idft = np.concatenate([np.cos(ph).T, -np.sin(ph).T], 0) / L
    return {"z_t": z.T.astype(f), "window": window.reshape(2, P, E).transpose(1, 0, 2),
            "dft": dft.reshape(2, P, 4 * P).transpose(1, 0, 2).astype(f),
            "idft": idft.reshape(4, P, NX).transpose(1, 0, 2).astype(f)}


def attention_constants():
    f = np.float32
    j = np.arange(NX).reshape(2, P).T[:, :, None]
    i = np.arange(NX)[None, None, :]
    dist = np.stack([np.maximum(i - j, 0), np.maximum(j - i, 0), NX + i - j, NX - i + j], 1).astype(f)
    out = {"distances": dist.reshape(P, 4, 2 * NX), "same": (i == j).astype(f).reshape(P, 2 * NX)}
    row, col = np.arange(NX) // GRID, np.arange(NX) % GRID
    rope = []
    for dim in (128, 64):
        n = dim // 4
        inv = (f(10000.0) ** (-np.arange(n, dtype=f) / n)).astype(f)
        ang = np.concatenate([row.astype(f)[:, None] * inv, col.astype(f)[:, None] * inv], 1).T
        q = np.arange(P)
        sign = np.where(q % dim < dim // 2, -1.0, 1.0).astype(f)
        rope += [np.cos(ang)[q % (dim // 2)], np.sin(ang)[q % (dim // 2)] * sign[:, None]]
    out["rope"] = np.stack(rope, 1).astype(f)
    q = np.arange(P)
    out["swaps"] = np.stack([(q[:, None] == (q[None, :] ^ s)) for s in (64, 32)], 1).astype(f)
    return out


def kernel(**inputs):
    import concourse.bacc as bacc
    from concourse.bass_utils import run_bass_kernel_spmd

    nc = bacc.Bacc("TRN2", target_bir_lowering=False, num_devices=1)
    arrays = {f"in_{k}": v for k, v in layouts({k: np.asarray(v) for k, v in inputs.items()}).items()}
    aps = {k[3:]: nc.dram_tensor(k, v.shape, mybir.dt.from_np(v.dtype), kind="ExternalInput").ap() for k, v in arrays.items()}
    out = nc.dram_tensor("out_x", (P, KD, NX), F32, kind="ExternalOutput").ap()
    program(nc, aps, out)
    got = run_bass_kernel_spmd(nc, [arrays], core_ids=[0]).results[0]["out_x"]
    return np.ascontiguousarray(got.transpose(2, 1, 0)).reshape(1, NX, D)
```

```python
import math
from contextlib import ExitStack, contextmanager

import numpy as np

import concourse.bass as bass
from concourse import mybir

F32 = mybir.dt.float32
ALU = mybir.AluOpType
ACT = mybir.ActivationFunctionType
AX_X = mybir.AxisListType.X
ds = bass.ds

P = 128
D = 1024
KD = D // P
E = 2048
KE = E // P
NX = 256
NT = 2 * NX
GRID = 64
HEAD = 64
C = 64
NCH = NT // C
LORA = 64
LEVELS = 6
EPS = 1e-6
GN_EPS = 64e-5
DECAY = math.exp(-0.5)
BW = 512
KB = BW // P
HEADS = 4
V_W0, V_A0, V_KK, V_KA, V_RK, V_LNW, V_LNB = 0, 2, 4, 5, 6, 7, 8
RING = 8
BIG = float(2 ** 23) * 1.5


class Named:
    pass


class Steps:

    def __init__(self, eng, sem):
        self.eng, self.sem, self.n = eng, sem, 0

    def __call__(self, ins):
        self.n += 1
        ins.then_inc(self.sem, 1)
        return self.n

    def wait(self, n=None):
        self.eng.wait_ge(self.sem, self.n if n is None else n)


STAGES = [0]


@contextmanager
def stage(nc, *names):
    with ExitStack() as c:
        STAGES[0] += 1
        sems = [c.enter_context(nc.semaphore(f"{n}_{STAGES[0]}")) for n in names]
        with nc.Block() as block:
            yield block, dict(zip(names, sems))
        numbers = sorted(sem.num for sem in sems)
        first = numbers[0]
        for n, number in enumerate(numbers):
            if n + 1 == len(numbers) or numbers[n + 1] != number + 1:
                nc.gpsimd.sem_clear(range(first, number + 1))
                first = numbers[n + 1] if n + 1 < len(numbers) else 0
        nc.all_engine_barrier()


@contextmanager
def repeat(eng, n):
    if n == 1:
        yield 0
    else:
        with eng.Fori(0, n) as i:
            yield i


def dense(nc, R, w, M, K, N, rhs, out, evac=None):
    S = max(1, K // 8)
    width = K * P // S
    G = min(M, RING // S)
    assert M % G == 0 and (G % 4 == 0)
    with stage(nc, *[f"w_loaded{s}" for s in range(RING)], "tile_done", "bank_free", "part") as (block, s):
        loaded = [s[f"w_loaded{j}"] for j in range(RING)]

        @block.sync
        def _(sp):
            with repeat(sp, M // G) as i:
                for j in range(G):
                    sp.wait_ge(s["tile_done"], i * G + (j + 1))
                    for h in range(S):
                        src = w[ds(i * G + j, 1), :, h * width:(h + 1) * width].rearrange("a p n -> p (a n)")
                        sp.dma_start(R.ring[:, j * S + h, 0:width], src).then_inc(loaded[j * S + h], 16)

        @block.tensor
        def _(pe):
            pe.sem_inc(s["tile_done"], G)
            with repeat(pe, M // G) as i:
                for j in range(G):
                    pe.wait_ge(s["bank_free"], i * G + (j + 1))
                    for k in range(K):
                        if k % 8 == 0:
                            pe.wait_ge(loaded[j * S + k // 8], i * 16 + 16)
                        a = (k % 8) * P
                        mm = pe.matmul(R.ps[:, j % 4, 0:N], R.ring[:, j * S + k // 8, a:a + P], rhs(k),
                                       start=(k == 0), stop=(k == K - 1))
                    mm.then_inc(s["tile_done"], 1)

        @block.vector
        def _(dve):
            dve.sem_inc(s["bank_free"], 4)
            with repeat(dve, M // G) as i:
                for j in range(G):
                    dve.wait_ge(s["tile_done"], i * G + (G + j + 1))
                    if evac is None:
                        last = dve.tensor_copy(out(i * G + j), R.ps[:, j % 4, 0:N])
                    else:
                        last = evac(dve, s, i * G + j, i * G + j, j % 4)
                    last.then_inc(s["bank_free"], 1)


RMS_SEMS = ("squared", "summed", "log", "rstd")


def rms_act(act, R, s, src, N):
    for t in range(KD):
        act.activation(R.sq[:, t, 0:N], src(t), ACT.Square).then_inc(s["squared"], 1)
    rstd = R.rstd[:, 0:N]
    act.wait_ge(s["summed"], 1)
    act.activation(rstd, R.ps[:, 0, 0:N], ACT.Ln, bias=R.eps[:, 0:1], scale=1.0 / D).then_inc(s["log"], 1)
    act.wait_ge(s["log"], 1)
    act.activation(rstd, rstd, ACT.Exp, scale=-0.5).then_inc(s["rstd"], 1)


def rms_pe(pe, R, s, N):
    for t in range(KD):
        pe.wait_ge(s["squared"], t + 1)
        mm = pe.matmul(R.ps[:, 0, 0:N], R.ones[:, :], R.sq[:, t, 0:N], start=(t == 0), stop=(t == KD - 1))
    mm.then_inc(s["summed"], 1)


def modulate(nc, R, mods, g, N):
    with stage(nc, *RMS_SEMS, "gain", "scaled", "shifted") as (block, s):
        @block.tensor
        def _(pe):
            rms_pe(pe, R, s, N)

        @block.vector
        def _(dve):
            for c in range(N // NX):
                dve.scalar_tensor_tensor(R.gain[:, c, :], mods[:, c, KD:2 * KD], 1.0, g, ALU.add, ALU.mult).then_inc(s["gain"], 1)
            dve.wait_ge(s["rstd"], 1)
            for k in range(KD):
                dve.tensor_tensor(R.h[:, k, 0:N], R.x[:, k, 0:N], R.rstd[:, 0:N], ALU.mult).then_inc(s["scaled"], 1)

        @block.scalar
        def _(act):
            rms_act(act, R, s, lambda t: R.x[:, t, 0:N], N)
            act.wait_ge(s["gain"], N // NX)
            for k in range(KD):
                act.wait_ge(s["scaled"], k + 1)
                for c in range(N // NX):
                    cols = slice(c * NX, (c + 1) * NX)
                    act.activation(R.h[:, k, cols], R.h[:, k, cols], ACT.Identity, bias=mods[:, c, k:k + 1],
                                   scale=R.gain[:, c, k:k + 1]).then_inc(s["shifted"], 1)


def add_back(nc, R, o, mods, g, N):
    with stage(nc, *RMS_SEMS, "gain", "scaled", "added") as (block, s):
        @block.tensor
        def _(pe):
            rms_pe(pe, R, s, N)

        @block.scalar
        def _(act):
            rms_act(act, R, s, lambda t: o[:, t, 0:N], N)

        @block.vector
        def _(dve):
            for c in range(N // NX):
                dve.tensor_tensor(R.gain[:, c, :], mods[:, c, 2 * KD:3 * KD], g, ALU.mult).then_inc(s["gain"], 1)
            dve.wait_ge(s["rstd"], 1)
            for k in range(KD):
                dve.tensor_tensor(o[:, k, 0:N], o[:, k, 0:N], R.rstd[:, 0:N], ALU.mult).then_inc(s["scaled"], 1)
            dve.wait_ge(s["gain"], N // NX)
            for k in range(KD):
                dve.wait_ge(s["scaled"], k + 1)
                for c in range(N // NX):
                    cols = slice(c * NX, (c + 1) * NX)
                    dve.scalar_tensor_tensor(R.x[:, k, cols], o[:, k, cols], R.gain[:, c, k:k + 1],
                                             R.x[:, k, cols], ALU.mult, ALU.add).then_inc(s["added"], 1)


def alloc(nc, R, sb, c):
    R.x = sb("x", KD, NT)
    R.h = sb("h", KD, NT)
    R.sq = sb("sq", KD, NT)
    R.ring = sb("ring", RING, D)
    R.eye, R.ones, R.head_ones = sb("eye", P), sb("ones", P), sb("head_ones", P)
    R.cond, R.vec = sb("cond", KD, 4), sb("vec", 9, 24)
    R.mods = sb("mods", 4, 2, 24)
    R.rstd, R.gain, R.eps = sb("rstd", NT), sb("gain", 2, KD), sb("eps", 1)
    R.ps = c.enter_context(nc.psum_tensor("ps", [P, 8, 512], F32))


def setup(nc, R, I):
    with stage(nc, "loaded", "silu", "ones") as (block, s):
        loads = [(R.x[:, :, :], I["x_t"]), (R.eye[:, :], I["eye"]), (R.head_ones[:, :], I["head_ones"]),
                 (R.cond[:, :, :], I["cond"]), (R.vec[:, :, :], I["vectors"])]

        @block.sync
        def _(sp):
            for dst, src in loads:
                sp.dma_start(dst, src).then_inc(s["loaded"], 16)

        @block.gpsimd
        def _(pool):
            pool.memset(R.ones[:, :], 1.0).then_inc(s["ones"], 1)
            pool.memset(R.eps[:, :], EPS).then_inc(s["ones"], 1)

        @block.scalar
        def _(act):
            act.wait_ge(s["loaded"], 16 * len(loads))
            act.activation(R.cond[:, :, :], R.cond[:, :, :], ACT.Silu).then_inc(s["silu"], 1)
    modulations(nc, R, I)


def modulations(nc, R, I):
    CH = 4
    CHUNKS = 4 * 3 * D // 512
    steps = CHUNKS // CH
    with ExitStack() as c:
        rows = c.enter_context(nc.sbuf_tensor("mod_rows", [4, CHUNKS, 512], F32))
        with stage(nc, *[f"w_loaded{n}" for n in range(RING)], "used", "copied", "turned", "bias") as (block, s):
            loaded = [s[f"w_loaded{n}"] for n in range(RING)]

            @block.sync
            def _(sp):
                with sp.Fori(0, steps) as i:
                    for q in range(CH):
                        for piece in range(4):
                            slot = 4 * (q % 2) + piece
                            sp.wait_ge(s["used"], i * (4 * CH) + (4 * q + piece + 1))
                            sp.dma_start(R.ring[:, slot, :], I["w_mods"][ds(i * CH + q, 1), piece].rearrange("a p n -> p (a n)")).then_inc(loaded[slot], 16)

            @block.tensor
            def _(pe):
                pe.sem_inc(s["used"], RING)
                with pe.Fori(0, steps) as i:
                    for q in range(CH):
                        pe.wait_ge(s["copied"], i * CH + (q + 1))
                        for k in range(KD):
                            slot = 4 * (q % 2) + k // 2
                            if k % 2 == 0:
                                pe.wait_ge(loaded[slot], i * (16 * CH // 2) + 16 * (q // 2 + 1))
                            mm = pe.matmul(R.ps[0:4, q, :], R.cond[:, k, :], R.ring[:, slot, (k % 2) * 512:(k % 2) * 512 + 512],
                                           start=(k == 0), stop=(k == KD - 1))
                            if k % 2:
                                mm.then_inc(s["used"], 1)
                for m in range(CHUNKS):
                    pe.wait_ge(s["copied"], CH + m + 1)
                    for t in range(4):
                        n = 4 * m + t
                        mm = pe.transpose(R.ps[:, 6, 4 * n:4 * n + 4], rows[:, m, t * P:(t + 1) * P], R.eye[0:4, 0:4])
                mm.then_inc(s["turned"], 1)

            @block.vector
            def _(dve):
                dve.sem_inc(s["copied"], CH)
                with dve.Fori(0, steps) as i:
                    for q in range(CH):
                        dve.wait_ge(s["used"], i * (4 * CH) + (RING + 4 * q + 4))
                        dve.tensor_copy(rows[:, ds(i * CH + q, 1), :].rearrange("p a n -> p (a n)"), R.ps[0:4, q, :]).then_inc(s["copied"], 1)
                dve.wait_ge(s["turned"], 1)
                turned = R.ps[:, 6, 0:4 * 4 * 24].rearrange("p (n m c) -> p n m c", m=24, c=4)
                for n in range(4):
                    for c in range(2):
                        dve.tensor_tensor(R.mods[:, n, c, :], turned[:, n, :, 2 * (n // 2) + c], R.vec[:, n, 0:24], ALU.add).then_inc(s["bias"], 1)



def shift_mix(nc, R, W, I):
    with stage(nc, "diff", "loaded") as (block, s):
        @block.sync
        def _(sp):
            sp.dma_start(W.mu[:, :, :], I["mu"]).then_inc(s["loaded"], 16)
            sp.wait_ge(s["loaded"], 16)

        @block.vector
        def _(dve):
            step = Steps(dve, s["diff"])
            h, d = R.h, R.sq
            for q in range(4):
                ks = slice(2 * q, 2 * q + 2)
                for k in (2 * q, 2 * q + 1):
                    hg = h[:, k, 0:NX].rearrange("p (r c) -> p r c", c=GRID)
                    dg = d[:, k, 0:NX].rearrange("p (r c) -> p r c", c=GRID)
                    if q == 0:
                        step(dve.tensor_tensor(dg[:, :, 1:], hg[:, :, :-1], hg[:, :, 1:], ALU.subtract))
                        step(dve.tensor_scalar(dg[:, :, 0:1], hg[:, :, 0:1], -1.0, None, ALU.mult))
                    elif q == 1:
                        step(dve.tensor_tensor(dg[:, :, :-1], hg[:, :, 1:], hg[:, :, :-1], ALU.subtract))
                        step(dve.tensor_scalar(dg[:, :, GRID - 1:], hg[:, :, GRID - 1:], -1.0, None, ALU.mult))
                    elif q == 2:
                        step(dve.tensor_tensor(dg[:, 1:, :], hg[:, :-1, :], hg[:, 1:, :], ALU.subtract))
                        step(dve.tensor_scalar(dg[:, 0:1, :], hg[:, 0:1, :], -1.0, None, ALU.mult))
                    else:
                        step(dve.tensor_tensor(dg[:, :-1, :], hg[:, 1:, :], hg[:, :-1, :], ALU.subtract))
                        step(dve.tensor_scalar(dg[:, 3:4, :], hg[:, 3:4, :], -1.0, None, ALU.mult))
            a, b = h[:, 0:4, NX:], d[:, 0:4, NX:]
            step(dve.tensor_tensor(b[:, :, 1:], a[:, :, :-1], a[:, :, 1:], ALU.subtract))
            step(dve.tensor_scalar(b[:, :, 0:1], a[:, :, 0:1], -1.0, None, ALU.mult))
            a, b = h[:, 4:8, NX:], d[:, 4:8, NX:]
            step(dve.tensor_tensor(b[:, :, :-1], a[:, :, 1:], a[:, :, :-1], ALU.subtract))
            step(dve.tensor_scalar(b[:, :, NX - 1:], a[:, :, NX - 1:], -1.0, None, ALU.mult))

    def mixes(groups):
        with stage(nc, "mixed") as (block, s):
            @block.vector
            def _(dve):
                for g, dst, N in groups:
                    for k in range(KD):
                        dve.scalar_tensor_tensor(dst[:, k, 0:N], R.sq[:, k, 0:N], W.mu[:, g, k:k + 1],
                                                 R.h[:, k, 0:N], ALU.mult, ALU.add).then_inc(s["mixed"], 1)

    mixes([(4, W.mix_k, NT), (5, W.mix_v, NT)])
    with stage(nc, "loaded", "done", "tanh") as (block, s):
        wt = R.ring[:, 0:2, :].rearrange("p a (k n) -> p a k n", n=P)

        @block.sync
        def _(sp):
            sp.dma_start(R.ring[:, 0:2, :], I["w_low"]).then_inc(s["loaded"], 16)

        @block.tensor
        def _(pe):
            pe.wait_ge(s["loaded"], 16)
            for n, mix in enumerate((W.mix_k, W.mix_v)):
                for k in range(KD):
                    mm = pe.matmul(R.ps[:, n, :], wt[:, n, k, :], mix[:, k, :], start=(k == 0), stop=(k == KD - 1))
                mm.then_inc(s["done"], 1)

        @block.scalar
        def _(act):
            act.wait_ge(s["done"], 1)
            act.activation(W.low[:, 0, :], R.ps[:, 0, :], ACT.Tanh).then_inc(s["tanh"], 1)
            act.wait_ge(s["done"], 2)
            act.activation(W.low[:, 1, :], R.ps[:, 1, :], ACT.Copy).then_inc(s["tanh"], 1)

    mixes([(0, W.mix_r, NX), (1, W.mix_k, NT), (2, W.mix_v, NT), (3, W.mix_g, NX)])


def nat(p):
    return 64 * p


def oth(p):
    return 64 - 64 * p


def rwkv_layer(nc, R, I):
    with ExitStack() as c:
        def sb(name, *shape):
            return c.enter_context(nc.sbuf_tensor(name, [P, *shape], F32))

        W = Named()
        W.mix_r, W.mix_g = sb("mix_r", KD, NX), sb("mix_g", KD, NX)
        W.mix_k, W.mix_v = sb("mix_k", KD, NT), sb("mix_v", KD, NT)
        W.low = sb("low", 2, NT)
        with ExitStack() as c2:
            W.mu = c2.enter_context(nc.sbuf_tensor("mu", [P, 6, KD], F32))
            shift_mix(nc, R, W, I)
        W.u_pairs = R.ring[:, 4:8, :].rearrange("p a (k n) -> p (a k) n", n=NX)
        hv = R.h[:, :, :]
        W.r, W.gate = hv[:, 0, 0:NX], hv[:, 0, NX:]
        W.k, W.kk, W.ksum, W.k1, W.k2, W.cum = (hv[:, n, :] for n in range(1, 7))
        W.sg = hv[:, 7, :]
        sv = R.sq[:, :, :]
        W.t0, W.t1, W.t2 = sv[:, 0, :], sv[:, 1, :], sv[:, 2, :]
        W.vtok = sv[:, 3, :].rearrange("p (j n) -> p j n", n=P)
        W.ytok = sv[:, 4, 0:NX].rearrange("p (j n) -> p j n", n=P)
        W.bonus = sv[:, 4, NX:].rearrange("p (j n) -> p j n", n=P)
        W.rate = sv[:, 5, :]
        W.tmp = sv[:, 6, :]
        W.tmp2 = sv[:, 7, :]
        W.pv = sb("pair_vec", 10)
        W.lw = sb("lora_w", 2, P)
        W.masks = R.x[:, 6:8, NX:].rearrange("p z (q n) -> p z q n", n=P)
        W.lmask = R.x[:, 0:LEVELS, NX:].rearrange("p l (z n) -> p l z n", n=P)
        W.bk = sb("bk", NCH, P)
        W.ar = sb("ar", 2, NCH, P)
        W.A = sb("A", 2, 2, 4, 2, P)
        W.BK = sb("BK", 2, 2, 4, 2, HEAD)
        W.U = sb("U", 2, 2, 4, P)
        W.Tm = sb("Tm", 2, 4, P)
        W.Y = sb("Y", 2, 4, P)
        W.At = sb("At", 2, 2, 4, P)
        W.vnext, W.gnext, W.ln, W.yt = sb("v_next", NT), sb("gate_next", NX), sb("ln", 2), sb("y_turned", NX)
        W.pc, W.pc_next = sb("pc", 2, NCH), sb("pc_next", NCH)
        W.H = sb("H", 2, 2, HEAD)
        W.HP = sb("HP", 2, 2, HEAD)
        W.Xs = sb("Xs", 2, 2, HEAD)
        W.Z = sb("Z", 2, 2, HEAD)
        W.st = sb("stats", 4, 4)
        W.coef = sb("coef", 4)
        W.reset = R.rstd
        with stage(nc, "loaded", "zeroed") as (block, s):
            @block.sync
            def _(sp):
                sp.dma_start(W.masks[:, :, :, :], I["masks"]).then_inc(s["loaded"], 16)
                sp.dma_start(W.lmask[:, :, :, :], I["level_masks"]).then_inc(s["loaded"], 16)
                sp.wait_ge(s["loaded"], 32)

            @block.vector
            def _(dve):
                step = Steps(dve, s["zeroed"])
                step(dve.memset(W.reset[:, :], 1.0))
                step.wait()
                step(dve.memset(W.reset[:, :].rearrange("p (c t) -> p c t", t=C)[:, :, 0:1], 0.0))
                step(dve.memset(W.At[:, :, :, :, :], 0.0))
                step(dve.memset(W.ar[:, :, :, :], 0.0))
        rwkv_project_first(nc, R, W, I)
        rwkv_pair(nc, R, W, I, 0, True, False)
        with nc.Fori(1, KE - 1) as pair:
            rwkv_pair(nc, R, W, I, pair, False, False)
        rwkv_pair(nc, R, W, I, KE - 1, False, True)
        with stage(nc, *READOUT_SEMS) as (block, s):
            @block.tensor
            def _(pe):
                for _ in readout_pe(pe, R, W, s):
                    pass

            @block.scalar
            def _(act):
                readout_act(act, R, W, s)

            @block.vector
            def _(dve):
                for _ in readout_dve(dve, R, W, s, KE - 1):
                    pass

        uT = W.mix_k[:, :, :].rearrange("p a (b n) -> p (a b) n", n=NX)
        with stage(nc, "moved") as (block, s):
            @block.vector
            def _(dve):
                dve.tensor_copy(uT, W.u_pairs).then_inc(s["moved"], 1)
        dense(nc, R, I["w_out0"], KD, KE, NX, lambda k: uT[:, k, :], lambda m: R.h[:, ds(m, 1), 0:NX].rearrange("p a n -> p (a n)"))
    add_back(nc, R, R.h, R.mods[:, 0], R.vec[:, 5, 0:KD], NX)


def at(i, n):
    return ds(i + n, 1)


def rwkv_pair(nc, R, W, I, pair, first, last):
    keys_and_inverses(nc, R, W, I, pair, first, last)
    rwkv_scan(nc, R, W, I, pair, last)



PROJECT_SEMS = ("k_done", "r_done", "g_done", "v_done", "k_out", "vt_out", "r_out", "g_out",
                "sq_out", "norm_sum", "norm_out", "root", "p_chain")


def project_pe(pe, R, W, s):
    wt = R.ring[:, 0:4, :].rearrange("p a (k n) -> p a k n", n=P)
    for k in range(KD):
        mm = pe.matmul(R.ps[:, 2, :], wt[:, 0, k, :], W.mix_k[:, k, :], start=(k == 0), stop=(k == KD - 1))
        if k == KD - 1:
            mm.then_inc(s["k_done"], 1)
        yield
    for j in range(4):
        if j == 3:
            pe.wait_ge(s["sq_out"], 1)
            pe.matmul(R.ps[:, 2, :], R.head_ones[:, :], W.tmp, start=True, stop=True).then_inc(s["norm_sum"], 1)
            yield
        for k in range(KD):
            mm = pe.matmul(R.ps[:, 3, j * P:(j + 1) * P], W.mix_v[:, k, j * P:(j + 1) * P], wt[:, 1, k, :],
                           start=(k == 0), stop=(k == KD - 1))
            if k == KD - 1 and j == 3:
                mm.then_inc(s["v_done"], 1)
            if k % 4 == 3:
                yield
    for n, mix, bank, done, read in ((2, W.mix_r, 3, "r_done", "vt_out"), (3, W.mix_g, 2, "g_done", "norm_out")):
        pe.wait_ge(s[read], 1)
        for k in range(KD):
            mm = pe.matmul(R.ps[:, bank, 0:NX], wt[:, n, k, :], mix[:, k, :], start=(k == 0), stop=(k == KD - 1))
            if k == KD - 1:
                mm.then_inc(s[done], 1)
            if k in ((2, 5, 7) if n == 2 else (1, 3, 5, 7)):
                yield


def load_vectors(act, W, s, I, pair):
    act.dma_start(W.pv[:, :], I["pair_vec"][pair].rearrange("a p n -> p (a n)")).then_inc(s["v_loaded"], 16)
    act.dma_start(W.lw[:, :, :], I["lora"][pair].rearrange("a p z n -> p (a z) n")).then_inc(s["v_loaded"], 16)


def project_act(act, R, W, s):
    act.wait_ge(s["k_out"], 1)
    act.activation(W.tmp, W.k, ACT.Square, scale=W.pv[:, V_KK:V_KK + 1]).then_inc(s["sq_out"], 1)
    yield
    act.wait_ge(s["v_done"], 1)
    act.activation(W.vnext[:, :], R.ps[:, 3, :], ACT.Copy).then_inc(s["vt_out"], 1)
    act.wait_ge(s["norm_out"], 1)
    act.activation(W.tmp2, W.tmp2, ACT.Ln).then_inc(s["root"], 1)
    act.wait_ge(s["root"], 1)
    act.activation(W.tmp2, W.tmp2, ACT.Exp, scale=-0.5).then_inc(s["root"], 1)
    yield
    act.wait_ge(s["r_done"], 1)
    act.activation(W.r, R.ps[:, 3, 0:NX], ACT.Copy).then_inc(s["r_out"], 1)
    act.wait_ge(s["g_done"], 1)
    act.activation(W.gnext[:, :], R.ps[:, 2, 0:NX], ACT.Silu).then_inc(s["g_out"], 1)
    yield


def project_dve(dve, R, W, s):
    step = Steps(dve, s["p_chain"])
    dve.wait_ge(s["k_done"], 1)
    dve.tensor_copy(W.k, R.ps[:, 2, :]).then_inc(s["k_out"], 1)
    yield
    dve.wait_ge(s["k_out"], 1)
    step(dve.tensor_scalar(W.k1, W.k, W.pv[:, V_KA:V_KA + 1], None, ALU.mult))
    step(dve.tensor_scalar(W.kk, W.k, W.pv[:, V_KK:V_KK + 1], None, ALU.mult))
    yield
    step.wait()
    step(dve.tensor_tensor(W.k2, W.k, W.k1, ALU.subtract))
    dve.wait_ge(s["norm_sum"], 1)
    dve.tensor_scalar(W.tmp2, R.ps[:, 2, :], 1e-24, None, ALU.max).then_inc(s["norm_out"], 1)
    yield
    dve.wait_ge(s["root"], 2)
    step(dve.tensor_tensor(W.kk, W.kk, W.tmp2, ALU.mult))
    yield


def rwkv_project_first(nc, R, W, I):
    with stage(nc, "w_loaded", "v_loaded", *PROJECT_SEMS) as (block, s):
        @block.sync
        def _(sp):
            for n in range(4):
                sp.dma_start(R.ring[:, n, :], I["w_rkvg"][0, :, n * D:(n + 1) * D]).then_inc(s["w_loaded"], 16)

        @block.tensor
        def _(pe):
            pe.wait_ge(s["w_loaded"], 64)
            for _ in project_pe(pe, R, W, s):
                pass

        @block.scalar
        def _(act):
            load_vectors(act, W, s, I, ds(0, 1))
            act.wait_ge(s["v_loaded"], 32)
            for _ in project_act(act, R, W, s):
                pass

        @block.vector
        def _(dve):
            dve.wait_ge(s["v_loaded"], 32)
            for _ in project_dve(dve, R, W, s):
                pass

    with stage(nc, *DECAY_SEMS) as (block, s):
        @block.tensor
        def _(pe):
            low_pe(pe, R, W, s, 0, (6, 7))

        @block.scalar
        def _(act):
            for _ in decay_act(act, R, W, s, 0, (6, 7), W.pc_next[:, :]):
                pass

        @block.vector
        def _(dve):
            decay_dve(dve, R, W, s, 0, W.pc_next[:, :])


DECAY_SEMS = ("low_done", "sig", "exps_in", "exps", "c_chain")
DIRECTION_SEMS = ("packed", "d_chain", "a_done", "a_out", "bk_done", "bk_out", "at_out")


def low_pe(pe, R, W, s, z, banks):
    for n in range(2):
        pe.matmul(R.ps[:, banks[n], :], W.lw[z * 64:z * 64 + 64, n, :], W.low[z * 64:z * 64 + 64, n, :],
                  start=True, stop=True).then_inc(s["low_done"], 1)


def direction_pe(pe, R, W, s, z, banks):
    pe.wait_ge(s["packed"], 8)
    nb = len(banks)
    for g in range(4):
        h, jj = g // 2, g % 2
        if g >= nb:
            pe.wait_ge(s["a_out"], g - nb + 1)
        for q in range(4):
            c = 2 * (2 * jj + q // 2) + q % 2
            mm = pe.matmul(R.ps[:, banks[g % nb], q * P:(q + 1) * P], W.bk[h * 64:h * 64 + 64, c, :],
                           W.ar[h * 64:h * 64 + 64, z, c, :], start=True, stop=True)
        mm.then_inc(s["a_done"], 1)
        yield
    for h in range(2):
        pe.wait_ge(s["a_out"], 3 + h if nb == 2 else 1 + h)
        for c in range(NCH):
            mm = pe.transpose(R.ps[:, banks[h], c * 64:(c + 1) * 64], W.bk[h * 64:h * 64 + 64, c, :],
                              R.eye[h * 64:h * 64 + 64, h * 64:h * 64 + 64])
        mm.then_inc(s["bk_done"], 1)
        yield


def decay_act(act, R, W, s, z, banks, pc):
    act.wait_ge(s["low_done"], 1)
    act.activation(W.sg, R.ps[:, banks[0], :], ACT.Sigmoid, bias=W.pv[:, V_W0 + z:V_W0 + z + 1]).then_inc(s["sig"], 1)
    act.wait_ge(s["low_done"], 2)
    act.activation(W.rate, R.ps[:, banks[1], :], ACT.Sigmoid, bias=W.pv[:, V_A0 + z:V_A0 + z + 1]).then_inc(s["sig"], 1)
    yield
    act.wait_ge(s["exps_in"], 1)
    act.activation(W.t0, W.cum, ACT.Exp, scale=-DECAY).then_inc(s["exps"], 1)
    act.activation(W.t2, W.cum, ACT.Exp, scale=DECAY).then_inc(s["exps"], 1)
    yield
    act.activation(W.t1, W.t1, ACT.Exp, scale=-DECAY).then_inc(s["exps"], 1)
    act.activation(pc, pc, ACT.Exp, scale=-DECAY).then_inc(s["exps"], 1)
    yield


def direction_act(act, R, W, s, z, banks):
    for h in range(2):
        act.wait_ge(s["bk_done"], h + 1)
        act.activation(W.BK[:, z, h].rearrange("p j q n -> p (j q n)"), R.ps[:, banks[h], :], ACT.Copy).then_inc(s["bk_out"], 1)
    yield


def decay_dve(dve, R, W, s, z, pc):
    chunks = lambda ap: ap.rearrange("p (c t) -> p c t", t=C)
    step = Steps(dve, s["c_chain"])
    dve.wait_ge(s["sig"], 1)
    step(dve.tensor_tensor_scan(W.cum, W.reset[:, :], W.sg, 0.0, ALU.mult, ALU.add))
    step.wait()
    tot = chunks(W.cum)[:, :, C - 1:C]
    step(dve.tensor_copy(pc, tot.rearrange("p c o -> p (c o)")))
    if z == 0:
        dve.tensor_tensor(W.t1, W.cum, W.sg, ALU.subtract).then_inc(s["exps_in"], 1)
    else:
        step(dve.tensor_tensor(chunks(W.t1), tot.broadcast_to([P, NCH, C]), chunks(W.cum), ALU.subtract))
        step.wait()
        dve.tensor_tensor(W.cum, W.t1, W.sg, ALU.add).then_inc(s["exps_in"], 1)


def direction_dve(dve, R, W, s, z, banks, ready):
    par = lambda ap, p: ap.rearrange("p (j q t) -> p j q t", q=2, t=C)[:, :, p, :]
    step = Steps(dve, s["d_chain"])
    if not ready:
        decay_dve(dve, R, W, s, z, W.pc[:, z, :])
        yield
    if not ready:
        dve.wait_ge(s["sig"], 2)
    step(dve.tensor_tensor(W.tmp, W.rate, W.k1, ALU.mult))
    step(dve.tensor_tensor(W.tmp2, W.rate, W.kk, ALU.mult))
    yield
    step.wait()
    step(dve.tensor_tensor(W.tmp, W.tmp, W.k2, ALU.add))
    step.wait()
    if z == 0:
        step(dve.tensor_copy(W.ksum, W.tmp))
    else:
        step(dve.tensor_tensor(W.ksum, W.ksum, W.tmp, ALU.add))
    yield
    bk = W.bk[:, :, :].rearrange("p (j q) n -> p j q n", q=2)
    ar = W.ar[:, z].rearrange("p (j q) n -> p j q n", q=2)
    if not ready:
        dve.wait_ge(s["exps"], 2)
    for p in range(2):
        dve.tensor_tensor(bk[:, :, p, nat(p):nat(p) + 64], par(W.tmp, p), par(W.t2, p), ALU.mult).then_inc(s["packed"], 1)
        dve.tensor_tensor(bk[:, :, p, oth(p):oth(p) + 64], par(W.tmp2, p), par(W.t2, p), ALU.mult).then_inc(s["packed"], 1)
        dve.tensor_tensor(ar[:, 0:2, p, nat(p):nat(p) + 64], par(W.r, p), par(W.t0[:, 0:NX], p), ALU.mult).then_inc(s["packed"], 1)
        yield
    if not ready:
        dve.wait_ge(s["exps"], 3)
    for p in range(2):
        dve.scalar_tensor_tensor(ar[:, :, p, oth(p):oth(p) + 64], par(W.t1, p), -1.0, par(W.kk, p), ALU.mult, ALU.mult).then_inc(s["packed"], 1)
    yield
    for g in range(4):
        h, jj = g // 2, g % 2
        dve.wait_ge(s["a_done"], g + 1)
        src = R.ps[:, banks[g % len(banks)], :].rearrange("p (j q) -> p j q", q=2 * P)
        dst = W.A[:, z, h, 2 * jj:2 * jj + 2].rearrange("p j q n -> p j (q n)")
        mask = W.masks[:, z].rearrange("p q n -> p (q n)").unsqueeze(1).broadcast_to([P, 2, 2 * P])
        dve.tensor_tensor(dst, src, mask, ALU.mult).then_inc(s["a_out"], 1)
        yield
    for h in range(2):
        dve.wait_ge(s["a_out"], 2 * h + 2)
        dve.tensor_copy(W.At[0:64, z, h, :, 0:64], W.A[0:64, z, h, :, 1, 0:64]).then_inc(s["at_out"], 1)
        dve.tensor_copy(W.At[64:128, z, h, :, 64:128], W.A[64:128, z, h, :, 0, 64:128]).then_inc(s["at_out"], 1)
    yield


def named(prefix, names):
    return [f"{prefix}_{n}" for n in names]


def keys_and_inverses(nc, R, W, I, pair, first, last):
    with stage(nc, "w_loaded", *named("fore", DIRECTION_SEMS), *READOUT_SEMS, *INVERSE_SEMS, *named("back", INVERSE_SEMS), *DECAY_SEMS, *named("next", DECAY_SEMS), *DIRECTION_SEMS,
               "rk", "coef", "coef_out", "bonus_out", "moved", "v_loaded") as (block, s):
        fore = {n: s[f"fore_{n}"] for n in DIRECTION_SEMS}
        back = {n: s[f"back_{n}"] for n in INVERSE_SEMS}
        ahead = {n: s[f"next_{n}"] for n in DECAY_SEMS}

        if not last:
            @block.sync
            def _(sp):
                for n in range(4):
                    sp.dma_start(R.ring[:, n, :], I["w_rkvg"][at(pair, 1), :, n * D:(n + 1) * D].rearrange("a p n -> p (a n)")).then_inc(s["w_loaded"], 16)
                sp.wait_ge(s["rk"], 1)
                sp.wait_ge(s["moved"], 4)
                sp.wait_ge(s["low_done"], 2)
                load_vectors(sp, W, s, I, at(pair, 1))
                sp.wait_ge(s["v_loaded"], 32)
                sp.wait_ge(s["w_loaded"], 64)

        @block.tensor
        def _(pe):
            low_pe(pe, R, W, s, 1, (6, 7))
            for _ in direction_pe(pe, R, W, fore, 0, (2, 3, 4, 5)):
                pass
            pe.wait_ge(fore["at_out"], 4)
            inverse = inverse_pe(pe, R, W, s, 0)
            next(inverse)
            pe.wait_ge(fore["bk_out"], 2)
            if not first:
                for _ in readout_pe(pe, R, W, s):
                    pass
            next(inverse)
            if not first:
                pe.wait_ge(s["out"], 1)
            for _ in range(4):
                next(inverse)
            pe.wait_ge(s["sig"], 2)
            part = direction_pe(pe, R, W, s, 1, (6, 7))
            while next(inverse, "end") != "end":
                next(part, None)
            for _ in part:
                pass
            pe.wait_ge(s["at_out"], 4)
            pe.wait_ge(s["u_out"], 2 * LEVELS)
            for n, _ in enumerate(inverse_pe(pe, R, W, back, 1)):
                if n == 1:
                    pe.wait_ge(s["rk"], 1)
                    pe.wait_ge(s["bk_out"], 1)
                    for j in range(2):
                        mm = pe.matmul(R.ps[:, 6, 2 * j:2 * j + 2], W.t0[:, j * P:(j + 1) * P], R.head_ones[:, 63:65], start=True, stop=True)
                    mm.then_inc(s["coef"], 1)
                if n == 3 and not last:
                    pe.wait_ge(s["v_loaded"], 32)
                    pe.wait_ge(s["coef_out"], 1)
                    pe.wait_ge(s["bk_out"], 2)
                    low_pe(pe, R, W, ahead, 0, (6, 7))

        @block.scalar
        def _(act):
            if not first:
                readout_act(act, R, W, s)
            for _ in direction_act(act, R, W, fore, 0, (2, 3)):
                pass
            decay = decay_act(act, R, W, s, 1, (6, 7), W.pc[:, 1, :])
            next(decay)
            for _ in inverse_act(act, R, W, s, 0):
                next(decay, None)
            for _ in direction_act(act, R, W, s, 1, (6, 7)):
                pass
            decay = iter(()) if last else decay_act(act, R, W, ahead, 0, (6, 7), W.pc_next[:, :])
            for n, _ in enumerate(inverse_act(act, R, W, back, 1)):
                if n == 1:
                    act.wait_ge(s["coef_out"], 1)
                if n:
                    next(decay, None)

        @block.gpsimd
        def _(pool):
            pool.tensor_copy(W.pc[:, 0, :], W.pc_next[:, :]).then_inc(s["moved"], 1)
            if not first:
                pool.wait_ge(s["out"], 1)
            pool.tensor_copy(W.vtok.rearrange("p j n -> p (j n)"), W.vnext[:, :]).then_inc(s["moved"], 1)
            pool.tensor_copy(W.gate, W.gnext[:, :]).then_inc(s["moved"], 1)
            pool.tensor_copy(W.ln[:, :], W.pv[:, V_LNW:V_LNB + 1]).then_inc(s["moved"], 1)

        @block.vector
        def _(dve):
            part = direction_dve(dve, R, W, fore, 0, (2, 3, 4, 5), True)
            out = iter(()) if first else readout_dve(dve, R, W, s, pair - 1)
            for _ in range(5):
                next(part)
            for _ in range(3):
                next(out, None)
                next(part)
            for _ in part:
                pass
            dve.wait_ge(fore["bk_done"], 2)
            part = direction_dve(dve, R, W, s, 1, (6, 7), False)
            for n, _ in enumerate(inverse_dve(dve, R, W, s, 0)):
                if n == 1:
                    next(out, None)
                if n in (2, 4, 5, 7, 8, 9, 11, 13, 14):
                    next(part)
            for _ in part:
                pass
            for n, _ in enumerate(inverse_dve(dve, R, W, back, 1)):
                if n == 0:
                    dve.scalar_tensor_tensor(W.t0[:, 0:NX], W.ksum[:, 0:NX], W.pv[:, V_RK:V_RK + 1], W.r, ALU.mult, ALU.mult).then_inc(s["rk"], 1)
                if n == 4:
                    dve.wait_ge(s["coef"], 1)
                    dve.tensor_copy(W.coef[:, :], R.ps[:, 6, 0:4]).then_inc(s["coef_out"], 1)
                    dve.wait_ge(s["coef_out"], 1)
                    bonus = W.bonus.rearrange("p j (h n) -> p (j h) n", n=64)
                    v4 = W.vnext[:, 0:NX].rearrange("p (g n) -> p g n", n=64)
                    dve.tensor_tensor(bonus, v4, W.coef[:, :].unsqueeze(2).broadcast_to([P, 4, 64]), ALU.mult).then_inc(s["bonus_out"], 1)
                if n == 8 and not last:
                    dve.wait_ge(s["moved"], 1)
                    decay_dve(dve, R, W, ahead, 0, W.pc_next[:, :])


INVERSE_SEMS = ("y_done", "t_done", "tr_done", "y_out", "t_out", "u_out")



def level_columns(ap, l, z):
    return ap.rearrange("p j (b two w) -> p j b two w", two=2, w=1 << l)[:, :, :, z, :]


def inverse_pe(pe, R, W, s, z):
    for l in range(LEVELS + 1):
        for h in range(2):
            if l:
                pe.wait_ge(s["t_out"], 2 * (l - 1) + h + 1)
            if l < LEVELS:
                for j in range(4):
                    out = R.ps[:, h, j * P:(j + 1) * P]
                    if l == 0:
                        mm = pe.transpose(out, W.At[:, z, h, j, :], R.eye[:, :])
                    else:
                        mm = pe.matmul(out, W.At[:, z, h, j, :], W.Tm[:, h, j, :], start=True, stop=True)
                mm.then_inc(s["y_done"], 1)
            if l:
                for j in range(4):
                    mm = pe.transpose(R.ps[:, 4 + h, j * P:(j + 1) * P], W.Tm[:, h, j, :], R.eye[:, :])
                mm.then_inc(s["tr_done"], 1)
        yield
        if 0 < l < LEVELS:
            for h in range(2):
                pe.wait_ge(s["y_out"], 2 * l + h + 1)
                pe.wait_ge(s["u_out"], 2 * (l - 1) + h + 1)
                for j in range(4):
                    mm = pe.matmul(R.ps[:, 2 + h, j * P:(j + 1) * P], W.U[:, z, h, j, :], W.Y[:, h, j, :], start=True, stop=True)
                mm.then_inc(s["t_done"], 1)
            yield


def inverse_act(act, R, W, s, z):
    for l in range(LEVELS):
        for h in range(2):
            act.wait_ge(s["tr_done"], 2 * l + h + 1)
            act.activation(W.U[:, z, h].rearrange("p j n -> p (j n)"), R.ps[:, 4 + h, :], ACT.Copy).then_inc(s["u_out"], 1)
        yield


def inverse_dve(dve, R, W, s, z):
    lm = lambda l, zz: W.lmask[:, l, zz, :].unsqueeze(1).broadcast_to([P, 4, P])
    eye4 = R.eye[:, :].unsqueeze(1).broadcast_to([P, 4, P])
    bank = lambda n: R.ps[:, n, :].rearrange("p (j n) -> p j n", n=P)
    for l in range(LEVELS):
        for h in range(2):
            n = 2 * l + h
            dve.wait_ge(s["y_done"], n + 1)
            cols = (lambda ap: level_columns(ap, l, z)) if l else (lambda ap: ap)
            dve.tensor_tensor(cols(W.Y[:, h]), cols(bank(h)), cols(lm(l, z)), ALU.mult).then_inc(s["y_out"], 1)
        yield
        for h in range(2):
            if l == 0:
                dve.wait_ge(s["y_out"], h + 1)
                dve.tensor_tensor(W.Tm[:, h], W.Y[:, h], eye4, ALU.add).then_inc(s["t_out"], 1)
                if h:
                    yield
            else:
                dve.wait_ge(s["t_done"], 2 * (l - 1) + h + 1)
                dve.wait_ge(s["tr_done"], 2 * (l - 1) + h + 1)
                dve.tensor_tensor(cols(W.Tm[:, h]), cols(W.Tm[:, h]), cols(bank(2 + h)), ALU.add).then_inc(s["t_out"], 1)
                yield


ORDER = ([4, 5, 6, 7, 0, 1, 2, 3], [7, 6, 5, 4, 3, 2, 1, 0])


def rwkv_scan(nc, R, W, I, pair, last):
    with stage(nc, "x_done", "u_done", "y_done", "h_done", "v_in", "x_out", "u_out", "h_scaled", "h_out", "y_out",
               *PROJECT_SEMS) as (block, s):
        first = {}
        for n in range(4, NCH):
            for z in range(2):
                first.setdefault(ORDER[z][n], (n, z))

        @block.tensor
        def _(pe):
            part = iter(()) if last else project_pe(pe, R, W, s)
            for n in range(NCH):
                for z in range(2):
                    ch = ORDER[z][n]
                    j, p, x = ch // 2, ch % 2, ch < 4
                    a, r = oth(p), nat(p)
                    pe.wait_ge(s["h_out"], 2 * n + z + 1 if n else 2)
                    if n >= 5:
                        pe.wait_ge(s["y_out"], 2 * (n - 5) + z + 1)
                    pe.matmul(R.ps[:, z, 0:P], W.ar[:, z, ch, :], W.H[:, z].rearrange("p h n -> p (h n)"), start=True, stop=True)
                    for h in range(2):
                        g = h * 64
                        mm = pe.matmul(R.ps[a:a + 64, z, g:g + 64], W.A[r:r + 64, z, h, j, p, a:a + 64],
                                       W.vtok[r:r + 64, j, g:g + 64], start=False, stop=True, skip_group_check=True)
                    mm.then_inc(s["x_done"], 1)
                next(part, None)
                for z in range(2):
                    ch = ORDER[z][n]
                    j, p = ch // 2, ch % 2
                    a = oth(p)
                    pe.wait_ge(s["x_out"], 2 * n + z + 1)
                    for h in range(2):
                        mm = pe.matmul(R.ps[a:a + 64, 4 + z, h * 64:h * 64 + 64], W.U[a:a + 64, z, h, j, a:a + 64],
                                       W.Xs[a:a + 64, z, h, :], start=True, stop=True)
                    mm.then_inc(s["u_done"], 1)
                next(part, None)
                for z in range(2):
                    ch = ORDER[z][n]
                    j, p, x = ch // 2, ch % 2, ch < 4
                    r = nat(p)
                    pe.wait_ge(s["u_out"], 2 * n + z + 1)
                    pe.wait_ge(s["v_in"], 2 * n + z + 1)
                    for h in range(2):
                        mm = pe.matmul(R.ps[h * 64:h * 64 + 64, 6 + z, 0:64], W.BK[:, z, h, j, p, :], W.Z[:, z, h, :], start=True, stop=True)
                    mm.then_inc(s["h_done"], 1)
                    if x:
                        for h in range(2):
                            mm = pe.matmul(R.ps[r:r + 64, z, h * 64:h * 64 + 64], W.A[:, z, h, j, p, r:r + 64], W.Z[:, z, h, :],
                                           start=False, stop=True, skip_group_check=True)
                    else:
                        mm = pe.nop()
                    mm.then_inc(s["y_done"], 1)
                next(part, None)
            for _ in part:
                pass

        @block.scalar
        def _(act):
            part = iter(()) if last else project_act(act, R, W, s)
            for n in range(NCH):
                if n in (4, 6):
                    next(part, None)
                for z in range(2):
                    ch = ORDER[z][n]
                    j, p = ch // 2, ch % 2
                    a = oth(p)
                    act.wait_ge(s["x_done"], 2 * n + z + 1)
                    act.activation(W.Xs[a:a + 64, z].rearrange("p h n -> p (h n)"), R.ps[a:a + 64, z, 0:P], ACT.Copy).then_inc(s["x_out"], 1)
                for z in range(2):
                    ch = ORDER[z][n]
                    j, p = ch // 2, ch % 2
                    a = oth(p)
                    if n:
                        act.wait_ge(s["y_done"], 2 * (n - 1) + z + 1)
                        act.wait_ge(s["h_done"], 2 * (n - 1) + z + 1)
                    act.wait_ge(s["u_done"], 2 * n + z + 1)
                    act.activation(W.Z[a:a + 64, z].rearrange("p h n -> p (h n)"), R.ps[a:a + 64, 4 + z, 0:128], ACT.Copy).then_inc(s["u_out"], 1)
            for _ in part:
                pass

        @block.gpsimd
        def _(pool):
            for n in range(NCH):
                for z in range(2):
                    ch = ORDER[z][n]
                    j, r = ch // 2, nat(ch % 2)
                    if n:
                        pool.wait_ge(s["y_done"], 2 * (n - 1) + z + 1)
                        pool.wait_ge(s["h_done"], 2 * (n - 1) + z + 1)
                    pool.tensor_copy(W.Z[r:r + 64, z].rearrange("p h n -> p (h n)"), W.vtok[r:r + 64, j, :]).then_inc(s["v_in"], 1)

        @block.vector
        def _(dve):
            for z in range(2):
                dve.memset(W.H[:, z], 0.0).then_inc(s["h_out"], 1)
            dve.wait_ge(s["h_out"], 2)
            part = iter(()) if last else project_dve(dve, R, W, s)
            for n in range(NCH):
                if n in (3, 4, 5, 7):
                    next(part, None)
                for z in range(2):
                    ch = ORDER[z][n]
                    dve.wait_ge(s["h_out"], 2 * n + z + 1)
                    dve.tensor_scalar(W.HP[:, z], W.H[:, z], W.pc[:, z, ch:ch + 1], None, ALU.mult).then_inc(s["h_scaled"], 1)
                for z in range(2):
                    ch = ORDER[z][n]
                    j, p = ch // 2, ch % 2
                    r = nat(p)
                    dve.wait_ge(s["h_done"], 2 * n + z + 1)
                    dve.wait_ge(s["h_scaled"], 2 * n + z + 1)
                    for h in range(2):
                        g = slice(h * 64, h * 64 + 64)
                        up = dve.scalar_tensor_tensor(W.H[g, z, h], R.ps[g, 6 + z, 0:64], W.pc[g, z, ch:ch + 1], W.HP[g, z, h],
                                                      ALU.mult, ALU.add)
                    up.then_inc(s["h_out"], 1)
                for z in range(2):
                    ch = ORDER[z][n]
                    j, p = ch // 2, ch % 2
                    r = nat(p)
                    if ch < 4:
                        dve.wait_ge(s["y_done"], 2 * n + z + 1)
                        y = W.ytok[r:r + 64, j]
                        src = R.ps[r:r + 64, z, 0:P]
                        if first[ch] == (n, z):
                            dve.tensor_copy(y, src).then_inc(s["y_out"], 1)
                        else:
                            n0, z0 = first[ch]
                            dve.wait_ge(s["y_out"], 2 * (n0 - 4) + z0 + 1)
                            dve.tensor_tensor(y, y, src, ALU.add).then_inc(s["y_out"], 1)
            for _ in part:
                pass


READOUT_SEMS = ("o_chain", "var", "root_out", "normed", "turned", "out")


def readout_pe(pe, R, W, s):
    for j in range(2):
        mm = pe.transpose(R.ps[:, 2, j * P:(j + 1) * P], W.bonus[:, j, :], R.eye[:, :])
    mm.then_inc(s["turned"], 1)
    yield
    pe.wait_ge(s["normed"], 1)
    for j in range(2):
        mm = pe.transpose(R.ps[:, 3, j * P:(j + 1) * P], W.ytok[:, j, :], R.eye[:, :])
    mm.then_inc(s["turned"], 1)
    yield


def readout_act(act, R, W, s):
    act.wait_ge(s["var"], 1)
    act.activation(W.st[:, 1, :], W.st[:, 1, :], ACT.Sqrt).then_inc(s["root_out"], 1)


def readout_dve(dve, R, W, s, pair):
    y4 = W.ytok.rearrange("p j (h n) -> p (j h) n", n=64)
    sq = W.yt[:, :].rearrange("p (g n) -> p g n", n=64)
    st = lambda n: W.st[:, n, :]
    wide = lambda ap: ap.unsqueeze(2).broadcast_to([P, 4, 64])
    step = Steps(dve, s["o_chain"])
    step(dve.tensor_reduce(st(0), y4, AX_X, ALU.add))
    step.wait()
    step(dve.tensor_scalar(st(0), st(0), 1.0 / HEAD, None, ALU.mult))
    step.wait()
    step(dve.tensor_tensor(y4, y4, wide(st(0)), ALU.subtract))
    yield
    step.wait()
    step(dve.tensor_tensor(sq, y4, y4, ALU.mult))
    step.wait()
    step(dve.tensor_reduce(st(1), sq, AX_X, ALU.add))
    step.wait()
    dve.tensor_scalar(st(1), st(1), 1.0 / HEAD, GN_EPS, ALU.mult, ALU.add).then_inc(s["var"], 1)
    yield
    dve.wait_ge(s["root_out"], 1)
    step(dve.reciprocal(st(2), st(1)))
    step.wait()
    dve.tensor_tensor(y4, y4, wide(st(2)), ALU.mult).then_inc(s["normed"], 1)
    yield
    y = W.yt[:, :]
    dve.wait_ge(s["turned"], 2)
    step(dve.tensor_scalar(y, R.ps[:, 3, 0:NX], W.ln[:, 0:1], W.ln[:, 1:2], ALU.mult, ALU.add))
    step.wait()
    step(dve.tensor_tensor(y, y, R.ps[:, 2, 0:NX], ALU.add))
    step.wait()
    dve.tensor_tensor(W.u_pairs[:, ds(pair, 1), :].rearrange("p a n -> p (a n)"), y, W.gate, ALU.mult).then_inc(s["out"], 1)
    yield



def hyena_layer(nc, R, I):
    with ExitStack() as c:
        def sb(name, *shape):
            return c.enter_context(nc.sbuf_tensor(name, [P, *shape], F32))

        W = Named()
        W.Kf = sb("filter_spectrum", 4, E)
        W.dft = sb("dft", 2, 4 * P)
        W.idft = sb("idft", 4, NX)
        W.hv = sb("hyena_vec", 5, 3 * KE)
        hyena_filters(nc, R, W, I)
        modulate(nc, R, R.mods[:, 1], R.vec[:, 4, KD:2 * KD], NX)
        W.proj = sb("hyena_proj", 4 * KE, NX)
        hyena_project(nc, R, W, I)
        hyena_convolve(nc, R, W)
        dense(nc, R, I["w_out1"], KD, KE, NX, lambda k: W.proj[:, k, :], lambda m: R.h[:, ds(m, 1), 0:NX].rearrange("p a n -> p (a n)"))
    add_back(nc, R, R.h, R.mods[:, 1], R.vec[:, 5, KD:2 * KD], NX)


def hyena_filters(nc, R, W, I):
    with ExitStack() as c:
        def sb(name, *shape):
            return c.enter_context(nc.sbuf_tensor(name, [P, *shape], F32))

        f1, f23, fb = sb("f_w1", 64), sb("f_w23", 2, 64), sb("f_vec", 4)
        zt, hid, arg, rnd = sb("z_t", NX), sb("hid", NX), sb("arg", NX), sb("rnd", NX)
        w4 = sb("f_w4", 2, E)
        sd = sb("sum_diff", 2, 2, E)
        win = sb("window", 2, E)
        with stage(nc, "loaded", "summed", "layer", "chain", "sine", "filt", "filt_out") as (block, s):
            loads = [(f1[0:33, :], I["f_w1"]), (f23[0:64, :, :], I["f_w23"]), (fb[0:64, :], I["f_vec"]), (zt[0:33, :], I["z_t"]),
                     (w4[0:64, :, :], I["f_w4"]), (win[:, :, :], I["window"]), (W.dft[:, :, :], I["dft"]),
                     (W.idft[:, :, :], I["idft"]), (W.hv[:, :, :], I["hyena_vec"])]

            @block.sync
            def _(sp):
                for dst, src in loads:
                    sp.dma_start(dst, src).then_inc(s["loaded"], 16)

            @block.tensor
            def _(pe):
                pe.wait_ge(s["loaded"], 16 * len(loads))
                for n in range(3):
                    if n:
                        pe.wait_ge(s["sine"], n)
                    w, x = (f1[0:33, :], zt[0:33, :]) if n == 0 else (f23[0:64, n - 1, :], hid[0:64, :])
                    pe.matmul(R.ps[0:64, 0, 0:NX], w, x, start=True, stop=True).then_inc(s["layer"], 1)
                pe.wait_ge(s["sine"], 3)
                pe.wait_ge(s["summed"], 3)
                for n in range(16):
                    t, q, ch = n // 8, n // 4 % 2, n % 4
                    if n >= 7:
                        pe.wait_ge(s["filt_out"], n - 6)
                    pe.matmul(R.ps[:, 1 + n % 7, :], hid[0:64, t * P:(t + 1) * P], w4[0:64, q, ch * 512:(ch + 1) * 512],
                              start=True, stop=True).then_inc(s["filt"], 1)

            @block.scalar
            def _(act):
                for n in range(3):
                    act.wait_ge(s["chain"], 6 * n + 6)
                    act.activation(hid[0:64, :], arg[0:64, :], ACT.Sin).then_inc(s["sine"], 1)

            @block.vector
            def _(dve):
                dve.wait_ge(s["loaded"], 16 * len(loads))
                step = Steps(dve, s["chain"])
                for n in range(3):
                    dve.wait_ge(s["layer"], n + 1)
                    a, r = arg[0:64, :], rnd[0:64, :]
                    step(dve.tensor_scalar(a, R.ps[0:64, 0, 0:NX], fb[0:64, n:n + 1], fb[0:64, 3:4], ALU.add, ALU.mult))
                    step.wait()
                    step(dve.tensor_scalar(r, a, 1 / (2 * math.pi), BIG, ALU.mult, ALU.add))
                    step.wait()
                    step(dve.tensor_scalar(r, r, -BIG, None, ALU.add))
                    step.wait()
                    step(dve.scalar_tensor_tensor(a, r, -6.28125, a, ALU.mult, ALU.add))
                    step.wait()
                    step(dve.scalar_tensor_tensor(a, r, -(2 * math.pi - 6.28125), a, ALU.mult, ALU.add))
                    step.wait()
                    step(dve.tensor_scalar(a, a, 3.1415925, -3.1415925, ALU.min, ALU.max))
                    if n == 0:
                        tmp = sd[0:64, 0, 0, :]
                        dve.tensor_tensor(tmp, w4[0:64, 0, :], w4[0:64, 1, :], ALU.subtract).then_inc(s["summed"], 1)
                        dve.wait_ge(s["summed"], 1)
                        dve.tensor_tensor(w4[0:64, 0, :], w4[0:64, 0, :], w4[0:64, 1, :], ALU.add).then_inc(s["summed"], 1)
                        dve.wait_ge(s["summed"], 2)
                        dve.tensor_copy(w4[0:64, 1, :], tmp).then_inc(s["summed"], 1)
                        dve.wait_ge(s["summed"], 3)
                for n in range(16):
                    t, q, ch = n // 8, n // 4 % 2, n % 4
                    cols = slice(ch * 512, (ch + 1) * 512)
                    dve.wait_ge(s["filt"], n + 1)
                    dve.tensor_tensor(sd[:, q, t, cols], R.ps[:, 1 + n % 7, :], win[:, t, cols], ALU.mult).then_inc(s["filt_out"], 1)

        with stage(nc, "done", "copied") as (block, s):
            @block.tensor
            def _(pe):
                for n in range(16):
                    f, ch = n // 4, n % 4
                    if n >= 8:
                        pe.wait_ge(s["copied"], n - 7)
                    for t in range(2):
                        mm = pe.matmul(R.ps[:, n % 8, :], W.dft[:, t, f * P:(f + 1) * P], sd[:, f // 2, t, ch * 512:(ch + 1) * 512],
                                       start=(t == 0), stop=(t == 1))
                    mm.then_inc(s["done"], 1)

            @block.vector
            def _(dve):
                for n in range(16):
                    f, ch = n // 4, n % 4
                    dve.wait_ge(s["done"], n + 1)
                    dve.tensor_copy(W.Kf[:, f, ch * 512:(ch + 1) * 512], R.ps[:, n % 8, :]).then_inc(s["copied"], 1)


def hyena_project(nc, R, W, I):
    conv = 3 * KE

    def evac(dve, s, n, m, bank):
        out = W.proj[:, ds(m, 1), :].rearrange("p a n -> p (a n)")
        vec = lambda q: W.hv[:, q, ds(m, 1)]
        dve.tensor_scalar(out, R.ps[:, bank, 0:NX], vec(1), vec(3), ALU.mult, ALU.add).then_inc(s["part"], 1)
        dve.wait_ge(s["part"], n * 2 + 1)
        dve.scalar_tensor_tensor(out[:, 1:], R.ps[:, bank, 0:NX - 1], vec(0), out[:, 1:], ALU.mult, ALU.add).then_inc(s["part"], 1)
        dve.wait_ge(s["part"], n * 2 + 2)
        return dve.scalar_tensor_tensor(out[:, :-1], R.ps[:, bank, 1:NX], vec(2), out[:, :-1], ALU.mult, ALU.add)

    dense(nc, R, I["w_in1"], conv, KD, NX, lambda k: R.h[:, k, 0:NX], None, evac)
    dense(nc, R, I["w_gate1"], KE, KD, NX, lambda k: R.h[:, k, 0:NX], lambda m: W.proj[:, ds(m + conv, 1), :].rearrange("p a n -> p (a n)"))


def hyena_convolve(nc, R, W):
    x0, u, v, gate = (W.proj[:, q * KE:(q + 1) * KE, :] for q in range(4))
    utok = R.sq[:, :, :].rearrange("p a b -> p (a b)").rearrange("p (t n) -> p t n", n=E)
    with stage(nc, "u", "gate", "turned", "utok", "spec", "spec_out", "chain", "mult", "conv", "out") as (block, s):
        @block.scalar
        def _(act):
            for q in range(4):
                act.activation(gate[:, 4 * q:4 * q + 4, :], gate[:, 4 * q:4 * q + 4, :], ACT.Silu).then_inc(s["gate"], 1)
            for n in range(8):
                t, q = n % 2, n // 2
                act.wait_ge(s["turned"], n + 1)
                act.activation(utok[:, t, q * 512:(q + 1) * 512], R.ps[:, n % 2, :], ACT.Copy).then_inc(s["utok"], 1)
            for q in range(4):
                for f in range(4):
                    act.wait_ge(s["spec"], 4 * q + f + 1)
                    if q >= 2:
                        act.wait_ge(s["mult"], q - 1)
                    act.activation(R.h[:, 4 * (q % 2) + f, :], R.ps[:, 2 + f, :], ACT.Copy).then_inc(s["spec_out"], 1)

        @block.tensor
        def _(pe):
            for n in range(8):
                t, q = n % 2, n // 2
                pe.wait_ge(s["u"], q + 1)
                if n >= 2:
                    pe.wait_ge(s["utok"], n - 1)
                for b in range(4):
                    mm = pe.transpose(R.ps[:, n % 2, b * P:(b + 1) * P], u[:, 4 * q + b, t * P:(t + 1) * P], R.eye[:, :])
                mm.then_inc(s["turned"], 1)
            for q in range(4):
                pe.wait_ge(s["utok"], 2 * q + 2)
                for f in range(4):
                    if q:
                        pe.wait_ge(s["spec_out"], 4 * (q - 1) + f + 1)
                    for t in range(2):
                        mm = pe.matmul(R.ps[:, 2 + f, :], W.dft[:, t, f * P:(f + 1) * P], utok[:, t, q * 512:(q + 1) * 512],
                                       start=(t == 0), stop=(t == 1))
                    mm.then_inc(s["spec"], 1)
            for m in range(KE):
                pe.wait_ge(s["mult"], m // 4 + 1)
                if m >= 2:
                    pe.wait_ge(s["out"], 3 * (m - 2) + 1)
                for f in range(4):
                    mm = pe.matmul(R.ps[:, 6 + m % 2, 0:NX], W.Kf[:, f, m * P:(m + 1) * P], W.idft[:, f, :],
                                   start=(f == 0), stop=(f == 3))
                mm.then_inc(s["conv"], 1)

        @block.vector
        def _(dve):
            step = Steps(dve, s["chain"])
            for q in range(4):
                a = slice(4 * q, 4 * q + 4)
                dve.tensor_tensor(u[:, a, :], v[:, a, :], u[:, a, :], ALU.mult).then_inc(s["u"], 1)
            dve.wait_ge(s["u"], 4)
            ta = v[:, 0:4, :].rearrange("p (a b) n -> p a (b n)", a=2)
            tb = v[:, 4:8, :].rearrange("p (a b) n -> p a (b n)", a=2)
            for q in range(4):
                dve.wait_ge(s["spec_out"], 4 * q + 4)
                cols = slice(q * 512, (q + 1) * 512)
                b = 4 * (q % 2)
                ure, uim = R.h[:, b:b + 2, :], R.h[:, b + 2:b + 4, :]
                kre, kim = W.Kf[:, 0:2, cols], W.Kf[:, 2:4, cols]
                step(dve.tensor_tensor(ta, uim, kim, ALU.mult))
                step(dve.tensor_tensor(tb, ure, kim, ALU.mult))
                step.wait()
                step(dve.tensor_tensor(kim, uim, kre, ALU.mult))
                step.wait()
                step(dve.tensor_tensor(kre, ure, kre, ALU.mult))
                step.wait()
                step(dve.tensor_tensor(kre, kre, ta, ALU.subtract))
                step(dve.tensor_tensor(kim, kim, tb, ALU.add))
                step.wait()
                dve.sem_inc(s["mult"], 1)
            dve.wait_ge(s["gate"], 4)
            for m in range(KE):
                dve.wait_ge(s["conv"], m + 1)
                n = 3 * m
                dve.scalar_tensor_tensor(u[:, m, :], u[:, m, :], W.hv[:, 4, m:m + 1], R.ps[:, 6 + m % 2, 0:NX], ALU.mult, ALU.add).then_inc(s["out"], 1)
                dve.wait_ge(s["out"], n + 1)
                dve.tensor_tensor(x0[:, m, :], x0[:, m, :], u[:, m, :], ALU.mult).then_inc(s["out"], 1)
                dve.wait_ge(s["out"], n + 2)
                dve.tensor_tensor(x0[:, m, :], x0[:, m, :], gate[:, m, :], ALU.mult).then_inc(s["out"], 1)



RK, DK, RQ, DQ, RG, DG, MU, MG = range(8)


def second_layer(nc, R, I, l):
    last = l == 1
    NQ = NX if last else NT
    w_feature, w_token, w_merge, w_last = ((I["w_feature0"], I["w_token0"], I["w_merge0"], I["w_last0"]),
                                           (I["w_feature1"], I["w_token1"], I["w_merge1"], I["w_last1"]))[l]
    modulate(nc, R, R.mods[:, 2 + l], R.vec[:, 6, l * 8:l * 8 + 8], NT)
    with ExitStack() as c:
        def sb(name, *shape):
            return c.enter_context(nc.sbuf_tensor(f"{name}_{l}", [P, *shape], F32))

        W = Named()
        W.F, W.D, W.sc = sb("features", 32, NT), sb("decays", HEADS, 4, NX), sb("scalars", 64)
        W.rv, W.dv, W.mv = sb("ret_v", 4, BW), sb("diff_v", 4, BW), sb("mlp_v", 4, BW)
        W.small = sb("small", 13, NX)
        dense(nc, R, w_feature[0:8], 8, KD, NT, lambda k: R.h[:, k, :], lambda m: W.F[:, ds(m, 1), :].rearrange("p a n -> p (a n)"))
        dense(nc, R, w_feature[8:32], 24, KD, NQ, lambda k: R.h[:, k, 0:NQ], lambda m: W.F[:, ds(m + 8, 1), 0:NQ].rearrange("p a n -> p (a n)"))
        values(nc, R, W, I, w_token, l, NQ)
        retention(nc, R, W, NQ)
        diff_attention(nc, R, W, NQ)
        lam_init = 0.8 - 0.6 * math.exp(-0.3 * l)
        merge(nc, R, W, I, w_merge, l, NQ, 1.0 - lam_init)
        dense(nc, R, w_last, KD, KD, NQ, lambda k: R.sq[:, k, 0:NQ], lambda m: R.h[:, ds(m, 1), 0:NQ].rearrange("p a n -> p (a n)"))
    add_back(nc, R, R.h, R.mods[:, 2 + l], R.vec[:, 7, l * 8:l * 8 + 8], NQ)


def values(nc, R, W, I, w_token, l, NQ):
    sc, small = W.sc, W.small[:, :, :].rearrange("p a n -> p (a n)")
    W.logit, W.lg, W.ax, W.y, W.s0, W.s1, W.s2, W.poly = (sc[:, 8 * n:8 * n + 8] for n in range(8))
    W.lam = sc[:, 56:57]
    W.tab = small[:, 0:4 * NX].rearrange("p (q n) -> p q n", n=NX)
    W.terms = small[:, 4 * NX:8 * NX].rearrange("p (q n) -> p q n", n=NX)
    W.swap = small[:, 8 * NX:9 * NX].rearrange("p (q n) -> p q n", n=P)
    W.same = small[:, 9 * NX:11 * NX]
    W.lamk = small[:, 11 * NX:12 * NX].rearrange("p (a b n) -> p a b n", a=2, b=2)
    W.prod = small[:, 12 * NX:12 * NX + P].rearrange("p (b n) -> p b n", b=2)
    W.lsum = small[:, 12 * NX + P:12 * NX + P + 2]
    W.dist = R.sq[:, 4:8, :]
    targets = (W.rv, W.dv, W.mv)
    jobs = [(g, t) for g in range(3) for t in range(4 if g < 2 else NQ // P)]
    J = len(jobs)
    w_sems = [f"w_loaded{g}" for g in range(3)]
    with stage(nc, *w_sems, "loaded", "done", "copied", "chain", "act", "swapped", "term", "scaled", "rotated") as (block, s):
        w_loaded = [s[n] for n in w_sems]
        wt = [R.ring[:, 4 * b:4 * b + 4, :].rearrange("p a (b n) -> p (a b) n", n=512) for b in range(2)]
        loads = [(W.tab, I["rope"]), (W.swap, I["swaps"]), (W.logit, I["ret_logit"][l]), (W.lamk, I["lambdas"][l]),
                 (W.dist, I["distances"]), (W.same, I["same"])]

        @block.sync
        def _(sp):
            for g in range(2):
                sp.dma_start(wt[g], w_token[g]).then_inc(w_loaded[g], 16)
            sp.wait_ge(s["done"], 4)
            sp.dma_start(wt[0], w_token[2]).then_inc(w_loaded[2], 16)

        @block.tensor
        def _(pe):
            swaps = rotate_pe(pe, R, W, s, 16 * len(loads))
            for n, (g, t) in enumerate(jobs):
                if t == 0:
                    pe.wait_ge(w_loaded[g], 16)
                if n >= 4:
                    pe.wait_ge(s["copied"], n - 3)
                for k in range(KD):
                    mm = pe.matmul(R.ps[:, n % 4, :], R.h[:, k, t * P:(t + 1) * P], wt[g % 2][:, k, :], start=(k == 0), stop=(k == KD - 1))
                mm.then_inc(s["done"], 1)
                next(swaps, None)
            for _ in swaps:
                pass

        @block.scalar
        def _(act):
            for dst, src in loads:
                act.dma_start(dst, src).then_inc(s["loaded"], 16)
            part = decays_act(act, R, W, s)
            for n, (g, t) in enumerate(jobs):
                if n in (J - 4, J - 2):
                    next(part)
                act.wait_ge(s["done"], n + 1)
                act.activation(targets[g][:, t, :], R.ps[:, n % 4, :], ACT.Copy).then_inc(s["copied"], 1)

        @block.vector
        def _(dve):
            dve.wait_ge(s["loaded"], 16 * len(loads))
            rotate_dve(dve, R, W, s)
            decays_dve(dve, R, W, s, l)


ROTATIONS = [(g, h) for h in range(4) for g in (RK, RQ, DK, DQ)]


def rotate_pe(pe, R, W, s, loaded):
    for n, (g, h) in enumerate(ROTATIONS):
        if n == 0:
            pe.wait_ge(s["loaded"], loaded)
        if n >= 4:
            pe.wait_ge(s["term"], n - 3)
        pe.matmul(R.ps[:, 4 + n % 4, 0:NX], W.swap[:, int(g in (DK, DQ)), :], W.F[:, 4 * g + h, 0:NX], start=True, stop=True).then_inc(s["swapped"], 1)
        if n % 2:
            yield


def rotate_dve(dve, R, W, s):
    for n, (g, h) in enumerate(ROTATIONS):
        q = 2 * int(g in (DK, DQ))
        x, t = W.F[:, 4 * g + h, 0:NX], W.terms[:, n % 4, :]
        dve.wait_ge(s["swapped"], n + 1)
        if n >= 4:
            dve.wait_ge(s["rotated"], n - 3)
        dve.tensor_tensor(t, R.ps[:, 4 + n % 4, 0:NX], W.tab[:, q + 1, :], ALU.mult).then_inc(s["term"], 1)
        dve.tensor_tensor(x, x, W.tab[:, q, :], ALU.mult).then_inc(s["scaled"], 1)
        dve.wait_ge(s["term"], n + 1)
        dve.wait_ge(s["scaled"], n + 1)
        dve.tensor_tensor(x, x, t, ALU.add).then_inc(s["rotated"], 1)


EXPONENTS_READY = 4 + 4 + 1 + 16 + 3 + 2 + 2 * HEADS + 1


def decays_dve(dve, R, W, s, l):
    lam_init = 0.8 - 0.6 * math.exp(-0.3 * l)
    logit, lg, ax, y, sd, s1, s2, poly = W.logit, W.lg, W.ax, W.y, W.s0, W.s1, W.s2, W.poly
    lamk, prod, lsum, dist, same = W.lamk, W.prod, W.lsum, W.dist, W.same
    step = Steps(dve, s["chain"])

    def seq(ins):
        step(ins)
        step.wait()

    seq(dve.tensor_scalar(ax, logit, -1.0, None, ALU.mult))
    seq(dve.tensor_tensor(ax, ax, logit, ALU.max))
    seq(dve.tensor_tensor(prod, lamk[:, 0], lamk[:, 1], ALU.mult))
    seq(dve.tensor_reduce(lsum, prod, AX_X, ALU.add))
    dve.wait_ge(s["act"], 2)
    seq(dve.tensor_scalar(sd, y, 2.0, None, ALU.add))
    seq(dve.reciprocal(sd, sd))
    seq(dve.tensor_tensor(s1, y, sd, ALU.mult))
    seq(dve.tensor_tensor(s2, s1, s1, ALU.mult))
    seq(dve.tensor_scalar(poly, s2, 1 / 19, 1 / 17, ALU.mult, ALU.add))
    for q in (15, 13, 11, 9, 7, 5, 3, 1):
        seq(dve.tensor_tensor(poly, poly, s2, ALU.mult))
        seq(dve.tensor_scalar(poly, poly, 1 / q, None, ALU.add))
    seq(dve.tensor_tensor(poly, poly, s1, ALU.mult))
    seq(dve.tensor_scalar(lg, logit, 0.0, None, ALU.min))
    seq(dve.scalar_tensor_tensor(lg, poly, -2.0, lg, ALU.mult, ALU.add))
    seq(dve.tensor_tensor(W.lam, lsum[:, 0:1], lsum[:, 1:2], ALU.subtract))
    seq(dve.tensor_scalar(W.lam, W.lam, lam_init, None, ALU.add))
    for h in range(HEADS):
        d = W.D[:, h, 0:2, :].rearrange("p a n -> p (a n)")
        seq(dve.tensor_scalar(d, dist[:, 0, :], lg[:, h:h + 1], None, ALU.mult))
        seq(dve.scalar_tensor_tensor(d, dist[:, 1, :], lg[:, 4 + h:5 + h], d, ALU.mult, ALU.add))
    dve.sem_inc(s["chain"], 1)
    step.n += 1
    for h in range(HEADS):
        dve.wait_ge(s["act"], 3 + h)
        d = W.D[:, h, 0:2, :].rearrange("p a n -> p (a n)")
        step(dve.tensor_tensor(d, d, same, ALU.add))
    for h in range(HEADS):
        dve.wait_ge(s["act"], 2 + HEADS + 2 * h + 2)
        d = W.D[:, h, 2:4, :].rearrange("p a n -> p (a n)")
        other = R.sq[:, h, :]
        step(dve.tensor_tensor(d, d, other, ALU.add))


def decays_act(act, R, W, s):
    lg, dist = W.lg, W.dist
    act.wait_ge(s["chain"], 4)
    act.activation(W.y, W.ax, ACT.Exp, scale=-1.0).then_inc(s["act"], 1)
    act.activation(W.lsum, W.lsum, ACT.Exp).then_inc(s["act"], 1)
    yield
    act.wait_ge(s["chain"], EXPONENTS_READY)
    for h in range(HEADS):
        d = W.D[:, h, 0:2, :].rearrange("p a n -> p (a n)")
        act.activation(d, d, ACT.Exp).then_inc(s["act"], 1)
    for h in range(HEADS):
        d = W.D[:, h, 2:4, :].rearrange("p a n -> p (a n)")
        act.activation(d, dist[:, 2, :], ACT.Exp, scale=lg[:, h:h + 1]).then_inc(s["act"], 1)
        act.activation(R.sq[:, h, :], dist[:, 3, :], ACT.Exp, scale=lg[:, 4 + h:5 + h]).then_inc(s["act"], 1)
    yield


def retention(nc, R, W, NQ):
    jobs = [(h, side) for h in range(HEADS) for side in range(NQ // NX)]
    with stage(nc, "scores", "decayed", "out", "out_copied") as (block, s):
        score = R.ring[:, 0:2, :].rearrange("p a (b n) -> p (a b) n", n=NX)

        def keys(side):
            return [(0, 0), (1, 1), (2, 2), (3, 3)] if side == 0 else [(2, 0), (3, 1)]

        first = [0]
        for _, side in jobs:
            first.append(first[-1] + len(keys(side)))

        @block.tensor
        def _(pe):
            for n, (h, side) in enumerate(jobs):
                q = W.F[:, 4 * RQ + h, side * NX:(side + 1) * NX]
                for i, (kt, _) in enumerate(keys(side)):
                    if n:
                        pe.wait_ge(s["decayed"], first[n])
                    pe.matmul(R.ps[:, i, 0:NX], W.F[:, 4 * RK + h, kt * P:(kt + 1) * P], q, start=True, stop=True).then_inc(s["scores"], 1)
                if n >= 2:
                    pe.wait_ge(s["out_copied"], n - 1)
                for i, (kt, _) in enumerate(keys(side)):
                    pe.wait_ge(s["decayed"], first[n] + i + 1)
                    mm = pe.matmul(R.ps[:, 4 + n % 2, 0:NX], W.rv[:, kt, h * P:(h + 1) * P], score[:, 4 * (n % 2) + i, :],
                                   start=(i == 0), stop=(i == len(keys(side)) - 1))
                mm.then_inc(s["out"], 1)

        @block.vector
        def _(dve):
            for n, (h, side) in enumerate(jobs):
                for i, (_, dt) in enumerate(keys(side)):
                    dve.wait_ge(s["scores"], first[n] + i + 1)
                    if n >= 2:
                        dve.wait_ge(s["out"], n - 1)
                    dve.scalar_tensor_tensor(score[:, 4 * (n % 2) + i, :], R.ps[:, i, 0:NX], float(P) ** -0.5,
                                             W.D[:, h, dt, :], ALU.mult, ALU.mult).then_inc(s["decayed"], 1)

        @block.scalar
        def _(act):
            for n, (h, side) in enumerate(jobs):
                act.wait_ge(s["out"], n + 1)
                act.activation(W.F[:, 4 * RQ + h, side * NX:(side + 1) * NX], R.ps[:, 4 + n % 2, 0:NX], ACT.Copy).then_inc(s["out_copied"], 1)


def diff_attention(nc, R, W, NQ):
    jobs = [(h, t) for h in range(HEADS) for t in range(NQ // P)]
    J, DEPTH = len(jobs), 3
    prob = R.ring[:, 0:6, :].rearrange("p (b a) (c n) -> p b (a c) n", b=3, n=512)
    st = R.rstd
    with stage(nc, "scores", "top", "expd", "chain", "mixed", "turned", "turned_out", "out", "out_copied") as (block, s):
        def span(n):
            return (0, 4) if jobs[n][1] < 2 else (2, 4)

        @block.tensor
        def _(pe):
            def scores(n):
                h, t = jobs[n]
                a, b = span(n)
                if n >= DEPTH:
                    pe.wait_ge(s["expd"], 2 * (n - DEPTH) + 2)
                for m in range(2):
                    r = slice(64 * m, 64 * m + 64)
                    mm = pe.matmul(R.ps[:, 2 * (n % DEPTH) + m, 0:(b - a) * P], W.F[r, 4 * DQ + h, t * P:(t + 1) * P],
                                   W.F[r, 4 * DK + h, a * P:b * P], start=True, stop=True)
                mm.then_inc(s["scores"], 1)

            def turn(n):
                a, b = span(n)
                pe.wait_ge(s["mixed"], n + 1)
                if n:
                    pe.wait_ge(s["turned_out"], n)
                for i in range(b - a):
                    mm = pe.transpose(R.ps[:, 6, i * P:(i + 1) * P], prob[:, n % DEPTH, 2, i * P:(i + 1) * P], R.eye[:, :])
                mm.then_inc(s["turned"], 1)

            def values(n):
                h, t = jobs[n]
                a, b = span(n)
                pe.wait_ge(s["turned_out"], n + 1)
                if n >= 2:
                    pe.wait_ge(s["out_copied"], n - 1)
                o = 256 * (n % 2)
                for i in range(b - a):
                    mm = pe.matmul(R.ps[:, 7, o:o + P], W.dv[:, a + i, h * P:(h + 1) * P], prob[:, n % DEPTH, 3, i * P:(i + 1) * P],
                                   start=(i == 0), stop=(i == b - a - 1))
                mm.then_inc(s["out"], 1)

            scores(0)
            scores(1)
            for n in range(J):
                if n + 2 < J:
                    scores(n + 2)
                if n:
                    values(n - 1)
                turn(n)
            values(J - 1)

        @block.scalar
        def _(act):
            def exps(n):
                a, b = span(n)
                act.wait_ge(s["top"], n + 1)
                if n >= DEPTH:
                    act.wait_ge(s["mixed"], n - DEPTH + 1)
                c = 16 * (n % DEPTH)
                for m in range(2):
                    act.activation(prob[:, n % DEPTH, m, 0:(b - a) * P], R.ps[:, 2 * (n % DEPTH) + m, 0:(b - a) * P], ACT.Exp,
                                   bias=st[:, c + m:c + m + 1], scale=0.125, accum_out=st[:, c + 2 + m:c + 3 + m]).then_inc(s["expd"], 1)

            def out_copy(n):
                h, t = jobs[n]
                act.wait_ge(s["out"], n + 1)
                o = 256 * (n % 2)
                act.activation(W.F[:, 4 * DQ + h, t * P:(t + 1) * P], R.ps[:, 7, o:o + P], ACT.Copy).then_inc(s["out_copied"], 1)

            exps(0)
            exps(1)
            for n in range(J):
                a, b = span(n)
                if n:
                    out_copy(n - 1)
                act.wait_ge(s["turned"], n + 1)
                if n >= DEPTH:
                    act.wait_ge(s["out"], n - DEPTH + 1)
                act.activation(prob[:, n % DEPTH, 3, 0:(b - a) * P], R.ps[:, 6, 0:(b - a) * P], ACT.Copy).then_inc(s["turned_out"], 1)
                if n + 2 < J:
                    exps(n + 2)
            out_copy(J - 1)

        @block.vector
        def _(dve):
            step = Steps(dve, s["chain"])

            def tops(n):
                a, b = span(n)
                c = 16 * (n % DEPTH)
                dve.wait_ge(s["scores"], n + 1)
                bank = 2 * (n % DEPTH)
                step(dve.tensor_reduce(st[:, c:c + 2], R.ps[:, bank:bank + 2, 0:(b - a) * P], AX_X, ALU.max))
                step.wait()
                dve.tensor_scalar(st[:, c:c + 2], st[:, c:c + 2], -0.125, None, ALU.mult).then_inc(s["top"], 1)

            tops(0)
            tops(1)
            for n in range(J):
                a, b = span(n)
                c = 16 * (n % DEPTH)
                p = prob[:, n % DEPTH]
                w = (b - a) * P
                dve.wait_ge(s["expd"], 2 * n + 2)
                step(dve.reciprocal(st[:, c + 4:c + 6], st[:, c + 2:c + 4]))
                step.wait()
                step(dve.scalar_tensor_tensor(st[:, c + 6:c + 7], st[:, c + 5:c + 6], -1.0, W.lam, ALU.mult, ALU.mult))
                step.wait()
                step(dve.tensor_scalar(p[:, 1, 0:w], p[:, 1, 0:w], st[:, c + 6:c + 7], None, ALU.mult))
                step.wait()
                if n >= DEPTH:
                    dve.wait_ge(s["turned"], n - DEPTH + 1)
                dve.scalar_tensor_tensor(p[:, 2, 0:w], p[:, 0, 0:w], st[:, c + 4:c + 5], p[:, 1, 0:w],
                                         ALU.mult, ALU.add).then_inc(s["mixed"], 1)
                if n + 2 < J:
                    tops(n + 2)


BRANCH_BANKS = (1, 3, 5, 6, 7)
NORMS = ((RQ, RG), (DQ, DG))


def branch_bank(n):
    return BRANCH_BANKS[n % len(BRANCH_BANKS)]


def branches_pe(pe, R, W, s, NQ):
    for n in range(2 * HEADS):
        pe.wait_ge(s["squared"], n + 1)
        if n >= len(BRANCH_BANKS):
            pe.wait_ge(s["log"], n - len(BRANCH_BANKS) + 1)
        pe.matmul(R.ps[:, branch_bank(n), 0:NQ], R.ones[:, :], R.sq[:, n, 0:NQ], start=True, stop=True).then_inc(s["summed"], 1)
    yield
    pe.wait_ge(s["mlp_loaded"], 32)
    pe.wait_ge(s["normed"], NQ // P)
    for g in range(4):
        n = 2 * HEADS + g
        pe.wait_ge(s["log"], n - len(BRANCH_BANKS) + 1)
        for t in range(NQ // P):
            mm = pe.matmul(R.ps[:, branch_bank(n), t * P:(t + 1) * P], W.mv[:, t, g * P:(g + 1) * P], W.mix_w[:, g, :], start=True, stop=True)
        mm.then_inc(s["mixed"], 1)
    yield


def branches_act(act, R, W, s, NQ):
    for n in range(2 * HEADS):
        O, h = NORMS[n // HEADS][0], n % HEADS
        act.activation(R.sq[:, n, 0:NQ], W.F[:, 4 * O + h, 0:NQ], ACT.Square).then_inc(s["squared"], 1)
    act.wait_ge(s["var"], 1)
    T = NQ // P
    act.activation(W.moments[:, 0:T, 1], W.moments[:, 0:T, 1], ACT.Sqrt, bias=R.eps[:, 0:1]).then_inc(s["root"], 1)
    for G in (MG, RG, DG):
        for h in range(HEADS):
            act.activation(W.F[:, 4 * G + h, 0:NQ], W.F[:, 4 * G + h, 0:NQ], ACT.Silu).then_inc(s["gate"], 1)
    for n in range(2 * HEADS):
        act.wait_ge(s["summed"], n + 1)
        act.activation(R.sq[:, n, 0:NQ], R.ps[:, branch_bank(n), 0:NQ], ACT.Ln, bias=R.eps[:, 0:1], scale=1.0 / P).then_inc(s["log"], 1)
    for n in range(2 * HEADS):
        act.wait_ge(s["log"], n + 1)
        act.activation(R.sq[:, n, 0:NQ], R.sq[:, n, 0:NQ], ACT.Exp, scale=-0.5).then_inc(s["rstd"], 1)


def branches_dve(dve, R, W, s, NQ, factor):
    T = NQ // P
    step = Steps(dve, s["b_chain"])
    for t in range(T):
        step(dve.bn_stats(W.stats[:, t, :], W.mv[:, t, :]))
    for t in range(T):
        step.wait(t + 1)
        step(dve.bn_aggr(W.moments[:, t, :], W.stats[:, t, :]))
    step.wait()
    dve.sem_inc(s["var"], 1)
    dve.wait_ge(s["root"], 1)
    step(dve.reciprocal(W.moments[:, 0:T, 1], W.moments[:, 0:T, 1]))
    step.wait()
    for t in range(T):
        dve.tensor_scalar(W.mv[:, t, :], W.mv[:, t, :], W.moments[:, t, 0:1], W.moments[:, t, 1:2], ALU.subtract, ALU.mult).then_inc(s["normed"], 1)
    for n in range(2 * HEADS):
        O, G = NORMS[n // HEADS]
        o, g = (W.F[:, 4 * x + n % HEADS, 0:NQ] for x in (O, G))
        dve.wait_ge(s["rstd"], n + 1)
        dve.tensor_tensor(o, o, R.sq[:, n, 0:NQ], ALU.mult).then_inc(s["scaled"], 1)
        dve.wait_ge(s["scaled"], n + 1)
        dve.wait_ge(s["gate"], 4 + n + 1)
        dve.scalar_tensor_tensor(g, o, 1.0 if n < HEADS else factor, g, ALU.mult, ALU.mult).then_inc(s["branch_out"], 1)
    dve.wait_ge(s["mlp_loaded"], 32)
    for g in range(4):
        dve.wait_ge(s["mixed"], g + 1)
        u, gate = W.F[:, 4 * MU + g, 0:NQ], W.F[:, 4 * MG + g, 0:NQ]
        x = W.F[:, 4 * RK + g, 0:NQ]
        step(dve.tensor_tensor(x.rearrange("p (t n) -> p t n", n=P), R.ps[:, branch_bank(2 * HEADS + g), 0:NQ].rearrange("p (t n) -> p t n", n=P),
                               W.mix_b[:, g, :].unsqueeze(1).broadcast_to([P, T, P]), ALU.add))
        step.wait()
        step(dve.tensor_tensor(x, x, u, ALU.mult))
        step.wait()
        dve.wait_ge(s["gate"], g + 1)
        dve.tensor_tensor(gate, x, gate, ALU.mult).then_inc(s["branch_out"], 1)


def merge(nc, R, W, I, w, l, NQ, factor):
    names = [f"w_loaded{b}" for b in range(3)]
    free = lambda slot: R.ring[:, slot, 512:]
    W.mix_w, W.mix_b = (free(n).rearrange("p (g n) -> p g n", n=P) for n in (1, 3))
    W.stats, W.moments = free(5)[:, 0:24].rearrange("p (t n) -> p t n", n=6), free(5)[:, 32:40].rearrange("p (t n) -> p t n", n=2)
    with stage(nc, *names, "logit_done", "branch_done", "sig", "mult", "out", "mlp_loaded", "squared", "summed", "log", "rstd",
               "gate", "scaled", "branch_out", "b_chain", "var", "root", "normed", "mixed") as (block, s):
        loaded = [s[n] for n in names]
        wt = R.ring[:, 0:6, :].rearrange("p (b a) n -> p b (a n)", b=3)[:, :, 0:12 * P].rearrange("p b (k n) -> p b k n", n=P)
        sig = R.ring[:, 6:8, :].rearrange("p a (b n) -> p (a b) n", n=512)

        @block.sync
        def _(sp):
            sp.dma_start(W.mix_w, I["mlp_w"][l]).then_inc(s["mlp_loaded"], 16)
            sp.dma_start(W.mix_b, I["mlp_b"][l]).then_inc(s["mlp_loaded"], 16)
            with sp.Fori(0, KD) as m:
                for b in range(3):
                    sp.wait_ge(s["branch_done"], m * 3 + (b + 1))
                    sp.dma_start(wt[:, b].rearrange("p k n -> p (k n)"), w[ds(m, 1), b].rearrange("a p n -> p (a n)")).then_inc(loaded[b], 16)

        @block.tensor
        def _(pe):
            def logits(m, b):
                pe.wait_ge(loaded[b], m * 16 + 16)
                pe.wait_ge(s["sig"], m * 3 + (b + 1))
                for k in range(KD):
                    mm = pe.matmul(R.ps[:, 2 * b, 0:NQ], wt[:, b, k, :], R.h[:, k, 0:NQ], start=(k == 0), stop=(k == KD - 1))
                mm.then_inc(s["logit_done"], 1)

            def branch(m, b):
                pe.wait_ge(s["mult"], m * 3 + (b + 1))
                for k in range(KB):
                    mm = pe.matmul(R.ps[:, 2 * b + 1, 0:NQ], wt[:, b, KD + k, :], W.F[:, 4 * (RG, MG, DG)[b] + k, 0:NQ], start=(k == 0), stop=(k == KB - 1))
                mm.then_inc(s["branch_done"], 1)

            pe.sem_inc(s["branch_done"], 3)
            part = branches_pe(pe, R, W, s, NQ)
            logits(0, 0)
            next(part)
            logits(0, 1)
            next(part)
            logits(0, 2)
            pe.wait_ge(s["branch_out"], 12)
            for b in range(3):
                branch(0, b)
            with pe.Fori(1, KD) as m:
                for b in range(3):
                    logits(m, b)
                    branch(m, b)

        @block.scalar
        def _(act):
            def sigmoid(m, b):
                act.wait_ge(s["logit_done"], m * 3 + (b + 1))
                act.wait_ge(s["mult"], m * 3 + (b + 1))
                act.activation(sig[:, b, 0:NQ], R.ps[:, 2 * b, 0:NQ], ACT.Sigmoid).then_inc(s["sig"], 1)

            act.sem_inc(s["sig"], 3)
            branches_act(act, R, W, s, NQ)
            with act.Fori(0, KD) as m:
                for b in range(3):
                    sigmoid(m, b)

        @block.vector
        def _(dve):
            dve.sem_inc(s["mult"], 3)
            branches_dve(dve, R, W, s, NQ, factor)
            with dve.Fori(0, KD) as m:
                y = R.sq[:, ds(m, 1), 0:NQ].rearrange("p a n -> p (a n)")
                for b in range(3):
                    dve.wait_ge(s["sig"], m * 3 + (b + 4))
                    dve.wait_ge(s["branch_done"], m * 3 + (b + 4))
                    if b == 0:
                        dve.tensor_tensor(y, R.ps[:, 1, 0:NQ], sig[:, 0, 0:NQ], ALU.mult).then_inc(s["mult"], 1)
                    else:
                        t = sig[:, b, 0:NQ]
                        dve.tensor_tensor(t, R.ps[:, 2 * b + 1, 0:NQ], t, ALU.mult).then_inc(s["out"], 1)
                        dve.wait_ge(s["out"], m * 2 + b)
                        dve.wait_ge(s["mult"], m * 3 + (b + 3))
                        dve.tensor_tensor(y, y, t, ALU.add).then_inc(s["mult"], 1)


def program(nc, I, out):
    with ExitStack() as c:
        R = Named()
        alloc(nc, R, lambda name, *shape: c.enter_context(nc.sbuf_tensor(name, [P, *shape], F32)), c)
        setup(nc, R, I)
        modulate(nc, R, R.mods[:, 0], R.vec[:, 4, 0:KD], NT)
        rwkv_layer(nc, R, I)
        hyena_layer(nc, R, I)
        with stage(nc, "loaded") as (block, s):
            @block.sync
            def _(sp):
                sp.dma_start(R.x[:, :, NX:], I["ctx_t"]).then_inc(s["loaded"], 16)
                sp.wait_ge(s["loaded"], 16)
        for l in range(2):
            second_layer(nc, R, I, l)
        with stage(nc, "stored") as (block, s):
            @block.sync
            def _(sp):
                sp.dma_start(out, R.x[:, :, 0:NX]).then_inc(s["stored"], 16)
                sp.wait_ge(s["stored"], 16)



def tiles(w):
    K, N = w.shape
    return np.ascontiguousarray(w.reshape(K // P, P, N // P, P).transpose(2, 1, 0, 3)).reshape(N // P, P, K)


def columns(v):
    return v.reshape(-1, P).T


def layouts(a):
    f = np.float32
    out = {}
    out["x_t"] = np.concatenate([a["x"][0].T, a["ctx"][0].T], 1).reshape(KD, P, NT).transpose(1, 0, 2)
    out["eye"] = np.eye(P, dtype=f)
    half = np.arange(P) // 64
    out["head_ones"] = (half[:, None] == half[None, :]).astype(f)
    out["cond"] = np.stack([a["c"][0], a["c_ctx"], a["c_2"][0], a["c_ctx_2"]], 1).reshape(KD, P, 4).transpose(1, 0, 2)
    vec = np.zeros((P, 9, 24), f)
    for n, b in enumerate((a["ada_b"][0], a["ada_b"][1], a["b_mod_2"][0], a["b_mod_2"][1])):
        vec[:, n, :] = columns(b)
    for l in range(2):
        vec[:, 4, l * 8:l * 8 + 8] = columns(a["norm_pre"][l])
        vec[:, 5, l * 8:l * 8 + 8] = columns(a["norm_post"][l])
        vec[:, 6, l * 8:l * 8 + 8] = columns(a["g_pre_2"][l])
        vec[:, 7, l * 8:l * 8 + 8] = columns(a["g_post_2"][l])
    out["vectors"] = vec
    mods = np.concatenate([a["ada_w"], a["w_mod_2"]]).reshape(4, 4, 2, P, 6, 512)
    out["w_mods"] = mods.transpose(0, 4, 1, 3, 2, 5).reshape(24, 4, P, D)
    out["w_out0"] = tiles(a["w_out"][0])
    out["mu"] = a["l0_mu"].reshape(6, KD, P).transpose(2, 0, 1)
    w = a["l0_w_in"]
    out["w_rkvg"] = np.concatenate([tiles(w[:, g * E:(g + 1) * E]) for g in (1, 2, 0, 3)], 2)
    out["w_low"] = np.concatenate(list(tiles(w[:, 4 * E:])), 1)
    pv = np.zeros((KE, P, 10), f)
    for n, v in enumerate((a["l0_w0"][0], a["l0_w0"][1], a["l0_a0"][0], a["l0_a0"][1], a["l0_k_k"], a["l0_k_a"],
                           a["l0_r_k"].reshape(-1), a["l0_ln_w"], a["l0_ln_b"])):
        pv[:, :, n] = v.reshape(KE, P)
    out["pair_vec"] = pv
    out["lora"] = np.stack([a["l0_w2"].reshape(P, KE, P), a["l0_a2"].reshape(P, KE, P)], 1).transpose(2, 0, 1, 3)
    t = np.arange(64)
    strict = [t[:, None] < t[None, :], t[:, None] > t[None, :]]
    incl = [t[:, None] <= t[None, :], t[:, None] >= t[None, :]]
    masks = np.zeros((P, 2, 2, P), f)
    for z in range(2):
        for p in range(2):
            for rows in (0, 64):
                masks[rows:rows + 64, z, p, oth(p):oth(p) + 64] = strict[z]
                masks[rows:rows + 64, z, p, nat(p):nat(p) + 64] = incl[z]
    out["masks"] = masks
    lm = np.zeros((P, LEVELS, 2, P), f)
    q = np.arange(P)
    for l in range(LEVELS):
        b = q >> l
        low = (b[:, None] == b[None, :] + 1) & (b[:, None] % 2 == 1)
        lm[:, l, 0, :] = low
        lm[:, l, 1, :] = low.T
    out["level_masks"] = lm
    out["ctx_t"] = a["ctx_2"][0].T.reshape(KD, P, NX).transpose(1, 0, 2)
    w = a["l1_w_in"]
    out["w_in1"], out["w_gate1"], out["w_out1"] = tiles(w[:, :3 * E]), tiles(w[:, 3 * E:]), tiles(a["w_out"][1])
    hv = np.zeros((P, 5, 3 * KE), f)
    for q in range(3):
        hv[:, q, :] = columns(a["l1_conv_w"][q])
    hv[:, 3, :] = columns(a["l1_conv_b"])
    hv[:, 4, 0:KE] = columns(a["l1_filter_bias"])
    out["hyena_vec"] = hv
    out["f_w1"] = a["l1_f_w1"]
    out["f_w23"] = np.stack([a["l1_f_w2"], a["l1_f_w3"]], 1)
    out["f_vec"] = np.stack([a["l1_f_b1"], a["l1_f_b2"], a["l1_f_b3"], a["l1_sin_freq"]], 1)
    out["f_w4"] = a["l1_f_w4"].reshape(64, 2, E)
    out.update(hyena_constants())
    for l in range(2):
        w = a["w_in_2"][l]
        col = lambda n: w[:, n * BW:(n + 1) * BW]
        out[f"w_feature{l}"] = np.concatenate([tiles(col(n)) for n in (0, 2, 4, 6, 5, 7, 8, 10)])
        out[f"w_token{l}"] = np.stack([col(n).reshape(KD, P, BW).transpose(1, 0, 2) for n in (1, 3, 9)])
        logits = tiles(w[:, 11 * BW:]).reshape(3, KD, P, D).transpose(1, 0, 2, 3)
        branch = np.stack([tiles(a["w_branch_out_2"][l, b]) for b in range(3)], 1)
        out[f"w_merge{l}"] = np.concatenate([logits, branch], 3)
        out[f"w_last{l}"] = tiles(a["w_out_2"][l])
    every = lambda v: np.broadcast_to(v[:, None], (v.shape[0], P) + v.shape[1:])
    out["ret_logit"] = every(a["ret_decay_logit_2"].reshape(2, 8))
    out["lambdas"] = every(np.stack([a["diff_lambda_q_2"], a["diff_lambda_k_2"]], 1))
    out["mlp_w"] = a["mlp_w_s_2"].transpose(0, 3, 1, 2)
    out["mlp_b"] = every(a["mlp_b_s_2"])
    out.update(attention_constants())
    return {k: np.ascontiguousarray(v) for k, v in out.items()}


def hyena_constants():
    f = np.float32
    L, bands = NX, 16
    t = np.linspace(0.0, 1.0, L, dtype=f)[:, None]
    freqs = np.linspace(1e-4, bands - 1, bands, dtype=f)[None, :]
    ang = f(2.0 * math.pi / L) * np.arange(L, dtype=f)[:, None] * freqs
    z = np.concatenate([t, np.cos(ang), -np.sin(ang)], 1)
    deltas = np.abs(np.linspace(math.log(1e-2) / 1.5, math.log(1e-2) / 0.3, E, dtype=f))
    window = np.exp(-t * deltas).astype(f)
    w = math.pi * (2 * np.arange(L) + 1) / (2 * L)
    ph = np.arange(L)[:, None] * w[None, :]
    dft = np.concatenate([np.cos(ph), -np.sin(ph)], 1)
    idft = np.concatenate([np.cos(ph).T, -np.sin(ph).T], 0) / L
    return {"z_t": z.T.astype(f), "window": window.reshape(2, P, E).transpose(1, 0, 2),
            "dft": dft.reshape(2, P, 4 * P).transpose(1, 0, 2).astype(f),
            "idft": idft.reshape(4, P, NX).transpose(1, 0, 2).astype(f)}


def attention_constants():
    f = np.float32
    j = np.arange(NX).reshape(2, P).T[:, :, None]
    i = np.arange(NX)[None, None, :]
    dist = np.stack([np.maximum(i - j, 0), np.maximum(j - i, 0), NX + i - j, NX - i + j], 1).astype(f)
    out = {"distances": dist.reshape(P, 4, 2 * NX), "same": (i == j).astype(f).reshape(P, 2 * NX)}
    row, col = np.arange(NX) // GRID, np.arange(NX) % GRID
    rope = []
    for dim in (128, 64):
        n = dim // 4
        inv = (f(10000.0) ** (-np.arange(n, dtype=f) / n)).astype(f)
        ang = np.concatenate([row.astype(f)[:, None] * inv, col.astype(f)[:, None] * inv], 1).T
        q = np.arange(P)
        sign = np.where(q % dim < dim // 2, -1.0, 1.0).astype(f)
        rope += [np.cos(ang)[q % (dim // 2)], np.sin(ang)[q % (dim // 2)] * sign[:, None]]
    out["rope"] = np.stack(rope, 1).astype(f)
    q = np.arange(P)
    out["swaps"] = np.stack([(q[:, None] == (q[None, :] ^ s)) for s in (64, 32)], 1).astype(f)
    return out


def kernel(**inputs):
    import concourse.bacc as bacc
    from concourse.bass_utils import run_bass_kernel_spmd

    nc = bacc.Bacc("TRN2", target_bir_lowering=False, num_devices=1)
    arrays = {f"in_{k}": v for k, v in layouts({k: np.asarray(v) for k, v in inputs.items()}).items()}
    aps = {k[3:]: nc.dram_tensor(k, v.shape, mybir.dt.from_np(v.dtype), kind="ExternalInput").ap() for k, v in arrays.items()}
    out = nc.dram_tensor("out_x", (P, KD, NX), F32, kind="ExternalOutput").ap()
    program(nc, aps, out)
    got = run_bass_kernel_spmd(nc, [arrays], core_ids=[0]).results[0]["out_x"]
    return np.ascontiguousarray(got.transpose(2, 1, 0)).reshape(1, NX, D)
```
